# Optimizing a Trainium2 kernel written in Bass

```python
import math
import jax, jax.numpy as jnp
from jax import lax
import numpy as np

D_MODEL = 1024
BATCH = 1
SEQ = 256
DEPTH = 2

HEAD_DIM = 64
ROPE_THETA = 500000.0
ROPE_FRAC = 4
EPS = 1e-6
Q_BLOCK = 128

A_WIDTH = D_MODEL // 2
A_GROUPS = 4
A_GDIM = A_WIDTH // A_GROUPS
A_CHUNK = 128

B_HEADS = 8
B_QK_DIM = 32
B_V_DIM = 2 * B_QK_DIM
B_WIDTH = B_HEADS * B_V_DIM

C_WIDTH = D_MODEL // 2
C_KERNEL = 31

D_HEADS = 8
D_KV_GROUPS = 2
D_WIDTH = D_HEADS * HEAD_DIM
CMP_BLOCK = 32
CMP_STRIDE = 16
CMP_HIDDEN = 2 * HEAD_DIM
SLC_BLOCK = 64
SLC_TOPK = 16
WINDOW = 512

MEM_TOKENS = 256
M_HEADS = 4
M_WIDTH = M_HEADS * HEAD_DIM

MIX_WIDTH = A_WIDTH + B_WIDTH + M_WIDTH
EVEN_SPLITS = (A_WIDTH, A_WIDTH, A_WIDTH,
               2 * B_HEADS * B_QK_DIM, 2 * B_HEADS * B_QK_DIM, B_WIDTH, B_WIDTH,
               M_WIDTH, M_WIDTH)
ODD_SPLITS = (C_WIDTH, C_WIDTH, C_WIDTH,
              D_WIDTH, 6 * D_KV_GROUPS * HEAD_DIM, 3 * D_HEADS, D_WIDTH,
              M_WIDTH, M_WIDTH)
EVEN_IN = sum(EVEN_SPLITS)
ODD_IN = sum(ODD_SPLITS)


def rms_norm(x, g):
    xf = x.astype(jnp.float32)
    y = xf * lax.rsqrt(jnp.mean(xf * xf, axis=-1, keepdims=True) + EPS)
    return (y * g.astype(jnp.float32)).astype(x.dtype)

def rope_partial(x, pos):
    d = x.shape[-1]
    rd = d // ROPE_FRAC
    half = rd // 2
    inv = ROPE_THETA ** (-jnp.arange(half, dtype=jnp.float32) / half)
    ang = pos.astype(jnp.float32)[:, None] * inv[None, :]
    cos = jnp.cos(ang).astype(x.dtype)
    sin = jnp.sin(ang).astype(x.dtype)
    x1, x2, rest = x[..., :half], x[..., half:rd], x[..., rd:]
    return jnp.concatenate([x1 * cos - x2 * sin, x1 * sin + x2 * cos, rest], axis=-1)

def masked_softmax(s, mask):
    s = jnp.where(mask, s, -jnp.inf)
    m = jnp.max(s, axis=-1, keepdims=True)
    m = jnp.where(jnp.isfinite(m), m, 0.0)
    e = jnp.where(mask, jnp.exp(s - m), 0.0)
    return e / jnp.maximum(jnp.sum(e, axis=-1, keepdims=True), jnp.finfo(jnp.float32).tiny)

def split_cols(x, sizes):
    return jnp.split(x, [int(v) for v in np.cumsum(sizes)[:-1]], axis=-1)

def chunked_sgu(u, v, w_s, b_s, v_gain):
    Bz, S, _ = v.shape
    v = rms_norm(v.reshape(Bz, S, A_GROUPS, A_GDIM), v_gain.reshape(A_GROUPS, A_GDIM))
    v = v.reshape(Bz, S // A_CHUNK, A_CHUNK, A_GROUPS, A_GDIM)
    causal = jnp.tril(jnp.ones((A_CHUNK, A_CHUNK), dtype=bool))
    w = jnp.where(causal[None], w_s, 0.0)
    z = jnp.einsum('gts,bcsgd->bctgd', w, v) + b_s.T[:, :, None]
    return u * z.reshape(Bz, S, A_WIDTH)

def diff_attention(q, k, v, lam):
    Bz, H, _, S, dk = q.shape
    dv = v.shape[-1]
    nblk = S // Q_BLOCK
    scale = dk ** -0.5
    kpos = jnp.arange(S)
    qb = q.reshape(Bz, H, 2, nblk, Q_BLOCK, dk).transpose(3, 0, 1, 2, 4, 5)

    def block(args):
        qi, c = args
        qpos = c * Q_BLOCK + jnp.arange(Q_BLOCK)
        s = jnp.einsum('bhmqd,bhmkd->bhmqk', qi, k).astype(jnp.float32) * scale
        s = jnp.where(kpos[None, :] <= qpos[:, None], s, -jnp.inf)
        p = jax.nn.softmax(s, axis=-1)
        pd = p[:, :, 0] - lam * p[:, :, 1]
        return jnp.einsum('bhqk,bhkd->bhqd', pd.astype(v.dtype), v)

    o = lax.map(block, (qb, jnp.arange(nblk)))
    return o.transpose(1, 0, 3, 2, 4).reshape(Bz, S, H, dv)

def memory_attention(q, mem_n, w_kv, qnorm, knorm):
    Bz, S, _ = q.shape
    k, v = jnp.split(mem_n @ w_kv, 2, axis=-1)
    q = rms_norm(q.reshape(Bz, S, M_HEADS, HEAD_DIM), qnorm)
    k = rms_norm(k.reshape(Bz, -1, M_HEADS, HEAD_DIM), knorm)
    v = v.reshape(Bz, -1, M_HEADS, HEAD_DIM)
    s = jnp.einsum('bshd,bmhd->bhsm', q, k).astype(jnp.float32) * (HEAD_DIM ** -0.5)
    p = jax.nn.softmax(s, axis=-1)
    return jnp.einsum('bhsm,bmhd->bshd', p.astype(v.dtype), v).reshape(Bz, S, M_WIDTH)

def conformer_conv(a, b, conv_w, conv_b, norm_g):
    h = a * jax.nn.sigmoid(b)
    hp = jnp.pad(h, ((0, 0), (C_KERNEL - 1, 0), (0, 0)))
    y = lax.conv_general_dilated(hp, conv_w[:, None, :], window_strides=(1,), padding='VALID',
                                 dimension_numbers=('NWC', 'WIO', 'NWC'),
                                 feature_group_count=C_WIDTH) + conv_b
    return jax.nn.silu(rms_norm(y, norm_g))

def compress(t, cmp_idx, pos_emb, w1, w2):
    Bz, _, G, hd = t.shape
    blocks = t[:, cmp_idx] + pos_emb[:, None, :]
    flat = blocks.transpose(0, 1, 3, 2, 4).reshape(Bz, cmp_idx.shape[0], G, CMP_BLOCK * hd)
    return jax.nn.silu(flat @ w1) @ w2

def cmp_to_slc_overlap(n_cmp, n_slc):
    start = np.arange(n_cmp) * CMP_STRIDE
    s0 = np.arange(n_slc) * SLC_BLOCK
    lo = np.maximum(start[:, None], s0[None, :])
    hi = np.minimum(start[:, None] + CMP_BLOCK, s0[None, :] + SLC_BLOCK)
    return (np.clip(hi - lo, 0, None) / CMP_BLOCK).astype(np.float32)

def nsa(q, kv, gates, pos, qnorm, knorm, cmp_pos_k, cmp_w1_k, cmp_w2_k,
        cmp_pos_v, cmp_w1_v, cmp_w2_v):
    Bz, S = q.shape[:2]
    G, R, hd = D_KV_GROUPS, D_HEADS // D_KV_GROUPS, HEAD_DIM
    nblk = S // Q_BLOCK
    n_cmp = (S - CMP_BLOCK) // CMP_STRIDE + 1
    n_slc = S // SLC_BLOCK
    n_sel = min(SLC_TOPK, n_slc)
    scale = hd ** -0.5

    q = rope_partial(rms_norm(q, qnorm).transpose(0, 2, 1, 3), pos).reshape(Bz, G, R, S, hd)
    k_cmp_raw, v_cmp_raw, k_slc, v_slc, k_win, v_win = [kv[:, :, i] for i in range(6)]

    cmp_idx = np.arange(n_cmp)[:, None] * CMP_STRIDE + np.arange(CMP_BLOCK)[None, :]
    cmp_end = jnp.asarray(cmp_idx[:, -1])
    kc = compress(k_cmp_raw, cmp_idx, cmp_pos_k, cmp_w1_k, cmp_w2_k)
    vc = compress(v_cmp_raw, cmp_idx, cmp_pos_v, cmp_w1_v, cmp_w2_v).transpose(0, 2, 1, 3)
    kc = rope_partial(rms_norm(kc, knorm).transpose(0, 2, 1, 3), cmp_end)

    ks = rope_partial(rms_norm(k_slc, knorm).transpose(0, 2, 1, 3), pos)
    kb = ks.reshape(Bz, G, n_slc, SLC_BLOCK, hd)
    vb = v_slc.transpose(0, 2, 1, 3).reshape(Bz, G, n_slc, SLC_BLOCK, hd)

    pad = ((0, 0), (0, 0), (WINDOW, 0), (0, 0))
    kw = jnp.pad(rope_partial(rms_norm(k_win, knorm).transpose(0, 2, 1, 3), pos), pad)
    vw = jnp.pad(v_win.transpose(0, 2, 1, 3), pad)

    overlap = jnp.asarray(cmp_to_slc_overlap(n_cmp, n_slc))
    b_ix = jnp.arange(Bz)[:, None, None, None]
    g_ix = jnp.arange(G)[None, :, None, None]
    blk_tok = jnp.arange(SLC_BLOCK)
    slc_ids = jnp.arange(n_slc)
    win_off = jnp.arange(WINDOW + Q_BLOCK) - WINDOW

    qb = q.reshape(Bz, G, R, nblk, Q_BLOCK, hd).transpose(3, 0, 1, 2, 4, 5)
    gb = gates.transpose(0, 2, 1, 3).reshape(Bz, G, R, nblk, Q_BLOCK, 3).transpose(3, 0, 1, 2, 4, 5)

    def block(args):
        qi, gt, c = args
        qpos = c * Q_BLOCK + jnp.arange(Q_BLOCK)
        s = jnp.einsum('bgrqd,bgnd->bgrqn', qi, kc).astype(jnp.float32) * scale
        p_c = masked_softmax(s, cmp_end[None, :] <= qpos[:, None])
        o_c = jnp.einsum('bgrqn,bgnd->bgrqd', p_c.astype(vc.dtype), vc)
        imp = jnp.einsum('bgrqn,nj->bgqj', p_c, overlap)
        cur = (qpos // SLC_BLOCK)[:, None]
        imp = jnp.where(slc_ids[None, :] > cur, -jnp.inf, imp)
        forced = (slc_ids[None, :] == 0) | (slc_ids[None, :] == cur) | (slc_ids[None, :] == cur - 1)
        imp = jnp.where(forced, jnp.inf, imp)
        _, sel = lax.top_k(imp, n_sel)
        ksel = kb[b_ix, g_ix, sel].reshape(Bz, G, Q_BLOCK, n_sel * SLC_BLOCK, hd)
        vsel = vb[b_ix, g_ix, sel].reshape(Bz, G, Q_BLOCK, n_sel * SLC_BLOCK, hd)
        kpos = (sel[..., None] * SLC_BLOCK + blk_tok).reshape(Bz, G, Q_BLOCK, n_sel * SLC_BLOCK)
        s = jnp.einsum('bgrqd,bgqkd->bgrqk', qi, ksel).astype(jnp.float32) * scale
        p_s = masked_softmax(s, (kpos <= qpos[:, None])[:, :, None])
        o_s = jnp.einsum('bgrqk,bgqkd->bgrqd', p_s.astype(vsel.dtype), vsel)
        kwi = lax.dynamic_slice_in_dim(kw, c * Q_BLOCK, WINDOW + Q_BLOCK, axis=2)
        vwi = lax.dynamic_slice_in_dim(vw, c * Q_BLOCK, WINDOW + Q_BLOCK, axis=2)
        wpos = c * Q_BLOCK + win_off
        dpos = qpos[:, None] - wpos[None, :]
        s = jnp.einsum('bgrqd,bgkd->bgrqk', qi, kwi).astype(jnp.float32) * scale
        p_w = masked_softmax(s, (wpos[None, :] >= 0) & (dpos >= 0) & (dpos < WINDOW))
        o_w = jnp.einsum('bgrqk,bgkd->bgrqd', p_w.astype(vwi.dtype), vwi)
        return gt[..., 0:1] * o_c + gt[..., 1:2] * o_s + gt[..., 2:3] * o_w

    o = lax.map(block, (qb, gb, jnp.arange(nblk)))
    return o.transpose(1, 0, 4, 2, 3, 5).reshape(Bz, S, D_WIDTH)

def even_layer(x, mem_n, pos, layer, norm_g, w_in, a_vnorm, a_ws, a_bs, b_qnorm, b_knorm,
               b_lq1, b_lk1, b_lq2, b_lk2, b_subln, m_wkv, m_qnorm, m_knorm, w_out):
    Bz, S, _ = x.shape
    h = rms_norm(x, norm_g)
    a_u, a_v, a_g, b_q, b_k, b_v, b_g, m_q, m_g = split_cols(h @ w_in, EVEN_SPLITS)
    y_a = chunked_sgu(jax.nn.gelu(a_u), jax.nn.gelu(a_v), a_ws, a_bs, a_vnorm) * jax.nn.silu(a_g)
    lam_init = 0.8 - 0.6 * math.exp(-0.3 * layer)
    lam = (jnp.exp(jnp.sum(b_lq1.astype(jnp.float32) * b_lk1.astype(jnp.float32)))
           - jnp.exp(jnp.sum(b_lq2.astype(jnp.float32) * b_lk2.astype(jnp.float32))) + lam_init)
    q = rms_norm(b_q.reshape(Bz, S, B_HEADS, 2, B_QK_DIM), b_qnorm).transpose(0, 2, 3, 1, 4)
    k = rms_norm(b_k.reshape(Bz, S, B_HEADS, 2, B_QK_DIM), b_knorm).transpose(0, 2, 3, 1, 4)
    q, k = rope_partial(q, pos), rope_partial(k, pos)
    v = b_v.reshape(Bz, S, B_HEADS, B_V_DIM).transpose(0, 2, 1, 3)
    o_b = rms_norm(diff_attention(q, k, v, lam), b_subln) * (1.0 - lam_init)
    y_b = o_b.reshape(Bz, S, B_WIDTH) * jax.nn.silu(b_g)
    y_m = memory_attention(m_q, mem_n, m_wkv, m_qnorm, m_knorm) * jax.nn.silu(m_g)
    return x + jnp.concatenate([y_a, y_b, y_m], axis=-1) @ w_out

def odd_layer(x, mem_n, pos, norm_g, w_in, c_conv_w, c_conv_b, c_norm, d_qnorm, d_knorm,
              cmp_pos_k, cmp_w1_k, cmp_w2_k, cmp_pos_v, cmp_w1_v, cmp_w2_v,
              m_wkv, m_qnorm, m_knorm, w_out):
    Bz, S, _ = x.shape
    h = rms_norm(x, norm_g)
    c_a, c_b, c_g, d_q, d_kv, d_bg, d_g, m_q, m_g = split_cols(h @ w_in, ODD_SPLITS)
    y_c = conformer_conv(c_a, c_b, c_conv_w, c_conv_b, c_norm) * jax.nn.silu(c_g)
    kv = d_kv.reshape(Bz, S, 6, D_KV_GROUPS, HEAD_DIM)
    gates = jax.nn.sigmoid(d_bg.reshape(Bz, S, D_HEADS, 3))
    y_d = nsa(d_q.reshape(Bz, S, D_HEADS, HEAD_DIM), kv, gates, pos, d_qnorm, d_knorm,
              cmp_pos_k, cmp_w1_k, cmp_w2_k, cmp_pos_v, cmp_w1_v, cmp_w2_v) * jax.nn.silu(d_g)
    y_m = memory_attention(m_q, mem_n, m_wkv, m_qnorm, m_knorm) * jax.nn.silu(m_g)
    return x + jnp.concatenate([y_c, y_d, y_m], axis=-1) @ w_out

def first_inputs(seed: int = 0) -> dict:
    key = jax.random.key(seed)
    keys = iter(jax.random.split(key, 48))

    def nrm(shape, scale):
        return jax.random.normal(next(keys), shape, jnp.float32) * scale

    def gain(n):
        return 1.0 + nrm((n,), 0.05)

    return {
        "x": nrm((BATCH, SEQ, D_MODEL), 1.0),
        "mem": nrm((BATCH, MEM_TOKENS, D_MODEL), 1.0),
        "mem_norm": gain(D_MODEL),
        "l0_norm": gain(D_MODEL),
        "l0_w_in": nrm((D_MODEL, EVEN_IN), D_MODEL ** -0.5),
        "l0_a_vnorm": gain(A_WIDTH),
        "l0_a_ws": nrm((A_GROUPS, A_CHUNK, A_CHUNK), A_CHUNK ** -0.5),
        "l0_a_bs": 1.0 + nrm((A_GROUPS, A_CHUNK), 0.1),
        "l0_b_qnorm": gain(B_QK_DIM),
        "l0_b_knorm": gain(B_QK_DIM),
        "l0_b_lq1": nrm((B_QK_DIM,), 0.1),
        "l0_b_lk1": nrm((B_QK_DIM,), 0.1),
        "l0_b_lq2": nrm((B_QK_DIM,), 0.1),
        "l0_b_lk2": nrm((B_QK_DIM,), 0.1),
        "l0_b_subln": gain(B_V_DIM),
        "l0_m_wkv": nrm((D_MODEL, 2 * M_WIDTH), D_MODEL ** -0.5),
        "l0_m_qnorm": gain(HEAD_DIM),
        "l0_m_knorm": gain(HEAD_DIM),
        "l0_w_out": nrm((MIX_WIDTH, D_MODEL), MIX_WIDTH ** -0.5),
        "l1_norm": gain(D_MODEL),
        "l1_w_in": nrm((D_MODEL, ODD_IN), D_MODEL ** -0.5),
        "l1_c_conv_w": nrm((C_KERNEL, C_WIDTH), C_KERNEL ** -0.5),
        "l1_c_conv_b": nrm((C_WIDTH,), 0.02),
        "l1_c_norm": gain(C_WIDTH),
        "l1_d_qnorm": gain(HEAD_DIM),
        "l1_d_knorm": gain(HEAD_DIM),
        "l1_d_cmp_pos_k": nrm((CMP_BLOCK, HEAD_DIM), 0.02),
        "l1_d_cmp_w1_k": nrm((CMP_BLOCK * HEAD_DIM, CMP_HIDDEN), (CMP_BLOCK * HEAD_DIM) ** -0.5),
        "l1_d_cmp_w2_k": nrm((CMP_HIDDEN, HEAD_DIM), CMP_HIDDEN ** -0.5),
        "l1_d_cmp_pos_v": nrm((CMP_BLOCK, HEAD_DIM), 0.02),
        "l1_d_cmp_w1_v": nrm((CMP_BLOCK * HEAD_DIM, CMP_HIDDEN), (CMP_BLOCK * HEAD_DIM) ** -0.5),
        "l1_d_cmp_w2_v": nrm((CMP_HIDDEN, HEAD_DIM), CMP_HIDDEN ** -0.5),
        "l1_m_wkv": nrm((D_MODEL, 2 * M_WIDTH), D_MODEL ** -0.5),
        "l1_m_qnorm": gain(HEAD_DIM),
        "l1_m_knorm": gain(HEAD_DIM),
        "l1_w_out": nrm((MIX_WIDTH, D_MODEL), MIX_WIDTH ** -0.5),
    }

def first_block(x, mem, mem_norm,
              l0_norm, l0_w_in, l0_a_vnorm, l0_a_ws, l0_a_bs, l0_b_qnorm, l0_b_knorm,
              l0_b_lq1, l0_b_lk1, l0_b_lq2, l0_b_lk2, l0_b_subln, l0_m_wkv, l0_m_qnorm,
              l0_m_knorm, l0_w_out,
              l1_norm, l1_w_in, l1_c_conv_w, l1_c_conv_b, l1_c_norm, l1_d_qnorm, l1_d_knorm,
              l1_d_cmp_pos_k, l1_d_cmp_w1_k, l1_d_cmp_w2_k, l1_d_cmp_pos_v, l1_d_cmp_w1_v,
              l1_d_cmp_w2_v, l1_m_wkv, l1_m_qnorm, l1_m_knorm, l1_w_out):
    pos = jnp.arange(x.shape[1], dtype=jnp.int32)
    mem_n = rms_norm(mem, mem_norm)
    even_params = (l0_norm, l0_w_in, l0_a_vnorm, l0_a_ws, l0_a_bs, l0_b_qnorm, l0_b_knorm,
                   l0_b_lq1, l0_b_lk1, l0_b_lq2, l0_b_lk2, l0_b_subln, l0_m_wkv, l0_m_qnorm,
                   l0_m_knorm, l0_w_out)
    odd_params = (l1_norm, l1_w_in, l1_c_conv_w, l1_c_conv_b, l1_c_norm, l1_d_qnorm, l1_d_knorm,
                  l1_d_cmp_pos_k, l1_d_cmp_w1_k, l1_d_cmp_w2_k, l1_d_cmp_pos_v, l1_d_cmp_w1_v,
                  l1_d_cmp_w2_v, l1_m_wkv, l1_m_qnorm, l1_m_knorm, l1_w_out)
    for layer in range(DEPTH):
        if layer % 2 == 0:
            x = even_layer(x, mem_n, pos, layer + 1, *even_params)
        else:
            x = odd_layer(x, mem_n, pos, *odd_params)
    return x


N_A_LAYERS = DEPTH // 2
N_B_LAYERS = DEPTH - N_A_LAYERS
D_RNN = D_MODEL
LRU_HEADS = 4
LRU_BLOCK = D_RNN // LRU_HEADS
CONV_WIDTH = 4
LRU_C = 8.0
MLA_HEADS = 16
QK_NOPE = 64
QK_ROPE = 32
V_HEAD = 64
Q_LORA = 384
KV_LORA = 256
ROPE_THETA_2 = 10000.0
ATTN_SCALE = 1.0 / math.sqrt(QK_NOPE + QK_ROPE)
PEER_HEADS = 8
N_KEYS = 128
N_EXPERTS = N_KEYS * N_KEYS
PEER_TOPK = 16
PEER_QDIM = 256
PEER_HALF = PEER_QDIM // 2
PEER_CHUNK = 128
RMS_EPS = 1e-6
NEG_INF = -1e30


def rmsnorm(x, g):
    xf = x.astype(jnp.float32)
    y = xf * lax.rsqrt(jnp.mean(xf * xf, axis=-1, keepdims=True) + RMS_EPS)
    return (y * g.astype(jnp.float32)).astype(x.dtype)

def rope(x, positions):
    half = QK_ROPE // 2
    freqs = ROPE_THETA_2 ** (-jnp.arange(half, dtype=jnp.float32) / half)
    ang = positions.astype(jnp.float32)[..., None] * freqs
    ang = ang.reshape(ang.shape[:2] + (1,) * (x.ndim - 3) + (half,))
    cos, sin = jnp.cos(ang), jnp.sin(ang)
    xf = x.astype(jnp.float32)
    x1, x2 = xf[..., :half], xf[..., half:]
    out = jnp.concatenate([x1 * cos - x2 * sin, x1 * sin + x2 * cos], axis=-1)
    return out.astype(x.dtype)

def _lru_combine(left, right):
    a1, b1 = left
    a2, b2 = right
    return a1 * a2, a2 * b1 + b2

def rglru_block(h, w_in, conv_w, conv_b, wa, ba, wx, bx, lam, w_out):
    B, S, _ = h.shape
    gate_in, rec_in = jnp.split(h @ w_in, 2, axis=-1)
    gate = jax.nn.gelu(gate_in, approximate=False)
    xp = jnp.pad(rec_in, ((0, 0), (CONV_WIDTH - 1, 0), (0, 0)))
    xc = conv_b
    for k in range(CONV_WIDTH):
        xc = xc + xp[:, k:k + S] * conv_w[k]
    xb = xc.reshape(B, S, LRU_HEADS, LRU_BLOCK)
    r = jax.nn.sigmoid(jnp.einsum('bshi,hij->bshj', xb, wa).reshape(B, S, D_RNN) + ba)
    i = jax.nn.sigmoid(jnp.einsum('bshi,hij->bshj', xb, wx).reshape(B, S, D_RNN) + bx)
    log_a = -LRU_C * r.astype(jnp.float32) * jax.nn.softplus(-lam.astype(jnp.float32))
    a = jnp.exp(log_a)
    b = jnp.sqrt(-jnp.expm1(2.0 * log_a)) * (i * xc).astype(jnp.float32)
    _, hs = lax.associative_scan(_lru_combine, (a, b), axis=1)
    return (gate * hs.astype(h.dtype)) @ w_out

def shared_kv(x, c, kv_ada_w, kv_ada_b, kv_norm_g, w_dkv, w_kr, kv_latent_g, w_uk, w_uv, positions):
    B, S, _ = x.shape
    shift, scale = jnp.split((jax.nn.silu(c) @ kv_ada_w + kv_ada_b)[:, None, :], 2, axis=-1)
    h = rmsnorm(x, kv_norm_g) * (1.0 + scale) + shift
    c_kv = rmsnorm(h @ w_dkv, kv_latent_g)
    k_rope = rope(h @ w_kr, positions)
    k_nope = (c_kv @ w_uk).reshape(B, S, MLA_HEADS, QK_NOPE)
    v = (c_kv @ w_uv).reshape(B, S, MLA_HEADS, V_HEAD)
    return k_nope, k_rope, v

def _to_blocks(t, block):
    B, S = t.shape[:2]
    return jnp.moveaxis(t.reshape((B, S // block, block) + t.shape[2:]), 1, 0)

def _from_blocks(t):
    nb, B, blk = t.shape[:3]
    return jnp.moveaxis(t, 0, 1).reshape((B, nb * blk) + t.shape[3:])

def mla_block(h, w_dq, q_latent_g, w_uq, w_o, k_nope, k_rope, v, positions):
    B, S, _ = h.shape
    q_lat = rmsnorm(h @ w_dq, q_latent_g)
    q = (q_lat @ w_uq).reshape(B, S, MLA_HEADS, QK_NOPE + QK_ROPE)
    q_nope = q[..., :QK_NOPE]
    q_rope = rope(q[..., QK_NOPE:], positions)

    def attend(args):
        qn, qr, qpos = args
        s = (jnp.einsum('bqhd,bkhd->bhqk', qn, k_nope)
             + jnp.einsum('bqhr,bkr->bhqk', qr, k_rope)).astype(jnp.float32) * ATTN_SCALE
        mask = positions[:, None, None, :] <= qpos[:, None, :, None]
        p = jax.nn.softmax(jnp.where(mask, s, NEG_INF), axis=-1).astype(v.dtype)
        return jnp.einsum('bhqk,bkhd->bqhd', p, v)

    out = lax.map(attend, (_to_blocks(q_nope, Q_BLOCK), _to_blocks(q_rope, Q_BLOCK),
                           _to_blocks(positions, Q_BLOCK)))
    out = _from_blocks(out).reshape(B, S, MLA_HEADS * V_HEAD)
    return out @ w_o

def peer(h, w_q, sub_keys, u_tab, v_tab):
    B, S, _ = h.shape
    q = (h @ w_q).reshape(B, S, PEER_HEADS, 2, PEER_HALF)
    s = jnp.einsum('bshpd,hpnd->bshpn', q, sub_keys).astype(jnp.float32)
    v1, i1 = lax.top_k(s[..., 0, :], PEER_TOPK)
    v2, i2 = lax.top_k(s[..., 1, :], PEER_TOPK)
    cand = (v1[..., :, None] + v2[..., None, :]).reshape(B, S, PEER_HEADS, PEER_TOPK * PEER_TOPK)
    cv, ci = lax.top_k(cand, PEER_TOPK)
    e1 = jnp.take_along_axis(i1, ci // PEER_TOPK, axis=-1)
    e2 = jnp.take_along_axis(i2, ci % PEER_TOPK, axis=-1)
    idx = e1 * N_KEYS + e2
    g = jax.nn.softmax(cv, axis=-1).astype(h.dtype)

    def experts(args):
        hc, ic, gc = args
        act = jax.nn.gelu(jnp.einsum('bcd,bchkd->bchk', hc, u_tab[ic]), approximate=False)
        return jnp.einsum('bchk,bchkd->bcd', gc * act, v_tab[ic])

    out = lax.map(experts, (_to_blocks(h, PEER_CHUNK), _to_blocks(idx, PEER_CHUNK),
                            _to_blocks(g, PEER_CHUNK)))
    return _from_blocks(out)

def _normal(key, shape, fan_in):
    return jax.random.normal(key, shape, jnp.float32) * (fan_in ** -0.5)

def _gain(key, shape):
    return 1.0 + 0.02 * jax.random.normal(key, shape, jnp.float32)

def _bias(key, shape):
    return 0.02 * jax.random.normal(key, shape, jnp.float32)

def second_inputs(seed: int = 0) -> dict:
    key = jax.random.key(seed)
    ks = iter(jax.random.split(key, 40))
    D = D_MODEL
    x = jax.random.normal(next(ks), (BATCH, SEQ, D), jnp.float32)
    c = jax.random.normal(next(ks), (BATCH, D), jnp.float32)
    offset = jax.random.randint(next(ks), (BATCH, 1), 0, 1024, dtype=jnp.int32)
    positions = offset + jnp.arange(SEQ, dtype=jnp.int32)[None, :]
    u = jax.random.uniform(next(ks), (N_A_LAYERS, D_RNN), jnp.float32, 0.9, 0.999)
    a0 = u ** (1.0 / LRU_C)
    lru_lambda = jnp.log(a0) - jnp.log1p(-a0)
    return {
        'x': x, 'c': c, 'positions': positions,
        'ada_w': _normal(next(ks), (DEPTH, D, 6 * D), D),
        'ada_b': _bias(next(ks), (DEPTH, 6 * D)),
        'norm_mix_g': _gain(next(ks), (DEPTH, D)),
        'norm_ffn_g': _gain(next(ks), (DEPTH, D)),
        'lru_w_in': _normal(next(ks), (N_A_LAYERS, D, 2 * D_RNN), D),
        'lru_conv_w': _normal(next(ks), (N_A_LAYERS, CONV_WIDTH, D_RNN), CONV_WIDTH),
        'lru_conv_b': _bias(next(ks), (N_A_LAYERS, D_RNN)),
        'lru_wa': _normal(next(ks), (N_A_LAYERS, LRU_HEADS, LRU_BLOCK, LRU_BLOCK), LRU_BLOCK),
        'lru_ba': _bias(next(ks), (N_A_LAYERS, D_RNN)),
        'lru_wx': _normal(next(ks), (N_A_LAYERS, LRU_HEADS, LRU_BLOCK, LRU_BLOCK), LRU_BLOCK),
        'lru_bx': _bias(next(ks), (N_A_LAYERS, D_RNN)),
        'lru_lambda': lru_lambda,
        'lru_w_out': _normal(next(ks), (N_A_LAYERS, D_RNN, D), D_RNN),
        'kv_ada_w': _normal(next(ks), (D, 2 * D), D),
        'kv_ada_b': _bias(next(ks), (2 * D,)),
        'kv_norm_g': _gain(next(ks), (D,)),
        'mla_w_dkv': _normal(next(ks), (D, KV_LORA), D),
        'mla_w_kr': _normal(next(ks), (D, QK_ROPE), D),
        'mla_kv_latent_g': _gain(next(ks), (KV_LORA,)),
        'mla_w_uk': _normal(next(ks), (KV_LORA, MLA_HEADS * QK_NOPE), KV_LORA),
        'mla_w_uv': _normal(next(ks), (KV_LORA, MLA_HEADS * V_HEAD), KV_LORA),
        'mla_w_dq': _normal(next(ks), (N_B_LAYERS, D, Q_LORA), D),
        'mla_q_latent_g': _gain(next(ks), (N_B_LAYERS, Q_LORA)),
        'mla_w_uq': _normal(next(ks), (N_B_LAYERS, Q_LORA, MLA_HEADS * (QK_NOPE + QK_ROPE)), Q_LORA),
        'mla_w_o': _normal(next(ks), (N_B_LAYERS, MLA_HEADS * V_HEAD, D), MLA_HEADS * V_HEAD),
        'peer_w_q': _normal(next(ks), (DEPTH, D, PEER_HEADS * PEER_QDIM), D),
        'peer_sub_keys': _normal(next(ks), (DEPTH, PEER_HEADS, 2, N_KEYS, PEER_HALF), PEER_HALF),
        'peer_u': _normal(next(ks), (DEPTH, N_EXPERTS, D), D),
        'peer_v': _normal(next(ks), (DEPTH, N_EXPERTS, D), PEER_HEADS),
        'final_g': _gain(next(ks), (D,)),
    }

def second_block(x, c, positions, ada_w, ada_b, norm_mix_g, norm_ffn_g,
              lru_w_in, lru_conv_w, lru_conv_b, lru_wa, lru_ba, lru_wx, lru_bx, lru_lambda, lru_w_out,
              kv_ada_w, kv_ada_b, kv_norm_g, mla_w_dkv, mla_w_kr, mla_kv_latent_g, mla_w_uk, mla_w_uv,
              mla_w_dq, mla_q_latent_g, mla_w_uq, mla_w_o,
              peer_w_q, peer_sub_keys, peer_u, peer_v, final_g):
    k_nope = k_rope = v = None
    for l in range(DEPTH):
        if l == N_A_LAYERS:
            k_nope, k_rope, v = shared_kv(x, c, kv_ada_w, kv_ada_b, kv_norm_g, mla_w_dkv, mla_w_kr,
                                          mla_kv_latent_g, mla_w_uk, mla_w_uv, positions)
        mod = (jax.nn.silu(c) @ ada_w[l] + ada_b[l])[:, None, :]
        sh1, sc1, g1, sh2, sc2, g2 = jnp.split(mod, 6, axis=-1)
        h = rmsnorm(x, norm_mix_g[l]) * (1.0 + sc1) + sh1
        if l < N_A_LAYERS:
            y = rglru_block(h, lru_w_in[l], lru_conv_w[l], lru_conv_b[l], lru_wa[l], lru_ba[l],
                            lru_wx[l], lru_bx[l], lru_lambda[l], lru_w_out[l])
        else:
            j = l - N_A_LAYERS
            y = mla_block(h, mla_w_dq[j], mla_q_latent_g[j], mla_w_uq[j], mla_w_o[j],
                          k_nope, k_rope, v, positions)
        x = x + g1 * y
        h = rmsnorm(x, norm_ffn_g[l]) * (1.0 + sc2) + sh2
        x = x + g2 * peer(h, peer_w_q[l], peer_sub_keys[l], peer_u[l], peer_v[l])
    return rmsnorm(x, final_g)


def setup_inputs(seed=0):
    out = dict(first_inputs(seed))
    for name, value in second_inputs(seed + 1).items():
        if name != "x":
            out[name + "_2"] = value
    return out


def reference(
    x, mem, mem_norm, l0_norm, l0_w_in, l0_a_vnorm, l0_a_ws, l0_a_bs, l0_b_qnorm, l0_b_knorm,
    l0_b_lq1, l0_b_lk1, l0_b_lq2, l0_b_lk2, l0_b_subln, l0_m_wkv, l0_m_qnorm, l0_m_knorm,
    l0_w_out, l1_norm, l1_w_in, l1_c_conv_w, l1_c_conv_b, l1_c_norm, l1_d_qnorm, l1_d_knorm,
    l1_d_cmp_pos_k, l1_d_cmp_w1_k, l1_d_cmp_w2_k, l1_d_cmp_pos_v, l1_d_cmp_w1_v, l1_d_cmp_w2_v,
    l1_m_wkv, l1_m_qnorm, l1_m_knorm, l1_w_out, c_2, positions_2, ada_w_2, ada_b_2,
    norm_mix_g_2, norm_ffn_g_2, lru_w_in_2, lru_conv_w_2, lru_conv_b_2, lru_wa_2, lru_ba_2,
    lru_wx_2, lru_bx_2, lru_lambda_2, lru_w_out_2, kv_ada_w_2, kv_ada_b_2, kv_norm_g_2,
    mla_w_dkv_2, mla_w_kr_2, mla_kv_latent_g_2, mla_w_uk_2, mla_w_uv_2, mla_w_dq_2,
    mla_q_latent_g_2, mla_w_uq_2, mla_w_o_2, peer_w_q_2, peer_sub_keys_2, peer_u_2, peer_v_2,
    final_g_2,
):
    x = first_block(
        x, mem, mem_norm, l0_norm, l0_w_in, l0_a_vnorm, l0_a_ws, l0_a_bs, l0_b_qnorm,
        l0_b_knorm, l0_b_lq1, l0_b_lk1, l0_b_lq2, l0_b_lk2, l0_b_subln, l0_m_wkv, l0_m_qnorm,
        l0_m_knorm, l0_w_out, l1_norm, l1_w_in, l1_c_conv_w, l1_c_conv_b, l1_c_norm, l1_d_qnorm,
        l1_d_knorm, l1_d_cmp_pos_k, l1_d_cmp_w1_k, l1_d_cmp_w2_k, l1_d_cmp_pos_v, l1_d_cmp_w1_v,
        l1_d_cmp_w2_v, l1_m_wkv, l1_m_qnorm, l1_m_knorm, l1_w_out,
    )
    return second_block(
        x, c_2, positions_2, ada_w_2, ada_b_2, norm_mix_g_2, norm_ffn_g_2, lru_w_in_2,
        lru_conv_w_2, lru_conv_b_2, lru_wa_2, lru_ba_2, lru_wx_2, lru_bx_2, lru_lambda_2,
        lru_w_out_2, kv_ada_w_2, kv_ada_b_2, kv_norm_g_2, mla_w_dkv_2, mla_w_kr_2,
        mla_kv_latent_g_2, mla_w_uk_2, mla_w_uv_2, mla_w_dq_2, mla_q_latent_g_2, mla_w_uq_2,
        mla_w_o_2, peer_w_q_2, peer_sub_keys_2, peer_u_2, peer_v_2, final_g_2,
    )


_drawn_inputs = setup_inputs


def setup_inputs(seed=0):
    import zlib

    import numpy as np

    out = dict(_drawn_inputs(seed))
    spreads = {}
    factors = {'mem_norm': 7.841,
     'l0_a_vnorm': 4.243,
     'l0_b_qnorm': 2.963,
     'l0_b_knorm': 2.703,
     'l0_b_lk1': 2.986,
     'l0_b_lq2': 8.0,
     'l0_b_subln': 3.196,
     'l0_m_qnorm': 8.0,
     'l0_m_knorm': 8.0,
     'l1_c_conv_b': 3.689,
     'l1_c_norm': 3.106,
     'l1_d_qnorm': 7.143,
     'l1_d_knorm': 7.319,
     'l1_d_cmp_pos_k': 8.0,
     'l1_d_cmp_pos_v': 8.0,
     'l1_m_qnorm': 8.0,
     'l1_m_knorm': 8.0,
     'norm_mix_g_2': 2.896,
     'norm_ffn_g_2': 3.319,
     'lru_ba_2': 8.0,
     'lru_bx_2': 5.959,
     'kv_ada_b_2': 6.417,
     'kv_norm_g_2': 8.0,
     'mla_kv_latent_g_2': 8.0,
     'mla_q_latent_g_2': 8.0,
     'final_g_2': 2.812}
    for name, (base, spread) in spreads.items():
        noise = np.random.default_rng([zlib.crc32(name.encode()), seed]).standard_normal(out[name].shape)
        drawn = base * np.exp(spread * noise) if base else spread * noise
        out[name] = __import__('jax').numpy.asarray(drawn.astype(out[name].dtype))
    for name, factor in factors.items():
        out[name] = (out[name] * factor).astype(out[name].dtype)
    return out
```

```python
import math
from contextlib import ExitStack

import numpy as np
import concourse.bass as bass
from concourse import mybir

F32 = mybir.dt.float32
F32R = mybir.dt.float32r
I32 = mybir.dt.int32
U32 = mybir.dt.uint32
ALU = mybir.AluOpType
ACT = mybir.ActivationFunctionType
AX = mybir.AxisListType

P = 128
S = 256
NT = S // P
D = 1024
KD = D // P
EPS = 1e-6
NEG = -1e30
TINY = 1.1754944e-38

B_HEADS, B_DK, B_DV = 8, 32, 64
M_HEADS, HD = 4, 64
D_HEADS, D_GROUPS = 8, 2
A_GROUPS = 4
C_KERNEL, C_BLOCKS = 31, 4
CMP_BLOCK, CMP_STRIDE = 32, 16
N_CMP = (S - CMP_BLOCK) // CMP_STRIDE + 1
MIX = 1280
KMIX = MIX // P
LAM_INIT = 0.8 - 0.6 * math.exp(-0.3)
ROPE_THETA, ROPE_THETA_2 = 500000.0, 10000.0

EVEN_IN, ODD_IN = 4096, 3864
CONV_WIDTH, LRU_HEADS = 4, 4
MLA_HEADS, QK_NOPE, QK_ROPE, V_HEAD = 16, 64, 32, 64
QK = QK_NOPE + QK_ROPE
Q_LORA, KV_LORA = 384, 256
PEER_HEADS, N_KEYS, TOPK = 8, 128, 16
SLOTS = PEER_HEADS * TOPK
TWO_PI = 2.0 * math.pi

EVEN_RANGES = [(0, 1024, "gelu_tanh"), (1024, 1536, "silu"), (1536, 3072, "copy"), (3072, 3584, "silu"),
               (3584, 3840, "copy"), (3840, 4096, "silu")]
ODD_RANGES = [(0, 512, "copy"), (512, 1024, "sigmoid"), (1024, 1536, "silu"), (1536, 2816, "copy"),
              (2816, 2840, "sigmoid"), (2840, 3352, "silu"), (3352, 3608, "copy"), (3608, 3864, "silu")]
FUNCS = {"gelu_tanh": ACT.Gelu_apprx_tanh, "silu": ACT.Silu, "sigmoid": ACT.Sigmoid, "copy": ACT.Copy}

VECTORS = [("mem_norm", 8), ("l0_norm", 8), ("l1_norm", 8), ("l0_a_bs", 4), ("l1_c_conv_w", 124),
           ("l1_c_conv_b", 4), ("norm_mix_g_2", 16), ("norm_ffn_g_2", 16), ("kv_norm_g_2", 8),
           ("lru_conv_w_2", 32), ("lru_conv_b_2", 8), ("lru_ba_2", 8), ("lru_bx_2", 8),
           ("lru_lambda_2", 8), ("c_2", 8),
           ("ada_b_2", 96), ("kv_ada_b_2", 16)]


def rope_constants():
    pos = np.arange(S, dtype=np.float32)
    end = (np.arange(N_CMP) * CMP_STRIDE + CMP_BLOCK - 1).astype(np.float32)
    out = {}
    for name, p, half in (("rope4", pos, 4), ("rope8", pos, 8), ("ropec", end, 8)):
        inv = (np.float32(ROPE_THETA) ** (-np.arange(half, dtype=np.float32) / half)).astype(np.float32)
        ang = (p[:, None] * inv[None, :]).astype(np.float32)
        out[name] = np.concatenate([np.cos(ang), np.sin(ang)], axis=1).astype(np.float32)
    half = QK_ROPE // 2
    out["freqs"] = (np.float32(ROPE_THETA_2) ** (-np.arange(half, dtype=np.float32) / half)).astype(np.float32)
    return out


class Ordered:

    def __init__(self, own, counts):
        self.own, self.counts, self.eng = own, counts, None

    def on(self, eng):
        self.eng = eng
        return self

    def __call__(self, ins, sem=None, wait=True):
        sem = self.own if sem is None else sem
        ins.then_inc(sem, 1)
        n = self.counts.get(sem.num, 0) + 1
        self.counts[sem.num] = n
        if wait:
            self.eng.wait_ge(sem, n)
        return n


def build(nc, I, out, upto=99):
    ctx = ExitStack()
    counts = {}
    lasting = lambda name: ctx.enter_context(nc.semaphore(name))
    of_stage, cleared = [], []

    def sem(name):
        of_stage.append(nc.alloc_semaphore(name))
        return of_stage[-1]

    class StageBlock:

        def __enter__(self):
            self.block = nc.Block()
            return self.block.__enter__()

        def __exit__(self, *exc):
            self.block.__exit__(*exc)
            for s in cleared:
                nc.release_semaphore(s)
            cleared[:] = of_stage
            of_stage.clear()
            for s in cleared:
                nc.sync.sem_clear(s)
                counts.pop(s.num, None)

    BASE = 16512
    TOP = 229344
    at = [BASE]

    def place(name, shape, dt=F32, size=None):
        n = size or int(np.prod(shape[1:])) * 4
        t = nc.alloc_sbuf_tensor_at(name, list(shape), dt, offset=at[0])
        at[0] += (n + 31) // 32 * 32
        return t

    NV = sum(n for _, n in VECTORS)
    NVT = (NV + P - 1) // P
    COLS = place("cols", [P, NVT * P])
    MOD = place("mod", [P, 2 * 48 + 16])
    GM = place("gain_mod", [P, 5, KD])
    ident = place("ident", [P, P])
    iota = place("iota_row", [P, P])
    stats = place("stats", [P, 64])
    CS = place("silu_c", [P, KD])
    X = place("x_res", [P, NT, D])
    AUX = at[0]
    HTH = place("h_t_high", [P, KD, S], F32R)
    HTL = place("h_t_low", [P, KD, S], F32R)
    at[0] = AUX
    GROW = place("gate_row", [P, D])
    TMP = place("gated", [P, 512])
    RINGS = at[0] = AUX + 4 * KD * S * 2
    HT = place("h_t", [P, KD, S])
    slot_e1 = place("slot_e1", [P, S])
    slot_e2 = place("slot_e2", [P, S])
    slot_g = place("slot_gate", [P, S])
    PANELS = at[0]
    col = {}
    n = 0
    for name, rows in VECTORS:
        col[name] = n
        n += rows

    def C(name, i=0, n=1):
        return COLS[:, col[name] + i:col[name] + i + n]

    SLOT = KMIX * 512 * 4
    WORK = max(PANELS + 2 * SLOT, RINGS + 53248)
    WORK_END = WORK + N_KEYS * S * 4
    assert WORK_END <= TOP, (WORK_END, TOP)
    slots = [nc.alloc_sbuf_tensor_at(f"panel{i}", [P, SLOT // 4], F32, offset=o)
             for i, o in enumerate((PANELS, PANELS + SLOT, WORK_END - SLOT))]

    class Zone:
        def __init__(self):
            self.at, self.n = WORK, 0

        def __call__(self, name, shape, dt=F32):
            self.n += 1
            t = nc.alloc_sbuf_tensor_at(f"{name}_{self.n}", list(shape), dt, offset=self.at)
            self.at += (int(np.prod(shape[1:])) * 4 + 31) // 32 * 32
            assert self.at <= WORK_END - SLOT, (name, self.at, WORK_END - SLOT)
            return t

    zone = Zone()
    banks = [nc.alloc_psum_tensor(f"bank{i}", [P, 512], F32) for i in range(8)]

    pe_order, act_order, dve_order, pool_order = (lasting(x) for x in ("pe_order", "act_order", "dve_order", "pool_order"))
    pe_f, act_f, dve_f, pool_f = (Ordered(s, counts) for s in (pe_order, act_order, dve_order, pool_order))
    loaded = [lasting(f"panel_loaded{i}") for i in range(3)]
    acc_ready = lasting("acc_ready")
    acc_free = {"a": lasting("acc_free_act"), "v": lasting("acc_free_dve")}
    small_loaded = lasting("small_loaded")
    small = [0]

    panels = []

    def panel(loads, groups):
        panels.append((loads, groups))
        return len(panels) - 1

    def rows_by_k(w, k, n0, n):
        view = lambda slot: slot[:, 0:k * n].rearrange("p (k n) -> p k n", k=k)
        return view, w[:, n0:n0 + n].rearrange("(k p) n -> p k n", p=P)

    def wide(w, k, total, groups=2, width=512):
        return [panel([rows_by_k(w, k, n0, min(width, total - n0))], groups) for n0 in range(0, total, width)]

    pn = {}
    pn["mkv"] = [panel([rows_by_k(I[f"l{l}_m_wkv"], KD, 0, 512)], 2) for l in range(2)]
    pn["even_in"] = wide(I["l0_w_in"], KD, EVEN_IN)
    pn["even_out"] = wide(I["l0_w_out"], KMIX, D)
    pn["odd_in"] = wide(I["l1_w_in"], KD, ODD_IN)

    def cmp_panel(w):
        def half(g):
            return (lambda slot: slot[64 * g:64 * g + 64, 0:CMP_BLOCK * P].rearrange("p (t h) -> p t h", h=P),
                    w.rearrange("(t d) h -> d t h", d=HD))
        return panel([half(0), half(1)], 1)

    pn["cmp"] = [cmp_panel(I["l1_d_cmp_w1_k"]), cmp_panel(I["l1_d_cmp_w1_v"])]
    pn["odd_out"] = wide(I["l1_w_out"], KMIX, D)
    pn["ada0"] = wide(I["ada_w_2"][0], KD, 6 * D, 1)
    pn["lru_in"] = wide(I["lru_w_in_2"][0], KD, 2 * D)

    def head_mats(w, o):
        view = lambda slot: slot[:, o:o + 2048].rearrange("p (h n) -> p h n", h=8)
        return view, w[0].rearrange("h (i p) j -> p (h i) j", p=P)

    pn["lru_gates"] = [panel([head_mats(I["lru_wa_2"], 0), head_mats(I["lru_wx_2"], 2048)], 8)]
    pn["lru_out"] = wide(I["lru_w_out_2"][0], KD, D)
    pn["peer_q0"] = wide(I["peer_w_q_2"][0], KD, 2 * D)
    pn["kv_ada"] = wide(I["kv_ada_w_2"], KD, 2 * D, 1)
    pn["ada1"] = wide(I["ada_w_2"][1], KD, 6 * D, 1)

    def side(w, k, o, n, total):
        view = lambda slot: slot[:, 0:k * total].rearrange("p (k n) -> p k n", k=k)[:, :, o:o + n]
        return view, w.rearrange("(k p) n -> p k n", p=P)

    pn["dkv"] = [panel([side(I["mla_w_dkv_2"], KD, 0, KV_LORA, 288), side(I["mla_w_kr_2"], KD, KV_LORA, 32, 288)], 2)]

    def stacked(w, k, o, n):
        view = lambda slot: slot[:, o * n:(o + k) * n].rearrange("p (k n) -> p k n", k=k)
        return view, w.rearrange("(k p) n -> p k n", p=P)

    pn["ukv"] = [panel([stacked(I["mla_w_uk_2"], 2, 0, D), stacked(I["mla_w_uv_2"], 2, 2, D)], 8)]
    pn["dq"] = [panel([rows_by_k(I["mla_w_dq_2"][0], KD, 0, Q_LORA)], 2)]
    pn["uq"] = [panel([rows_by_k(I["mla_w_uq_2"][0], 3, 0, MLA_HEADS * QK)], 6)]
    pn["mla_out"] = wide(I["mla_w_o_2"][0], KD, D)
    pn["peer_q1"] = wide(I["peer_w_q_2"][1], KD, 2 * D)

    first_group, dma_value = [0], []
    slot_count = [0, 0, 0]
    for i, (loads, groups) in enumerate(panels):
        first_group.append(first_group[-1] + groups)
        slot_count[i % 3] += 16 * len(loads)
        dma_value.append(slot_count[i % 3])
    issued = [0]

    def load_panels(sp, last):
        while issued[0] <= min(last, len(panels) - 1):
            i = issued[0]
            if i >= 3:
                sp.wait_ge(acc_ready, first_group[i - 2])
            for view, src in panels[i][0]:
                sp.dma_start(view(slots[i % 3]), src).then_inc(loaded[i % 3], 16)
            issued[0] += 1

    def wait_panel(pe, i):
        pe.wait_ge(loaded[i % 3], dma_value[i])

    owners = []

    def acc_bank(g):
        return banks[g % 4]

    def wait_acc_free(pe, g):
        if g >= 4:
            o = owners[g - 4]
            pe.wait_ge(acc_free[o], owners[:g - 3].count(o))

    def load_small(eng, pairs):
        for dst, src in pairs:
            eng.dma_start(dst, src).then_inc(small_loaded, 16)
            small[0] += 16

    def bcast(vec):
        return vec.partition_broadcast(P)

    class Stage:
        count = 0

    def stage():
        Stage.count += 1
        return Stage.count <= upto


    def project(name, lhs, evac, owner, K=KD, width=None, chunks=None, ahead=3):
        if not stage():
            return
        ps = pn[name]
        if chunks is None:
            ns = [min(512, width - 512 * i) for i in range(len(ps))]
            chunks = [(i, (lambda slot, n=n: slot[:, 0:K * n].rearrange("p (k n) -> p k n", k=K)), K)
                      for i, n in enumerate(ns)]
        g0 = first_group[ps[0]]
        todo = [(i, ps[c], view, k, t) for i, (c, view, k) in enumerate(chunks) for t in range(NT)]
        owners.extend(owner(i, t) for i, _, _, _, t in todo)
        with StageBlock() as block:
            @block.sync
            def _(sp):
                load_panels(sp, ps[-1] + ahead)

            @block.tensor
            def _(pe):
                for j, (i, p, view, k, t) in enumerate(todo):
                    w = view(slots[p % 3])
                    n = w.shape[2]
                    wait_panel(pe, p)
                    wait_acc_free(pe, g0 + j)
                    for q in range(k):
                        last = nc.tensor.matmul(acc_bank(g0 + j)[:, 0:n], lhs(i, q, t), w[:, q, :],
                                                start=(q == 0), stop=(q == k - 1))
                    last.then_inc(acc_ready, 1)

            for who, get, eng_name in (("a", act_f, "scalar"), ("v", dve_f, "vector")):
                def body(eng, who=who, get=get):
                    f = get.on(eng)
                    for j, (i, _, _, _, t) in enumerate(todo):
                        if owners[g0 + j] == who:
                            eng.wait_ge(acc_ready, g0 + j + 1)
                            evac(f, who, i, t, acc_bank(g0 + j), acc_free[who])
                (block.scalar if who == "a" else block.vector)(body)

    def copy_evac(dst, c_of):
        def evac(f, who, i, t, bank, free):
            c0, n = c_of(i)
            if who == "a":
                f(nc.scalar.activation(dst[:, t, c0:c0 + n], bank[:, 0:n], ACT.Copy), free, wait=False)
            else:
                f(nc.vector.tensor_copy(dst[:, t, c0:c0 + n], bank[:, 0:n]), free, wait=False)
        return evac

    def project_t(name, w_of, groups, ks, rhs, evac, owner, ahead=3):
        if not stage():
            return
        ps = pn[name]
        g0 = first_group[ps[0]]
        per = groups // len(ps)
        owners.extend(owner(g) for g in range(groups))
        with StageBlock() as block:
            @block.sync
            def _(sp):
                load_panels(sp, ps[-1] + ahead)

            @block.tensor
            def _(pe):
                for g in range(groups):
                    p = ps[g // per]
                    wait_panel(pe, p)
                    wait_acc_free(pe, g0 + g)
                    for h in range(2):
                        for k in range(ks):
                            last = nc.tensor.matmul(acc_bank(g0 + g)[:, h * S:(h + 1) * S],
                                                    w_of(slots[p % 3], g, h, k), rhs(g, h, k),
                                                    start=(k == 0), stop=(k == ks - 1))
                    last.then_inc(acc_ready, 1)

            def body(eng, who, get):
                f = get.on(eng)
                for g in range(groups):
                    if owners[g0 + g] == who:
                        eng.wait_ge(acc_ready, g0 + g + 1)
                        evac(f, who, g, acc_bank(g0 + g), acc_free[who])

            @block.scalar
            def _(act):
                body(act, "a", act_f)

            @block.vector
            def _(dve):
                body(dve, "v", dve_f)

    def project_col(name, rhs_cols, dst, bias, ahead=3):
        if not stage():
            return
        ps = pn[name]
        g0 = first_group[ps[0]]
        owners.extend("v" for _ in ps)
        with StageBlock() as block:
            @block.sync
            def _(sp):
                load_panels(sp, ps[-1] + ahead)

            @block.tensor
            def _(pe):
                for i, p in enumerate(ps):
                    w = slots[p % 3][:, 0:KD * 512].rearrange("p (k n) -> p k n", k=KD)
                    wait_panel(pe, p)
                    wait_acc_free(pe, g0 + i)
                    for j in range(4):
                        for k in range(KD):
                            last = nc.tensor.matmul(acc_bank(g0 + i)[:, j:j + 1], w[:, k, j * P:(j + 1) * P],
                                                    rhs_cols[:, k:k + 1], start=(k == 0), stop=(k == KD - 1))
                    last.then_inc(acc_ready, 1)

            @block.vector
            def _(dve):
                f = dve_f.on(dve)
                for i, p in enumerate(ps):
                    dve.wait_ge(acc_ready, g0 + i + 1)
                    f(nc.vector.tensor_tensor(dst[:, 4 * i:4 * i + 4], acc_bank(g0 + i)[:, 0:4],
                                              bias[:, 4 * i:4 * i + 4], ALU.add), acc_free["v"], wait=False)

    def inverse_root(f, v, y, t, mean_done, root_done, eng):
        eng.wait_ge(root_done, 1)
        f(nc.vector.reciprocal(y, y))
        f(nc.vector.tensor_tensor(t, y, y, ALU.mult))
        f(nc.vector.tensor_tensor(t, t, v, ALU.mult))
        f(nc.vector.tensor_scalar(t, t, -0.5, 1.5, ALU.mult, ALU.add))
        f(nc.vector.tensor_tensor(y, y, t, ALU.mult))

    def norm_transpose(src, dst, jobs, width=D):
        if not stage():
            return
        K = width // P
        mark = zone.at
        xn = zone("normed", [P, NT, width])
        n = Stage.count
        sq_done, mean_done, root_done, xn_done, tr_done, tr_free = (
            sem(f"norm{n}_{x}") for x in ("squares", "mean", "root", "normed", "transposed", "free"))
        with StageBlock() as block:
            @block.scalar
            def _(act):
                f = act_f.on(act)
                for t in range(NT):
                    f(nc.scalar.activation(xn[:, t, :], src[:, t, 0:width], ACT.Square,
                                           accum_out=stats[:, t:t + 1]), sq_done)
                act.wait_ge(mean_done, 1)
                f(nc.scalar.activation(stats[:, 4:4 + NT], stats[:, 0:NT], ACT.Sqrt), root_done)

            @block.vector
            def _(dve):
                f = dve_f.on(dve)
                dve.wait_ge(sq_done, NT)
                f(nc.vector.tensor_scalar(stats[:, 0:NT], stats[:, 0:NT], 1.0 / width, EPS, ALU.mult, ALU.add), mean_done)
                inverse_root(f, stats[:, 0:NT], stats[:, 4:4 + NT], stats[:, 8:8 + NT], mean_done, root_done, dve)
                for t in range(NT):
                    f(nc.vector.tensor_scalar(xn[:, t, :], src[:, t, 0:width], stats[:, 4 + t:5 + t], None, ALU.mult),
                      xn_done)
                for k in range(K):
                    dve.wait_ge(tr_done, (k | 1) + 1)
                    got = banks[4 + (k // 2) % 4][:, (k % 2) * S:(k % 2 + 1) * S]
                    for d, mult, add in jobs:
                        if add is None:
                            ins = nc.vector.tensor_scalar(d[:, k, :], got, mult[:, k:k + 1], None, ALU.mult)
                        else:
                            ins = nc.vector.tensor_scalar(d[:, k, :], got, mult[:, k:k + 1], add[:, k:k + 1],
                                                          ALU.mult, ALU.add)
                        f(ins, wait=False)

            @block.tensor
            def _(pe):
                pe.wait_ge(xn_done, NT)
                for k in range(K):
                    for t in range(NT):
                        c = (k % 2) * S + t * P
                        last = nc.tensor.transpose(banks[4 + (k // 2) % 4][:, c:c + P],
                                                   xn[:, t, k * P:(k + 1) * P], ident[:, :])
                    last.then_inc(tr_done, 1)
        zone.at = mark

    def transpose_all(pieces, loads=()):
        if not stage():
            return
        n = Stage.count
        tr_done = sem(f"tr{n}_done")
        freed = {"a": sem(f"tr{n}_free_act"), "v": sem(f"tr{n}_free_dve")}
        v0 = small[0] + 16 * len(loads)
        with StageBlock() as block:
            @block.sync
            def _(sp):
                load_small(sp, loads)

            @block.tensor
            def _(pe):
                if loads:
                    pe.wait_ge(small_loaded, v0)
                for i, (dst, src) in enumerate(pieces):
                    r, c = src.shape
                    if i >= 8:
                        who = "a" if i % 2 == 0 else "v"
                        pe.wait_ge(freed[who], (i - 8) // 2 + 1)
                    nc.tensor.transpose(banks[i % 8][0:c, 0:r], src, ident[0:r, 0:r]).then_inc(tr_done, 1)

            def body(eng, who, get):
                f = get.on(eng)
                for i, (dst, src) in enumerate(pieces):
                    if ("a" if i % 2 == 0 else "v") != who:
                        continue
                    r, c = src.shape
                    eng.wait_ge(tr_done, i + 1)
                    if who == "a":
                        ins = nc.scalar.activation(dst, banks[i % 8][0:c, 0:r], ACT.Copy)
                    else:
                        ins = nc.vector.tensor_copy(dst, banks[i % 8][0:c, 0:r])
                    f(ins, freed[who], wait=False)

            @block.scalar
            def _(act):
                body(act, "a", act_f)

            @block.vector
            def _(dve):
                body(dve, "v", dve_f)

    def group_norms(f, eng, ss, todo, mean_done, root_done, sq):
        p = todo[0][0].shape[0]
        c = 0
        for i, (src, dst, gain, d) in enumerate(todo):
            G = src.shape[1]
            view = sq[0:p, 0:G * d].rearrange("p (g d) -> p g d", d=d)
            f(nc.vector.tensor_tensor(view, src, src, ALU.mult))
            f(nc.vector.tensor_reduce(ss[0:p, 0, c:c + G], view, AX.X, ALU.add))
            f(nc.vector.tensor_scalar(ss[0:p, 0, c:c + G], ss[0:p, 0, c:c + G], 1.0 / d, EPS, ALU.mult, ALU.add),
              mean_done if i == len(todo) - 1 else None)
            c += G
        inverse_root(f, ss[0:p, 0, 0:c], ss[0:p, 1, 0:c], ss[0:p, 2, 0:c], mean_done, root_done, eng)
        c = 0
        for src, dst, gain, d in todo:
            G = src.shape[1]
            f(nc.vector.tensor_tensor(dst, src, ss[0:p, 1, c:c + G].unsqueeze(2).broadcast_to([p, G, d]), ALU.mult))
            if len(gain.shape) == 2:
                gain = gain[0:p].unsqueeze(1).broadcast_to([p, G, d])
            f(nc.vector.tensor_tensor(dst, dst, gain, ALU.mult))
            c += G

    def group_roots(f, eng, ss, todo, mean_done, root_done):
        p, c = todo[0][0].shape[0], sum(src.shape[1] for src, _, _, _ in todo)
        eng.wait_ge(mean_done, 1)
        f(nc.scalar.activation(ss[0:p, 1, 0:c], ss[0:p, 0, 0:c], ACT.Sqrt), root_done)

    def rope(f, x, cos, sin, half, tmp):
        p, G, _ = x.shape
        c = cos.unsqueeze(1).broadcast_to([p, G, half])
        s = sin.unsqueeze(1).broadcast_to([p, G, half])
        v = [tmp[0:p, i * G * half:(i + 1) * G * half].rearrange("p (g h) -> p g h", h=half) for i in range(4)]
        x1, x2 = x[:, :, 0:half], x[:, :, half:2 * half]
        f(nc.vector.tensor_tensor(v[0], x1, c, ALU.mult), wait=False)
        f(nc.vector.tensor_tensor(v[1], x2, s, ALU.mult), wait=False)
        f(nc.vector.tensor_tensor(v[2], x1, s, ALU.mult), wait=False)
        f(nc.vector.tensor_tensor(v[3], x2, c, ALU.mult))
        f(nc.vector.tensor_tensor(x1, v[0], v[1], ALU.subtract), wait=False)
        f(nc.vector.tensor_tensor(x2, v[2], v[3], ALU.add))

    def attention(units):
        if not stage():
            return
        mark = zone.at
        n = Stage.count
        s_sb = [zone("scores", [P, S]) for _ in range(2)]
        p_sb = [zone("probs", [P, S]) for _ in range(2)]
        pt_sb = [zone("probs_t", [P, NT, P]) for _ in range(2)]
        st = zone("softmax_stats", [P, 4, 4])
        scored, maxed, exped, turned, pt_ready, pv_done, out_done, s_taken = (
            sem(f"att{n}_{x}") for x in ("scored", "maxed", "exped", "turned", "pt_ready", "pv_done", "out_done", "s_taken"))
        N = len(units)
        tiles = lambda u: [(k, min(P, u["nk"] - k * P)) for k in range((u["nk"] + P - 1) // P)]
        with StageBlock() as block:
            @block.tensor
            def _(pe):
                for i in range(N + 2):
                    if i < N:
                        u = units[i]
                        if i >= 2:
                            pe.wait_ge(s_taken, i - 1)
                        nc.tensor.matmul(banks[i % 2][:, 0:u["nk"]], u["qT"], u["kT"], start=True, stop=True)\
                            .then_inc(scored, 1)
                    if 1 <= i <= N:
                        j, u = i - 1, units[i - 1]
                        pe.wait_ge(exped, j + 1)
                        if j >= 2:
                            pe.wait_ge(pt_ready, j - 1)
                        for k, m in tiles(u):
                            last = nc.tensor.transpose(banks[2 + j % 2][0:m, k * P:(k + 1) * P],
                                                       p_sb[j % 2][:, k * P:k * P + m], ident[:, :])
                        last.then_inc(turned, 1)
                    if i >= 2:
                        j, u = i - 2, units[i - 2]
                        pe.wait_ge(pt_ready, j + 1)
                        if j >= 2:
                            pe.wait_ge(out_done, j - 1)
                        tl = tiles(u)
                        for k, m in tl:
                            last = nc.tensor.matmul(banks[4 + j % 2][:, 0:u["v"][0].shape[1]], pt_sb[j % 2][0:m, k, :],
                                                    u["v"][k], start=(k == 0), stop=(k == len(tl) - 1))
                        last.then_inc(pv_done, 1)

            @block.scalar
            def _(act):
                f = act_f.on(act)
                for i in range(N + 1):
                    if i < N:
                        u = units[i]
                        act.wait_ge(maxed, i + 1)
                        if i >= 2:
                            act.wait_ge(turned, i - 1)
                        f(nc.scalar.activation(p_sb[i % 2][:, 0:u["nk"]], s_sb[i % 2][:, 0:u["nk"]], ACT.Exp,
                                               bias=st[:, i % 4, 0:1], accum_out=st[:, i % 4, 1:2]), exped)
                    if i >= 1:
                        j, u = i - 1, units[i - 1]
                        act.wait_ge(turned, j + 1)
                        if j >= 2:
                            act.wait_ge(pv_done, j - 1)
                        m = min(P, u["nk"])
                        w = len(tiles(u)) * P
                        f(nc.scalar.activation(pt_sb[j % 2][0:m, :, :].rearrange("p a b -> p (a b)")[:, 0:w],
                                               banks[2 + j % 2][0:m, 0:w], ACT.Copy), pt_ready)

            @block.vector
            def _(dve):
                f = dve_f.on(dve)
                for i in range(N + 3):
                    if i < N:
                        u = units[i]
                        nk = u["nk"]
                        dve.wait_ge(scored, i + 1)
                        if i >= 2:
                            dve.wait_ge(exped, i - 1)
                        if u["mask"] is None:
                            ins = nc.vector.tensor_scalar(s_sb[i % 2][:, 0:nk], banks[i % 2][:, 0:nk], u["scale"], None,
                                                          ALU.mult)
                        else:
                            ins = nc.vector.scalar_tensor_tensor(s_sb[i % 2][:, 0:nk], banks[i % 2][:, 0:nk], u["scale"],
                                                                 u["mask"], ALU.mult, ALU.add)
                        f(ins, s_taken)
                        ins = nc.vector.tensor_reduce(st[:, i % 4, 0:1], s_sb[i % 2][:, 0:nk], AX.X, ALU.max, negate=True)
                        if u["guard"]:
                            f(ins)
                            ins = nc.vector.tensor_scalar(st[:, i % 4, 0:1], st[:, i % 4, 0:1], 1e29, None, ALU.min)
                        f(ins, maxed)
                    if i >= 3:
                        j, u = i - 3, units[i - 3]
                        dve.wait_ge(pv_done, j + 1)
                        total, inv = st[:, j % 4, 1:2], st[:, j % 4, 2:3]
                        if u["guard"]:
                            f(nc.vector.tensor_scalar(total, total, TINY, None, ALU.max))
                        f(nc.vector.reciprocal(inv, total))
                        if u["coef"] is not None:
                            f(nc.vector.tensor_tensor(inv, inv, u["coef"], ALU.mult))
                        bank = banks[4 + j % 2][:, 0:u["v"][0].shape[1]]
                        if u["add"]:
                            f(nc.vector.scalar_tensor_tensor(u["out"], bank, inv, u["out"], ALU.mult, ALU.add), out_done)
                        else:
                            f(nc.vector.tensor_scalar(u["out"], bank, inv, None, ALU.mult), out_done)
        zone.at = mark

    def elementwise(dve_body=None, act_body=None, loads=(), pool_body=None, pe_body=None, prefetch_to=None):
        if not stage():
            return
        v0 = small[0] + 16 * len(loads)
        with StageBlock() as block:
            @block.sync
            def _(sp):
                load_small(sp, loads)
                if prefetch_to is not None:
                    load_panels(sp, prefetch_to)

            if act_body:
                @block.scalar
                def _(act):
                    if loads:
                        act.wait_ge(small_loaded, v0)
                    act_body(act_f.on(act), act)

            if dve_body:
                @block.vector
                def _(dve):
                    if loads:
                        dve.wait_ge(small_loaded, v0)
                    dve_body(dve_f.on(dve), dve)

            if pool_body:
                @block.gpsimd
                def _(pool):
                    if loads:
                        pool.wait_ge(small_loaded, v0)
                    pool_body(pool_f.on(pool), pool)

            if pe_body:
                @block.tensor
                def _(pe):
                    if loads:
                        pe.wait_ge(small_loaded, v0)
                    pe_body(pe_f.on(pe), pe)

    causal = zone("causal_mask", [P, S])
    cmpmask = zone("cmp_mask", [P, NT, N_CMP])
    masks_end = zone.at
    memx = zone("mem_rows", [P, NT, D])
    staged = zone("vector_rows", [P, NVT, P])
    vec_dmas, row = [], 0
    for name, rows in VECTORS:
        src = I[name]
        flat = src.rearrange(" ".join(f"d{i}" for i in range(len(src.shape))) + " -> (" +
                             " ".join(f"d{i}" for i in range(len(src.shape))) + ")") if len(src.shape) > 1 else src
        flat = flat.rearrange("(r c) -> r c", c=P)
        done = 0
        while done < rows:
            tile, r = divmod(row, P)
            m = min(rows - done, P - r)
            vec_dmas.append((staged[r:r + m, tile, :], flat[done:done + m, :]))
            done += m
            row += m

    def pool_constants(f, pool):
        f(nc.gpsimd.memset(ident[:, :], 0.0))
        f(nc.gpsimd.affine_select(out=ident[:, :], in_=ident[:, :], compare_op=ALU.not_equal, fill=1.0, base=0,
                                  pattern=[[-1, P]], channel_multiplier=1))
        f(nc.gpsimd.memset(causal[:, :], 0.0))
        f(nc.gpsimd.affine_select(out=causal[:, P:S], in_=causal[:, P:S], compare_op=ALU.is_ge, fill=NEG, base=0,
                                  pattern=[[-1, P]], channel_multiplier=1))
        f(nc.gpsimd.memset(cmpmask[:, :, :], 0.0))
        f(nc.gpsimd.affine_select(out=cmpmask[:, :, :], in_=cmpmask[:, :, :], compare_op=ALU.is_ge, fill=NEG,
                                  base=-(CMP_BLOCK - 1), pattern=[[P, NT], [-CMP_STRIDE, N_CMP]], channel_multiplier=1))
        f(nc.gpsimd.iota(iota[:, :], pattern=[[1, P]], base=0, channel_multiplier=0,
                         allow_small_or_imprecise_dtypes=True))

    elementwise(pool_body=pool_constants,
                loads=[(X[:, :, :], I["x"][0].rearrange("(t p) d -> p t d", p=P)),
                       (memx[:, :, :], I["mem"][0].rearrange("(t p) d -> p t d", p=P))] + vec_dmas,
                prefetch_to=2)
    last_rows = NV - (NVT - 1) * P
    transpose_all([(COLS[:, t * P:t * P + (P if t < NVT - 1 else last_rows)],
                    staged[0:(P if t < NVT - 1 else last_rows), t, :]) for t in range(NVT)])

    norm_transpose(memx, HT, [(HT, C("mem_norm", 0, 8), None)])
    zone.at = masks_end
    MKT = zone("mem_k_t", [P, 2, 2, S])
    MV = zone("mem_v", [P, 2, NT, 256])
    keep_first = zone.at
    kv_nat = zone("mem_kv", [P, NT, 2, 512])
    ht = lambda i, k, t: HT[:, k, t * P:(t + 1) * P]
    project("mkv", ht,
            lambda f, who, i, t, bank, free: f(
                nc.scalar.activation(kv_nat[:, t, i, :], bank[:, :], ACT.Copy) if who == "a" else
                nc.vector.tensor_copy(kv_nat[:, t, i, :], bank[:, :]), free, wait=False),
            lambda i, t: "av"[t], width=1024)
    gk = zone("mem_gains", [P, 2, HD])
    sq = zone("squares", [P, D])
    ss = zone("sums", [P, 3, 80])

    def norm_stage(todo, loads=(), after=None, before=None):
        if Stage.count >= upto:
            stage()
            return
        n = Stage.count
        mean_done, root_done = sem(f"gn{n}_mean"), sem(f"gn{n}_root")

        def dve_body(f, dve):
            if before:
                before(f, dve)
            group_norms(f, dve, ss, todo, mean_done, root_done, sq)
            if after:
                after(f, dve)

        elementwise(dve_body, lambda f, act: group_roots(f, act, ss, todo, mean_done, root_done), loads=loads)

    def mem_copy_v(f, dve):
        for t in range(NT):
            for l in range(2):
                f(nc.vector.tensor_copy(MV[:, l, t, :], kv_nat[:, t, l, 256:512]), wait=False)

    norm_stage([(kv_nat[:, t, l, 0:256].rearrange("p (h d) -> p h d", d=HD),
                 kv_nat[:, t, l, 0:256].rearrange("p (h d) -> p h d", d=HD), gk[:, l, :], HD)
                for t in range(NT) for l in range(2)],
               loads=[(gk[:, l, :], bcast(I[f"l{l}_m_knorm"])) for l in range(2)], after=mem_copy_v)
    transpose_all([(MKT[:, l, b, t * P:(t + 1) * P], kv_nat[:, t, l, b * P:(b + 1) * P])
                   for l in range(2) for b in range(2) for t in range(NT)])

    def ranges_evac(dst, ranges, width):
        def evac(f, who, i, t, bank, free):
            c0 = i * 512
            n = min(512, width - c0)
            parts = [(max(a, c0), min(b, c0 + n), fn) for a, b, fn in ranges if max(a, c0) < min(b, c0 + n)]
            for j, (a, b, fn) in enumerate(parts):
                last = j == len(parts) - 1
                if who == "v":
                    ins = nc.vector.tensor_copy(dst[:, t, a:b], bank[:, a - c0:b - c0])
                else:
                    ins = nc.scalar.activation(dst[:, t, a:b], bank[:, a - c0:b - c0], FUNCS[fn])
                f(ins, free if last else None, wait=False)
        return evac

    def ranges_owner(ranges, width):
        def owner(i, t):
            c0 = i * 512
            n = min(512, width - c0)
            return "v" if all(fn == "copy" for a, b, fn in ranges if max(a, c0) < min(b, c0 + n)) else "a"
        return owner

    def memory_units(l, qt, outs):
        return [dict(qT=qt[64 * (h % 2):64 * (h % 2) + 64, h // 2, t * P:(t + 1) * P],
                     kT=MKT[64 * (h % 2):64 * (h % 2) + 64, l, h // 2, :], nk=S,
                     v=[MV[:, l, k, h * HD:(h + 1) * HD] for k in range(NT)], scale=HD ** -0.5, mask=None,
                     coef=None, out=outs[:, t, h * HD:(h + 1) * HD], add=False, guard=False)
                for h in range(M_HEADS) for t in range(NT)]

    def out_project(name, K, mixt, gate=None):
        def evac(f, who, i, t, bank, free):
            xs = X[:, t, i * 512:(i + 1) * 512]
            if gate is None:
                f(nc.vector.tensor_tensor(xs, bank[:, :], xs, ALU.add), free)
            else:
                tmp = gate[1][:, 0:512]
                f(nc.vector.tensor_tensor(tmp, bank[:, :], gate[0][:, i * 512:(i + 1) * 512], ALU.mult), free)
                f(nc.vector.tensor_tensor(xs, tmp, xs, ALU.add))
        project(name, lambda i, k, t: mixt[:, k, t * P:(t + 1) * P], evac, lambda i, t: "v", K=K, width=D)

    norm_transpose(X, HT, [(HT, C("l0_norm", 0, 8), None)])
    zone.at = keep_first
    ss = zone("sums", [P, 3, 80])
    P0 = zone("even_in", [P, NT, EVEN_IN])
    mix = zone("mix", [P, NT, MIX])
    project("even_in", ht, ranges_evac(P0, EVEN_RANGES, EVEN_IN), ranges_owner(EVEN_RANGES, EVEN_IN), width=EVEN_IN)

    mark0 = zone.at
    vgain = zone("a_vgain", [P, 512])
    sq = zone("squares", [P, D])
    ws = zone("a_ws", [P, A_GROUPS, P])
    wst = zone("a_ws_t", [P, A_GROUPS, P])
    norm_stage([(P0[:, t, 512:1024].rearrange("p (g d) -> p g d", d=P),
                 P0[:, t, 512:1024].rearrange("p (g d) -> p g d", d=P),
                 vgain[:, :].rearrange("p (g d) -> p g d", d=P), P) for t in range(NT)],
               loads=[(vgain[:, :], bcast(I["l0_a_vnorm"])),
                      (ws[:, :, :], I["l0_a_ws"].rearrange("g t s -> t g s"))])
    transpose_all([(wst[:, g, :], ws[:, g, :]) for g in range(A_GROUPS)])
    if Stage.count < upto:
        wmask, z_done = sem("a_w_masked"), sem("a_z_done")

        def a_pool(f, pool):
            f(nc.gpsimd.affine_select(out=wst[:, :, :], in_=wst[:, :, :], compare_op=ALU.is_ge, fill=0.0, base=0,
                                      pattern=[[0, A_GROUPS], [1, P]], channel_multiplier=-1), wmask)

        def a_pe(f, pe):
            pe.wait_ge(wmask, 1)
            for t in range(NT):
                for g in range(A_GROUPS):
                    last = nc.tensor.matmul(banks[t][:, g * P:(g + 1) * P], wst[:, g, :],
                                            P0[:, t, 512 + g * P:512 + (g + 1) * P], start=True, stop=True)
                last.then_inc(z_done, 1)

        def a_dve(f, dve):
            for t in range(NT):
                dve.wait_ge(z_done, t + 1)
                for g in range(A_GROUPS):
                    c = slice(g * P, (g + 1) * P)
                    f(nc.vector.scalar_tensor_tensor(mix[:, t, c], banks[t][:, c], C("l0_a_bs", g),
                                                     P0[:, t, c], ALU.add, ALU.mult))
                f(nc.vector.tensor_tensor(mix[:, t, 0:512], mix[:, t, 0:512], P0[:, t, 1024:1536], ALU.mult))
        elementwise(a_dve, pool_body=a_pool, pe_body=a_pe)
    else:
        stage()
    zone.at = mark0

    sq = zone("squares", [P, D])
    bg = zone("b_gains", [P, 2, B_DK])
    mg = zone("m_qgain", [P, HD])
    rp = zone("rope4", [P, NT, 8])
    lamv = zone("lambda_vecs", [P, 4, B_DK])
    lam = zone("lambda", [P, 4])
    QT = zone("b_q_t", [P, 4, S])
    KT = zone("b_k_t", [P, 4, S])
    MQT = zone("m_q_t", [P, 2, S])
    if Stage.count < upto:
        lam_prod, lam_exp = sem("lambda_dots"), sem("lambda_exps")
        n = Stage.count
        mean_done, root_done = sem(f"gn{n}_mean"), sem(f"gn{n}_root")
        todo = []
        for t in range(NT):
            for a, b, g, d in ((1536, 2048, bg[:, 0, :], B_DK), (2048, 2560, bg[:, 1, :], B_DK), (3584, 3840, mg[:, :], HD)):
                v = P0[:, t, a:b].rearrange("p (g d) -> p g d", d=d)
                todo.append((v, v, g, d))

        def qk_dve(f, dve):
            for i in range(2):
                f(nc.vector.tensor_tensor(lamv[:, 2 * i, :], lamv[:, 2 * i, :], lamv[:, 2 * i + 1, :], ALU.mult))
                f(nc.vector.tensor_reduce(lam[:, i:i + 1], lamv[:, 2 * i, :], AX.X, ALU.add), lam_prod)
            group_norms(f, dve, ss, todo, mean_done, root_done, sq)
            for t in range(NT):
                for v in (todo[3 * t][0], todo[3 * t + 1][0]):
                    rope(f, v, rp[:, t, 0:4], rp[:, t, 4:8], 4, sq)
            dve.wait_ge(lam_exp, 1)
            f(nc.vector.tensor_tensor(lam[:, 2:3], lam[:, 1:2], lam[:, 0:1], ALU.subtract))
            f(nc.vector.tensor_scalar(lam[:, 2:3], lam[:, 2:3], -LAM_INIT, None, ALU.add))

        def qk_act(f, act):
            act.wait_ge(lam_prod, 2)
            f(nc.scalar.activation(lam[:, 0:2], lam[:, 0:2], ACT.Exp), lam_exp)
            group_roots(f, act, ss, todo, mean_done, root_done)

        elementwise(qk_dve, qk_act,
                    loads=[(bg[:, 0, :], bcast(I["l0_b_qnorm"])), (bg[:, 1, :], bcast(I["l0_b_knorm"])),
                           (mg[:, :], bcast(I["l0_m_qnorm"])),
                           (rp[:, :, :], I["rope4"].rearrange("(t p) c -> p t c", p=P))] +
                          [(lamv[:, i, :], bcast(I[f"l0_b_{x}"])) for i, x in enumerate(("lq1", "lk1", "lq2", "lk2"))])
    else:
        stage()
    transpose_all([(T[:, b, t * P:(t + 1) * P], P0[:, t, c0 + b * P:c0 + (b + 1) * P])
                   for T, c0, nb in ((QT, 1536, 4), (KT, 2048, 4), (MQT, 3584, 2)) for b in range(nb) for t in range(NT)])
    units = []
    for h in range(B_HEADS):
        for m in range(2):
            for t in range(NT):
                g = 2 * h + m
                r = slice(32 * (g % 4), 32 * (g % 4) + 32)
                nk = (t + 1) * P
                units.append(dict(qT=QT[r, g // 4, t * P:(t + 1) * P], kT=KT[r, g // 4, 0:nk], nk=nk,
                                  v=[P0[:, k, 2560 + h * B_DV:2560 + (h + 1) * B_DV] for k in range(t + 1)],
                                  scale=B_DK ** -0.5, mask=causal[:, S - nk:S], coef=lam[:, 2:3] if m else None,
                                  out=mix[:, t, 512 + h * B_DV:512 + (h + 1) * B_DV], add=bool(m), guard=False))
    attention(units + memory_units(0, MQT, mix[:, :, 1024:1280]))
    subln = zone("b_subln", [P, B_DV])
    sn = [mix[:, t, 512:1024].rearrange("p (h d) -> p h d", d=B_DV) for t in range(NT)]

    def after_b(f, dve):
        for t in range(NT):
            f(nc.vector.scalar_tensor_tensor(mix[:, t, 512:1024], mix[:, t, 512:1024], 1.0 - LAM_INIT,
                                             P0[:, t, 3072:3584], ALU.mult, ALU.mult), wait=False)
            f(nc.vector.tensor_tensor(mix[:, t, 1024:1280], mix[:, t, 1024:1280], P0[:, t, 3840:4096], ALU.mult))

    norm_stage([(v, v, subln[:, :], B_DV) for v in sn], loads=[(subln[:, :], bcast(I["l0_b_subln"]))], after=after_b)
    mixt = P0[:, :, :].rearrange("p a b -> p (a b)")[:, 0:KMIX * S].rearrange("p (k s) -> p k s", k=KMIX)
    transpose_all([(mixt[:, k, t * P:(t + 1) * P], mix[:, t, k * P:(k + 1) * P]) for k in range(KMIX) for t in range(NT)])
    out_project("even_out", KMIX, mixt)


    norm_transpose(X, HT, [(HT, C("l1_norm", 0, 8), None)])
    zone.at = keep_first
    ss = zone("sums", [P, 3, 80])
    P1 = zone("odd_in", [P, NT, ODD_IN])
    mix = zone("mix", [P, NT, MIX])
    project("odd_in", ht, ranges_evac(P1, ODD_RANGES, ODD_IN), ranges_owner(ODD_RANGES, ODD_IN), width=ODD_IN)
    mark1 = zone.at

    PAD = C_KERNEL - 1
    CT = zone("conv_in_t", [P, C_BLOCKS, PAD + S])
    CY = zone("conv_out_t", [P, C_BLOCKS, S])
    CN = zone("conv_out", [P, NT, 512])
    sq = zone("squares", [P, D])
    cgain = zone("c_norm", [P, 512])

    def glu_dve(f, dve):
        f(nc.vector.memset(CT[:, :, 0:PAD], 0.0), wait=False)
        for t in range(NT):
            f(nc.vector.tensor_tensor(P1[:, t, 0:512], P1[:, t, 0:512], P1[:, t, 512:1024], ALU.mult), wait=False)

    elementwise(glu_dve)
    transpose_all([(CT[:, b, PAD + t * P:PAD + (t + 1) * P], P1[:, t, b * P:(b + 1) * P])
                   for b in range(C_BLOCKS) for t in range(NT)])

    def conv_dve(f, dve):
        for k in range(C_KERNEL):
            for b in range(C_BLOCKS):
                w = C("l1_c_conv_w", C_BLOCKS * k + b)
                if k == 0:
                    ins = nc.vector.tensor_scalar(CY[:, b, :], CT[:, b, 0:S], w, C("l1_c_conv_b", b), ALU.mult, ALU.add)
                else:
                    ins = nc.vector.scalar_tensor_tensor(CY[:, b, :], CT[:, b, k:k + S], w, CY[:, b, :],
                                                         ALU.mult, ALU.add)
                f(ins, wait=(b == C_BLOCKS - 1))

    elementwise(conv_dve)
    transpose_all([(CN[:, t, b * P:(b + 1) * P], CY[:, b, t * P:(t + 1) * P])
                   for b in range(C_BLOCKS) for t in range(NT)])
    norm_stage([(CN[:, t, :].unsqueeze(1), CN[:, t, :].unsqueeze(1), cgain[:, :], 512) for t in range(NT)],
               loads=[(cgain[:, :], bcast(I["l1_c_norm"]))])
    if Stage.count < upto:
        c_silu = sem("c_silu")

        def c_act(f, act):
            f(nc.scalar.activation(CN[:, :, :], CN[:, :, :], ACT.Silu), c_silu)

        def c_dve(f, dve):
            dve.wait_ge(c_silu, 1)
            f(nc.vector.tensor_tensor(mix[:, :, 0:512], CN[:, :, :], P1[:, :, 1024:1536], ALU.mult))
        elementwise(c_dve, c_act)
    else:
        stage()
    zone.at = mark1

    sq = zone("squares", [P, D])
    dg = zone("d_gains", [P, 2, HD])
    mg = zone("m_qgain", [P, HD])
    rp = zone("rope8", [P, NT, 16])
    rc = zone("rope_cmp", [P, 16])
    KDUP = zone("k_twice", [P, NT, 2, D_GROUPS, 2, HD])
    DQT = zone("d_q_t", [P, 4, S])
    KDT = zone("d_k_t", [P, 2, D_GROUPS, S])
    RT = zone("cmp_raw_t", [P, 2, S])
    MQT = zone("m_q_t", [P, 2, S])
    posr = zone("cmp_pos", [CMP_BLOCK, 2, 2, HD])
    POST = zone("cmp_pos_t", [P, 2, CMP_BLOCK])
    OP = zone("cmp_operand", [P, 2, CMP_BLOCK, N_CMP])
    HID = zone("cmp_hidden", [P, 2, D_GROUPS, N_CMP])
    W2 = zone("cmp_w2", [P, 2, HD])
    KC = zone("k_cmp", [N_CMP, 2, D_GROUPS, HD])
    KCD = zone("k_cmp_twice", [N_CMP, D_GROUPS, 2, HD])
    KCT = zone("k_cmp_t", [P, D_GROUPS, N_CMP])

    heads = lambda t, a, b: P1[:, t, a:b].rearrange("p (g d) -> p g d", d=HD)
    K_SLC, K_WIN = 2304, 2560
    todo = []
    for t in range(NT):
        for a, b, g in ((1536, 2048, dg[:, 0, :]), (K_SLC, K_SLC + P, dg[:, 1, :]), (K_WIN, K_WIN + P, dg[:, 1, :]),
                        (3352, 3608, mg[:, :])):
            todo.append((heads(t, a, b), heads(t, a, b), g, HD))

    def rotate(f, dve):
        for t in range(NT):
            for a, b in ((1536, 2048), (K_SLC, K_SLC + P), (K_WIN, K_WIN + P)):
                rope(f, heads(t, a, b), rp[:, t, 0:8], rp[:, t, 8:16], 8, sq)
            for i, a in enumerate((K_SLC, K_WIN)):
                f(nc.vector.tensor_copy(KDUP[:, t, i, :, :, :],
                                        heads(t, a, a + P).unsqueeze(2).broadcast_to([P, D_GROUPS, 2, HD])), wait=False)

    norm_stage(todo, loads=[(dg[:, 0, :], bcast(I["l1_d_qnorm"])), (dg[:, 1, :], bcast(I["l1_d_knorm"])),
                            (mg[:, :], bcast(I["l1_m_qnorm"])),
                            (rp[:, :, :], I["rope8"].rearrange("(t p) c -> p t c", p=P)),
                            (rc[0:N_CMP, :], I["ropec"])] +
               [(posr[:, i, j, :], I[f"l1_d_cmp_pos_{x}"]) for i, x in enumerate("kv") for j in range(2)] +
               [(W2[:, i, :], I[f"l1_d_cmp_w2_{x}"]) for i, x in enumerate("kv")], after=rotate)
    transpose_all([(DQT[:, b, t * P:(t + 1) * P], P1[:, t, 1536 + b * P:1536 + (b + 1) * P])
                   for b in range(4) for t in range(NT)] +
                  [(KDT[:, i, g, t * P:(t + 1) * P], KDUP[:, t, i, g, :, :].rearrange("p a d -> p (a d)"))
                   for i in range(2) for g in range(D_GROUPS) for t in range(NT)] +
                  [(RT[:, i, t * P:(t + 1) * P], P1[:, t, 2048 + i * P:2048 + (i + 1) * P])
                   for i in range(2) for t in range(NT)] +
                  [(MQT[:, b, t * P:(t + 1) * P], P1[:, t, 3352 + b * P:3352 + (b + 1) * P])
                   for b in range(2) for t in range(NT)] +
                  [(POST[:, i, :], posr[:, i, :, :].rearrange("p a d -> p (a d)")) for i in range(2)])

    if Stage.count < upto:
        operand_ready, hid_ready, cmp_done = sem("cmp_operand_ready"), sem("cmp_hidden_ready"), sem("cmp_done")
        g0 = first_group[pn["cmp"][0]]
        owners.extend("aa")

        def cmp_dve(f, dve):
            for i in range(2):
                for n in range(N_CMP):
                    f(nc.vector.tensor_tensor(OP[:, i, :, n], RT[:, i, n * CMP_STRIDE:n * CMP_STRIDE + CMP_BLOCK],
                                              POST[:, i, :], ALU.add), operand_ready, wait=False)
            dve.wait_ge(cmp_done, 1)
            f(nc.vector.tensor_copy(KC[:, :, :, :].rearrange("p a g d -> p (a g d)"),
                                    acc_bank(g0)[0:N_CMP, 0:2 * D_GROUPS * HD]))

        def cmp_pe(f, pe):
            for i, p in enumerate(pn["cmp"]):
                w = slots[p % 3][:, 0:CMP_BLOCK * P].rearrange("p (t h) -> p t h", h=P)
                wait_panel(pe, p)
                pe.wait_ge(operand_ready, (i + 1) * N_CMP)
                for g in range(D_GROUPS):
                    r = slice(HD * g, HD * g + HD)
                    for t in range(CMP_BLOCK):
                        last = nc.tensor.matmul(banks[4 + 2 * i + g][:, 0:N_CMP], w[r, t, :], OP[r, i, t, :],
                                                start=(t == 0), stop=(t == CMP_BLOCK - 1))
                last.then_inc(acc_ready, 1)
            pe.wait_ge(acc_free["a"], owners[:g0 + 2].count("a"))
            for i in range(2):
                for g in range(D_GROUPS):
                    c = (i * D_GROUPS + g) * HD
                    last = nc.tensor.matmul(acc_bank(g0)[0:N_CMP, c:c + HD], HID[:, i, g, :], W2[:, i, :],
                                            start=True, stop=True)
            last.then_inc(cmp_done, 1)

        def cmp_act(f, act):
            for i in range(2):
                act.wait_ge(acc_ready, g0 + i + 1)
                for g in range(D_GROUPS):
                    f(nc.scalar.activation(HID[:, i, g, :], banks[4 + 2 * i + g][:, 0:N_CMP], ACT.Silu),
                      acc_free["a"] if g else hid_ready, wait=False)

        elementwise(cmp_dve, cmp_act, pe_body=cmp_pe, prefetch_to=pn["cmp"][-1] + 3)
    else:
        stage()
    kcv = KC[:, 0, :, :]

    def rotate_cmp(f, dve):
        rope(f, kcv, rc[0:N_CMP, 0:8], rc[0:N_CMP, 8:16], 8, sq)
        f(nc.vector.tensor_copy(KCD[:, :, :, :], kcv.unsqueeze(2).broadcast_to([N_CMP, D_GROUPS, 2, HD])))

    norm_stage([(kcv, kcv, dg[:, 1, :], HD)], after=rotate_cmp)
    transpose_all([(KCT[:, g, :], KCD[:, g, :, :].rearrange("p a d -> p (a d)")) for g in range(D_GROUPS)])
    units = []
    for h in range(D_HEADS):
        g = h // (D_HEADS // D_GROUPS)
        r = slice(64 * (h % 2), 64 * (h % 2) + 64)
        for t in range(NT):
            nk = (t + 1) * P
            same = dict(qT=DQT[r, h // 2, t * P:(t + 1) * P], scale=HD ** -0.5,
                        out=mix[:, t, 512 + h * HD:512 + (h + 1) * HD])
            gate = lambda j: P1[:, t, 2816 + 3 * h + j:2816 + 3 * h + j + 1]
            units.append(dict(same, kT=KCT[r, g, :], nk=N_CMP, v=[KC[:, 1, g, :]], mask=cmpmask[:, t, :],
                              coef=gate(0), add=False, guard=True))
            for j, (i, v0) in enumerate(((0, 2432), (1, 2688))):
                units.append(dict(same, kT=KDT[r, i, g, 0:nk], nk=nk,
                                  v=[P1[:, k, v0 + g * HD:v0 + (g + 1) * HD] for k in range(t + 1)],
                                  mask=causal[:, S - nk:S], coef=gate(1 + j), add=True, guard=False))
    attention(units + memory_units(1, MQT, mix[:, :, 1024:1280]))

    def gate_d(f, dve):
        for t in range(NT):
            f(nc.vector.tensor_tensor(mix[:, t, 512:1024], mix[:, t, 512:1024], P1[:, t, 2840:3352], ALU.mult), wait=False)
            f(nc.vector.tensor_tensor(mix[:, t, 1024:1280], mix[:, t, 1024:1280], P1[:, t, 3608:3864], ALU.mult), wait=False)

    elementwise(gate_d)
    mixt = P1[:, :, :].rearrange("p a b -> p (a b)")[:, 0:KMIX * S].rearrange("p (k s) -> p k s", k=KMIX)
    transpose_all([(mixt[:, k, t * P:(t + 1) * P], mix[:, t, k * P:(k + 1) * P]) for k in range(KMIX) for t in range(NT)])
    out_project("odd_out", KMIX, mixt)

    zone.at = WORK
    elementwise(act_body=lambda f, act: f(nc.scalar.activation(CS[:, :], C("c_2", 0, 8), ACT.Silu)))
    project_col("ada0", CS, MOD[:, 0:48], C("ada_b_2", 0, 48))

    def mods(base):
        return [MOD[:, base + 8 * i:base + 8 * i + 8] for i in range(6)]

    def gain_stage(jobs):
        def body(f, dve):
            for i, scale, gain in jobs:
                f(nc.vector.scalar_tensor_tensor(GM[:, i, :], scale, 1.0, gain, ALU.add, ALU.mult), wait=False)
        elementwise(body)

    def gate_row(cols):
        if not stage():
            return
        mark = zone.at
        diag = zone("gate_diag", [P, KD, P])
        ones = zone("ones", [P, P])
        n = Stage.count
        diag_ready, row_ready = sem(f"diag{n}_ready"), sem(f"row{n}_ready")
        with StageBlock() as block:
            @block.vector
            def _(dve):
                f = dve_f.on(dve)
                f(nc.vector.memset(ones[:, :], 1.0))
                f(nc.vector.tensor_tensor(diag[:, :, :], ident[:, :].unsqueeze(1).broadcast_to([P, KD, P]),
                                          cols.unsqueeze(2).broadcast_to([P, KD, P]), ALU.mult), diag_ready)
                for i in range(2):
                    dve.wait_ge(row_ready, i + 1)
                    f(nc.vector.tensor_copy(GROW[:, i * 512:(i + 1) * 512], banks[i][:, :]), wait=False)

            @block.tensor
            def _(pe):
                pe.wait_ge(diag_ready, 1)
                for i in range(2):
                    nc.tensor.matmul(banks[i][:, :], ones[:, :],
                                     diag[:, 4 * i:4 * i + 4, :].rearrange("p a b -> p (a b)"),
                                     start=True, stop=True).then_inc(row_ready, 1)
        zone.at = mark

    sh1, sc1, g1, sh2, sc2, g2 = mods(0)
    gain_stage([(0, sc1, C("norm_mix_g_2", 0, 8)), (1, sc2, C("norm_ffn_g_2", 0, 8))])
    norm_transpose(X, HT, [(HT, GM[:, 0, :], sh1)])

    LP = CONV_WIDTH - 1
    RC = zone("rec_in_t", [P, KD, LP + S])
    GT = zone("gate_t", [P, KD, S])
    XC = zone("conv_t", [P, KD, S])
    R = zone("r_t", [P, KD, S])
    IG = zone("i_t", [P, KD, S])
    A = zone("a_t", [P, KD, S])
    TH = zone("tanh_t", [P, KD, S])
    HS = zone("hs_t", [P, KD, S])
    SPL = zone("softplus", [P, 6, KD])

    def block_of(slot, K, b):
        return slot[:, 0:K * 512].rearrange("p (k n) -> p k n", k=K)[:, :, b * P:(b + 1) * P]

    def lru_evac(f, who, g, bank, free):
        if g < 4:
            f(nc.scalar.activation(GT[:, 2 * g:2 * g + 2, :].rearrange("p a b -> p (a b)"), bank[:, :], ACT.Gelu), free, wait=False)
        else:
            f(nc.vector.tensor_copy(RC[:, 2 * (g - 4):2 * (g - 4) + 2, LP:LP + S], bank[:, :].rearrange("p (a b) -> p a b", a=2)),
              free, wait=False)

    ht_all = lambda g, h, k: HT[:, k, :]
    panel_block = lambda slot, g, h, k: block_of(slot, KD, 2 * (g % 2) + h)[:, k, :]
    project_t("lru_in", panel_block, 8, KD, ht_all, lru_evac, lambda g: "a" if g < 4 else "v")

    if Stage.count < upto:
        exp_in, exp_out = sem("softplus_in"), sem("softplus_exp")

        def lru_conv(f, dve):
            f(nc.vector.memset(RC[:, :, 0:LP], 0.0))
            for k in range(CONV_WIDTH):
                for b in range(KD):
                    w = C("lru_conv_w_2", KD * k + b)
                    if k == 0:
                        ins = nc.vector.tensor_scalar(XC[:, b, :], RC[:, b, 0:S], w, C("lru_conv_b_2", b), ALU.mult, ALU.add)
                    else:
                        ins = nc.vector.scalar_tensor_tensor(XC[:, b, :], RC[:, b, k:k + S], w, XC[:, b, :],
                                                             ALU.mult, ALU.add)
                    f(ins, wait=(b == KD - 1))
            lamc = C("lru_lambda_2", 0, 8)
            v = [SPL[:, i, :] for i in range(6)]
            f(nc.vector.tensor_scalar(v[1], lamc, -1.0, None, ALU.mult))
            f(nc.vector.tensor_tensor(v[2], v[1], lamc, ALU.min), exp_in)
            dve.wait_ge(exp_out, 1)
            f(nc.vector.tensor_scalar(v[3], v[2], 2.0, None, ALU.add))
            f(nc.vector.reciprocal(v[3], v[3]))
            f(nc.vector.tensor_tensor(v[2], v[2], v[3], ALU.mult))
            f(nc.vector.tensor_tensor(v[3], v[2], v[2], ALU.mult))
            f(nc.vector.memset(v[4], 1.0 / 19))
            for n in range(17, 0, -2):
                f(nc.vector.tensor_tensor(v[4], v[4], v[3], ALU.mult))
                f(nc.vector.tensor_scalar(v[4], v[4], 1.0 / n, None, ALU.add))
            f(nc.vector.tensor_tensor(v[4], v[4], v[2], ALU.mult))
            f(nc.vector.tensor_scalar(v[1], v[1], 0.0, None, ALU.max))
            f(nc.vector.scalar_tensor_tensor(v[0], v[4], 2.0, v[1], ALU.mult, ALU.add))
            f(nc.vector.tensor_scalar(v[0], v[0], -8.0, None, ALU.mult))

        def lru_exp(f, act):
            act.wait_ge(exp_in, 1)
            f(nc.scalar.activation(SPL[:, 2, :], SPL[:, 2, :], ACT.Exp), exp_out)
        elementwise(lru_conv, lru_exp)
    else:
        stage()

    def gates_evac(f, who, g, bank, free):
        dst, name, h = (R, "lru_ba_2", g) if g < 4 else (IG, "lru_bx_2", g - 4)
        for j in range(2):
            f(nc.scalar.activation(dst[:, 2 * h + j, :], bank[:, j * S:(j + 1) * S], ACT.Sigmoid,
                                   bias=C(name, 2 * h + j)), free if j else None, wait=False)

    project_t("lru_gates",
              lambda slot, g, h, k: slot[:, 2048 * (g // 4):2048 * (g // 4) + 2048].rearrange("p (h n) -> p h n", h=8)
              [:, 2 * (g % 4) + k, h * P:(h + 1) * P], 8, 2,
              lambda g, h, k: XC[:, 2 * (g % 4) + k, :], gates_evac, lambda g: "a")
    if Stage.count < upto:
        la_ready, a_ready, th_ready, m_ready, root_ready = (sem(f"lru_{x}") for x in ("la", "a", "tanh", "mult", "root"))

        def scan_dve(f, dve):
            for b in range(KD):
                f(nc.vector.tensor_scalar(R[:, b, :], R[:, b, :], SPL[:, 0, b:b + 1], None, ALU.mult), wait=(b == KD - 1))
            f(nc.vector.memset(SPL[:, 1, :], 0.0), la_ready)
            f(nc.vector.tensor_tensor(IG[:, :, :], IG[:, :, :], XC[:, :, :], ALU.mult))
            dve.wait_ge(th_ready, 1)
            f(nc.vector.tensor_tensor(R[:, :, :], A[:, :, :], A[:, :, :], ALU.mult))
            f(nc.vector.scalar_tensor_tensor(TH[:, :, :], R[:, :, :], 1.0, TH[:, :, :], ALU.add, ALU.mult), m_ready)
            dve.wait_ge(root_ready, 1)
            f(nc.vector.tensor_tensor(TH[:, :, :], TH[:, :, :], IG[:, :, :], ALU.mult))
            for b in range(KD):
                f(nc.vector.tensor_tensor_scan(HS[:, b, :], A[:, b, :], TH[:, b, :], 0.0, ALU.mult, ALU.add),
                  wait=(b == KD - 1))
            f(nc.vector.tensor_tensor(HS[:, :, :], HS[:, :, :], GT[:, :, :], ALU.mult))

        def scan_act(f, act):
            act.wait_ge(la_ready, 1)
            f(nc.scalar.activation(A[:, :, :], R[:, :, :], ACT.Exp), a_ready)
            f(nc.scalar.activation(TH[:, :, :], R[:, :, :], ACT.Tanh), th_ready)
            act.wait_ge(m_ready, 1)
            f(nc.scalar.activation(TH[:, :, :], TH[:, :, :], ACT.Sqrt, scale=-1.0), root_ready)
        elementwise(scan_dve, scan_act)
    else:
        stage()
    gate_row(g1)
    out_project("lru_out", KD, HS, gate=(GROW, TMP))

    def peer(l, q_name, gain, shift, gate_cols):
        norm_transpose(X, HT, [(HT, gain, shift)])
        zone.at = WORK
        QT = zone("peer_q_t", [P, 2 * PEER_HEADS, S])
        SK = zone("sub_keys", [P, 2 * PEER_HEADS, P])
        SKT = zone("sub_keys_t", [P, 2 * PEER_HEADS, P])
        SC = zone("key_scores", [P, NT, 2 * PEER_HEADS, N_KEYS])
        VAL = zone("key_values", [P, NT, 2 * PEER_HEADS, TOPK])
        IDX = zone("key_index", [P, NT, 2 * PEER_HEADS, TOPK], U32)
        IDF = zone("key_index_f", [P, NT, 2 * PEER_HEADS, TOPK])

        def q_evac(f, who, g, bank, free):
            dst = QT[:, 2 * g:2 * g + 2, :].rearrange("p a b -> p (a b)")
            f(nc.scalar.activation(dst, bank[:, :], ACT.Copy) if who == "a" else nc.vector.tensor_copy(dst, bank[:, :]),
              free, wait=False)

        project_t(q_name, panel_block, 8, KD, ht_all, q_evac, lambda g: "av"[g % 2], ahead=0)
        transpose_all([(SKT[:, j, :], SK[:, j, :]) for j in range(2 * PEER_HEADS)],
                      loads=[(SK[:, :, :], I["peer_sub_keys_2"][l].rearrange("h p n d -> n (h p) d"))])
        if stage():
            n = Stage.count
            scored, = (sem(f"peer{l}_scored"),)
            with StageBlock() as block:
                @block.tensor
                def _(pe):
                    for t in range(NT):
                        for q in range(4):
                            for j in range(4):
                                last = nc.tensor.matmul(banks[4 * t + q][:, j * P:(j + 1) * P],
                                                        QT[:, 4 * q + j, t * P:(t + 1) * P], SKT[:, 4 * q + j, :],
                                                        start=True, stop=True)
                            last.then_inc(scored, 1)

                @block.scalar
                def _(act):
                    f = act_f.on(act)
                    for i in range(8):
                        act.wait_ge(scored, i + 1)
                        f(nc.scalar.activation(SC[:, i // 4, 4 * (i % 4):4 * (i % 4) + 4, :].rearrange("p a b -> p (a b)"),
                                               banks[i][:, :], ACT.Copy), wait=False)

        def top16(f, scores, vals, idx):
            f(nc.vector.max(vals[:, 0:8], scores))
            f(nc.vector.max_index(idx[:, 0:8], vals[:, 0:8], scores))
            f(nc.vector.match_replace(scores, vals[:, 0:8], scores, -3e38))
            f(nc.vector.max(vals[:, 8:16], scores))
            f(nc.vector.max_index(idx[:, 8:16], vals[:, 8:16], scores), wait=False)

        def keys_top(f, dve):
            for t in range(NT):
                for j in range(2 * PEER_HEADS):
                    top16(f, SC[:, t, j, :], VAL[:, t, j, :], IDX[:, t, j, :])
            dve.wait_ge(dve_order, counts[dve_order.num])
            f(nc.vector.tensor_copy(IDF[:, :, :, :].rearrange("p t j k -> p (t j k)"),
                                    IDX[:, :, :, :].rearrange("p t j k -> p (t j k)")))
        elementwise(keys_top)

        zone.at = WORK
        CAND = zone("candidates", [P, NT, PEER_HEADS, TOPK * TOPK])
        EQ = zone("pick", [P, SLOTS, TOPK])
        CV = nc.alloc_sbuf_tensor_at(f"cand_values{l}", [P, NT, PEER_HEADS, TOPK], F32, offset=zone.at)
        zone.at += NT * SLOTS * 4
        CI = zone("cand_index", [P, NT, PEER_HEADS, TOPK], U32)
        C12 = zone("cand_pair", [P, 2, NT, SLOTS], U32)
        C12F = zone("cand_pair_f", [P, 2, NT, SLOTS])
        EN = zone("expert_keys", [P, 3, NT, SLOTS])
        SUM = zone("gate_sums", [P, NT * PEER_HEADS])
        VAL_AT = WORK + 16384 + 8192 + 8192 + 16384
        assert zone.at <= VAL_AT, (zone.at, VAL_AT)
        if Stage.count < upto:
            exp_in, exp_out = sem(f"peer{l}_shifted"), sem(f"peer{l}_exped")

            def pick_dve(f, dve):
                for t in range(NT):
                    for h in range(PEER_HEADS):
                        a = VAL[:, t, 2 * h, :].unsqueeze(2).broadcast_to([P, TOPK, TOPK])
                        b = VAL[:, t, 2 * h + 1, :].unsqueeze(1).broadcast_to([P, TOPK, TOPK])
                        f(nc.vector.tensor_tensor(CAND[:, t, h, :].rearrange("p (a b) -> p a b", a=TOPK), a, b, ALU.add))
                        top16(f, CAND[:, t, h, :], CV[:, t, h, :], CI[:, t, h, :])
                dve.wait_ge(dve_order, counts[dve_order.num])
                cv = CV[:, :, :, :].rearrange("p t h k -> p (t h) k")
                gw = EN[:, 2, :, :].rearrange("p t (h k) -> p (t h) k", h=PEER_HEADS)
                th = NT * PEER_HEADS
                f(nc.vector.tensor_tensor(gw, cv, cv[:, :, 0:1].broadcast_to([P, th, TOPK]), ALU.subtract), exp_in)
                ci = CI[:, :, :, :].rearrange("p t h k -> p (t h k)")
                c12 = [C12[:, i, :, :].rearrange("p t s -> p (t s)") for i in range(2)]
                f(nc.vector.tensor_scalar(c12[0], ci, 4, None, ALU.logical_shift_right))
                f(nc.vector.tensor_scalar(c12[1], ci, 15, None, ALU.bitwise_and))
                f(nc.vector.tensor_copy(C12F[:, :, :, :].rearrange("p i t s -> p (i t s)"),
                                        C12[:, :, :, :].rearrange("p i t s -> p (i t s)")))
                for i in range(2):
                    for t in range(NT):
                        eq3 = EQ[:, :, :]
                        f(nc.vector.tensor_tensor(eq3, C12F[:, i, t, :].unsqueeze(2).broadcast_to([P, SLOTS, TOPK]),
                                                  iota[:, 0:TOPK].unsqueeze(1).broadcast_to([P, SLOTS, TOPK]), ALU.is_equal))
                        for h in range(PEER_HEADS):
                            e = EQ[:, h * TOPK:(h + 1) * TOPK, :]
                            f(nc.vector.tensor_tensor(e, e, IDF[:, t, 2 * h + i, :].unsqueeze(1).broadcast_to([P, TOPK, TOPK]),
                                                      ALU.mult), wait=(h == PEER_HEADS - 1))
                        f(nc.vector.tensor_reduce(EN[:, i, t, :], eq3, AX.X, ALU.add))
                dve.wait_ge(exp_out, 1)
                f(nc.vector.tensor_reduce(SUM[:, :], gw, AX.X, ALU.add))
                f(nc.vector.reciprocal(SUM[:, :], SUM[:, :]))
                f(nc.vector.tensor_tensor(gw, gw, SUM[:, :].unsqueeze(2).broadcast_to([P, th, TOPK]), ALU.mult))

            def pick_act(f, act):
                act.wait_ge(exp_in, 1)
                g = EN[:, 2, :, :].rearrange("p t s -> p (t s)")
                f(nc.scalar.activation(g, g, ACT.Exp), exp_out)
            elementwise(pick_dve, pick_act)
        else:
            stage()
        transpose_all([(dst[:, t * P:(t + 1) * P], EN[:, i, t, :])
                       for i, dst in enumerate((slot_e1, slot_e2, slot_g)) for t in range(NT)])

        G = nc.alloc_sbuf_tensor_at(f"gates{l}", [P, N_KEYS, S], F32, offset=WORK)
        O1 = nc.alloc_sbuf_tensor_at(f"onehot1_{l}", [P, 2, 4, P], F32, offset=PANELS)
        O2 = nc.alloc_sbuf_tensor_at(f"onehot2_{l}", [P, 2, 4, P], F32, offset=PANELS + 4096)
        if stage():
            hot, built, stored = sem(f"peer{l}_onehots"), sem(f"peer{l}_built"), sem(f"peer{l}_stored")
            high = sem(f"peer{l}_h_high")

            def at_least(eng, s, value):
                if type(value) is not int or value > 0:
                    eng.wait_ge(s, value)

            with StageBlock() as block:
                @block.vector
                def _(dve):
                    dve.wait_ge(high, 1)
                    nc.vector.tensor_tensor(HTL[:, :, :], HT[:, :, :], HTH[:, :, :].bitcast(F32), ALU.subtract)\
                        .then_inc(dve_order, 1)
                    counts[dve_order.num] += 1

                    def step(n, s):
                        at_least(dve, built, n - 1)
                        for u in range(4):
                            tok = slice(4 * n + u, 4 * n + u + 1) if type(n) is int else bass.ds(4 * n + u, 1)
                            nc.vector.tensor_scalar(O2[:, s, u, :], iota[:, :], slot_e2[:, tok], None, ALU.is_equal)
                            last = nc.vector.tensor_scalar(O1[:, s, u, :], iota[:, :], slot_e1[:, tok], slot_g[:, tok],
                                                           ALU.is_equal, ALU.mult)
                        last.then_inc(hot, 1)
                    for s in range(2):
                        step(s, s)
                    with dve.Fori(1, S // 8) as i:
                        for s in range(2):
                            step(2 * i + s, s)

                @block.tensor
                def _(pe):
                    def step(n, s):
                        pe.wait_ge(hot, n + 1)
                        at_least(pe, stored, n - 1)
                        for u in range(4):
                            last = nc.tensor.matmul(banks[s][:, u * P:(u + 1) * P], O2[:, s, u, :], O1[:, s, u, :],
                                                    start=True, stop=True)
                        last.then_inc(built, 1)
                    for s in range(2):
                        step(s, s)
                    with pe.Fori(1, S // 8) as i:
                        for s in range(2):
                            step(2 * i + s, s)

                @block.scalar
                def _(act):
                    nc.scalar.activation(HTH[:, :, :], HT[:, :, :], ACT.Copy).then_inc(high, 1)

                    def step(n, s):
                        act.wait_ge(built, n + 1)
                        tok = slice(4 * n, 4 * n + 4) if type(n) is int else bass.ds(4 * n, 4)
                        nc.scalar.activation(G[:, :, tok], banks[s][:, :].rearrange("p (t e) -> p e t", t=4), ACT.Copy)\
                            .then_inc(stored, 1)
                    for s in range(2):
                        step(s, s)
                    with act.Fori(1, S // 8) as i:
                        for s in range(2):
                            step(2 * i + s, s)

        NB = N_KEYS
        o = RINGS

        def ring(name, shape, dt=F32):
            nonlocal o
            t = nc.alloc_sbuf_tensor_at(f"{name}{l}", [P] + shape, dt, offset=o)
            o += int(np.prod(shape)) * 4
            assert o <= WORK
            return t

        UTH, UTL = ring("u_t_high", [2, KD, P], F32R), ring("u_t_low", [2, KD, P], F32R)
        VH, VL = ring("v_high", [2, D], F32R), ring("v_low", [2, D], F32R)
        UR, VR = ring("u_ring", [2, D]), ring("v_ring", [2, D])
        AA = ring("activated", [2, S])
        WH, WL = ring("weighted_high", [S], F32R), ring("weighted_low", [S], F32R)
        if stage():
            u_loaded = [sem(f"peer{l}_u_loaded{i}") for i in range(2)]
            v_loaded = [sem(f"peer{l}_v_loaded{i}") for i in range(2)]
            turned, ut_high, ut_low, v_high, v_low, acted, gelued, w_full, w_high, weighted, applied, cleared_acc, zeroed = (
                sem(f"peer{l}_{x}") for x in ("turned", "ut_high", "ut_low", "v_high", "v_low", "acted", "gelued", "w_full",
                                              "w_high", "weighted", "applied", "cleared", "zeroed"))
            u_dram, v_dram = I["peer_u_2"][l], I["peer_v_2"][l]

            def rows(b):
                return slice(b * P, (b + 1) * P) if type(b) is int else bass.ds(b * P, P)

            with StageBlock() as block:
                @block.sync
                def _(sp):
                    def step(b, k):
                        at_least(sp, turned, 2 * b - 2)
                        sp.dma_start(UR[:, k, :], u_dram[rows(b), :]).then_inc(u_loaded[k], 16)
                        at_least(sp, v_low, b - 1)
                        sp.dma_start(VR[:, k, :], v_dram[rows(b), :]).then_inc(v_loaded[k], 16)
                    for k in range(2):
                        step(k, k)
                    with sp.Fori(1, NB // 2) as i:
                        for k in range(2):
                            step(2 * i + k, k)

                @block.tensor
                def _(pe):
                    def turn(b, k, lap):
                        pe.wait_ge(u_loaded[k], 16 * lap + 16)
                        for half in range(2):
                            at_least(pe, ut_low, 2 * b - 1 + half)
                            for j in range(4):
                                c = 4 * half + j
                                last = nc.tensor.transpose(banks[half][:, j * P:(j + 1) * P],
                                                           UR[:, k, c * P:(c + 1) * P], ident[:, :])
                            last.then_inc(turned, 1)

                    def act_on(b, k):
                        at_least(pe, gelued, b - 1)
                        pe.wait_ge(ut_low, 2 * b + 2)
                        for n, (u, h) in enumerate(((UTH, HTH), (UTH, HTL), (UTL, HTH))):
                            for j in range(KD):
                                last = nc.tensor.matmul(banks[2 + k][:, 0:S], u[:, k, j, :], h[:, j, :],
                                                        start=(n + j == 0), stop=(n == 2 and j == KD - 1))
                        last.then_inc(acted, 1)

                    def apply(b, k, final):
                        pe.wait_ge(v_low, b + 1)
                        pe.wait_ge(weighted, b + 1)
                        for t in range(NT):
                            for n, (w, v) in enumerate(((WH, VH), (WH, VL), (WL, VH))):
                                for half in range(2):
                                    last = nc.tensor.matmul(banks[4 + 2 * t + half][:, :], w[:, t * P:(t + 1) * P],
                                                            v[:, k, half * 512:(half + 1) * 512], start=False,
                                                            stop=final and n == 2, skip_group_check=True)
                        last.then_inc(applied, 1)

                    pe.wait_ge(zeroed, 1)
                    for i in range(4):
                        nc.tensor.matmul(banks[4 + i][:, :], WH[:, 0:P], HTH[:, 0:2, :].rearrange("p a b -> p (a b)"),
                                         start=True, stop=False, skip_group_check=True).then_inc(cleared_acc, 1)
                    turn(0, 0, 0)
                    turn(1, 1, 0)
                    act_on(0, 0)

                    def step(b, k, lap, turns=True, acts=True, final=False):
                        if turns:
                            turn(b + 2, k, lap + 1)
                        if acts:
                            act_on(b + 1, 1 - k)
                        apply(b, k, final)
                    for k in range(2):
                        step(k, k, 0)
                    with pe.Fori(1, NB // 2 - 1) as i:
                        for k in range(2):
                            step(2 * i + k, k, i)
                    for k in range(2):
                        step(NB - 2 + k, k, 0, turns=False, acts=k < 1, final=k == 1)

                def pipeline(eng, split_u, split_v, other, lap_of=lambda i: i):
                    split_u(0, 0)
                    split_u(1, 1)
                    split_v(0, 0, 0)
                    other(0, 0)

                    def step(b, k, lap, turns=True, others=True):
                        if turns:
                            split_u(b + 2, k)
                        if others:
                            split_v(b + 1, 1 - k, lap + k)
                            other(b + 1, 1 - k)
                    for k in range(2):
                        step(k, k, 0)
                    with eng.Fori(1, NB // 2 - 1) as i:
                        for k in range(2):
                            step(2 * i + k, k, i)
                    for k in range(2):
                        step(NB - 2 + k, k, NB // 2 - 1, turns=False, others=k < 1)

                @block.scalar
                def _(act):
                    def split_u(b, s):
                        for half in range(2):
                            act.wait_ge(turned, 2 * b + 1 + half)
                            at_least(act, acted, b - 1)
                            nc.scalar.activation(UTH[:, s, 4 * half:4 * half + 4, :].rearrange("p a b -> p (a b)"),
                                                 banks[half][:, :], ACT.Copy).then_inc(ut_high, 1)

                    def split_v(b, s, lap):
                        act.wait_ge(v_loaded[s], 16 * lap + 16)
                        at_least(act, applied, b - 1)
                        nc.scalar.activation(VH[:, s, :], VR[:, s, :], ACT.Copy).then_inc(v_high, 1)

                    def gelu(b, s):
                        act.wait_ge(acted, b + 1)
                        at_least(act, weighted, b - 1)
                        nc.scalar.activation(AA[:, s, :], banks[2 + s][:, 0:S], ACT.Gelu).then_inc(gelued, 1)
                    pipeline(act, split_u, split_v, gelu)

                @block.vector
                def _(dve):
                    f = dve_f.on(dve)
                    f(nc.vector.memset(WH[:, 0:P].bitcast(F32), 0.0), zeroed)
                    dve.wait_ge(cleared_acc, 4)

                    def split_u(b, s):
                        for half in range(2):
                            dve.wait_ge(ut_high, 2 * b + 1 + half)
                            at_least(dve, acted, b - 1)
                            c = slice(4 * half, 4 * half + 4)
                            nc.vector.tensor_tensor(UTL[:, s, c, :].rearrange("p a b -> p (a b)"), banks[half][:, :],
                                                    UTH[:, s, c, :].rearrange("p a b -> p (a b)").bitcast(F32),
                                                    ALU.subtract).then_inc(ut_low, 1)

                    def split_v(b, s, lap):
                        dve.wait_ge(v_high, b + 1)
                        at_least(dve, applied, b - 1)
                        nc.vector.tensor_tensor(VL[:, s, :], VR[:, s, :], VH[:, s, :].bitcast(F32), ALU.subtract)\
                            .then_inc(v_low, 1)

                    def weigh(b, s):
                        dve.wait_ge(gelued, b + 1)
                        g = G[:, b, :] if type(b) is int else G[:, bass.ds(b, 1), :].rearrange("p a s -> p (a s)")
                        nc.vector.tensor_tensor(AA[:, s, :], AA[:, s, :], g, ALU.mult).then_inc(w_full, 1)
                        dve.wait_ge(w_full, b + 1)
                        at_least(dve, applied, b)
                        nc.vector.tensor_copy(WH[:, :], AA[:, s, :]).then_inc(w_high, 1)
                        dve.wait_ge(w_high, b + 1)
                        nc.vector.tensor_tensor(WL[:, :], AA[:, s, :], WH[:, :].bitcast(F32), ALU.subtract)\
                            .then_inc(weighted, 1)
                    pipeline(dve, split_u, split_v, weigh)
        zone.at = WORK
        gate_row(gate_cols)

        def add_experts(f, dve):
            for t in range(NT):
                for half in range(2):
                    c = slice(half * 512, (half + 1) * 512)
                    f(nc.vector.tensor_tensor(TMP[:, :], banks[4 + 2 * t + half][:, :], GROW[:, c], ALU.mult))
                    f(nc.vector.tensor_tensor(X[:, t, c], X[:, t, c], TMP[:, :], ALU.add))
        elementwise(add_experts)

    peer(0, "peer_q0", GM[:, 1, :], sh2, g2)

    project_col("kv_ada", CS, MOD[:, 96:112], C("kv_ada_b_2", 0, 16))
    project_col("ada1", CS, MOD[:, 48:96], C("ada_b_2", 48, 48))
    sh1, sc1, g1, sh2, sc2, g2 = mods(48)
    gain_stage([(2, sc1, C("norm_mix_g_2", 8, 8)), (3, sc2, C("norm_ffn_g_2", 8, 8)),
                (4, MOD[:, 104:112], C("kv_norm_g_2", 0, 8))])
    HKV = zone("h_kv_t", [P, KD, S])
    norm_transpose(X, HT, [(HT, GM[:, 2, :], sh1), (HKV, GM[:, 4, :], MOD[:, 96:104])])
    DKV = zone("latent_kv", [P, NT, 288])
    DQ = zone("latent_q", [P, NT, Q_LORA])
    LT = zone("latent_kv_t", [P, 2, S])
    QLT = zone("latent_q_t", [P, 3, S])
    KN = zone("k_rows", [P, NT, MLA_HEADS, QK])
    VN = zone("v_rows", [P, NT, D])
    QN = zone("q_rows", [P, NT, MLA_HEADS, QK])
    sq = zone("squares", [P, D])
    lg = zone("latent_gains", [P, KV_LORA + Q_LORA])
    ss = zone("sums", [P, 3, 16])
    posi = zone("positions", [P, NT], I32)
    posri = zone("positions_row", [P, S], I32)
    posf = zone("positions_f", [P, NT])
    posrf = zone("positions_row_f", [P, S])
    frq = zone("freqs", [P, 16])
    ang = zone("angles", [P, 6, NT, 16])
    pmask = zone("pos_mask", [P, NT, S])

    def row_evac(dst_of):
        def evac(f, who, i, t, bank, free):
            dst, n = dst_of(i, t)
            src = bank[:, 0:n] if len(dst.shape) == 2 else bank[:, 0:n].rearrange("p (a b) -> p a b", a=dst.shape[1])
            f(nc.scalar.activation(dst, src, ACT.Copy) if who == "a" else nc.vector.tensor_copy(dst, src), free, wait=False)
        return evac

    alternate = lambda i, t: "av"[t]
    project("dkv", lambda i, k, t: HKV[:, k, t * P:(t + 1) * P], row_evac(lambda i, t: (DKV[:, t, :], 288)), alternate,
            width=288)
    if Stage.count < upto:
        n = Stage.count
        mean_done, root_done = sem(f"gn{n}_mean"), sem(f"gn{n}_root")
        sin_in, sin_out = sem("angle_reduced"), sem("angle_sines")
        todo = [(DKV[:, t, 0:KV_LORA].unsqueeze(1), DKV[:, t, 0:KV_LORA].unsqueeze(1), lg[:, 0:KV_LORA], KV_LORA)
                for t in range(NT)]
        flat = lambda i: ang[:, i, :, :].rearrange("p t h -> p (t h)")
        MAGIC = 12582912.0
        C1, C2 = 6.28125, TWO_PI - 6.28125
        C2H = float(np.float32(C2))
        C3 = float(C2 - C2H)
        PI = 3.1415925

        def kv_dve(f, dve):
            group_norms(f, dve, ss, todo, mean_done, root_done, sq)
            f(nc.vector.tensor_copy(posf[:, :], posi[:, :]))
            f(nc.vector.tensor_copy(posrf[:, :], posri[:, :]))
            for t in range(NT):
                f(nc.vector.tensor_scalar(ang[:, 0, t, :], frq[:, :], posf[:, t:t + 1], None, ALU.mult))
                f(nc.vector.tensor_scalar(pmask[:, t, :], posrf[:, :], posf[:, t:t + 1], NEG, ALU.is_gt, ALU.mult))
            f(nc.vector.tensor_scalar(flat(1), flat(0), 1.0 / TWO_PI, None, ALU.mult))
            f(nc.vector.tensor_scalar(flat(1), flat(1), MAGIC, None, ALU.add))
            f(nc.vector.tensor_scalar(flat(1), flat(1), MAGIC, None, ALU.subtract))
            for c in (C1, C2H, C3):
                f(nc.vector.scalar_tensor_tensor(flat(0), flat(1), -c, flat(0), ALU.mult, ALU.add))
            f(nc.vector.tensor_scalar(flat(0), flat(0), PI, -PI, ALU.min, ALU.max))
            f(nc.vector.tensor_scalar(flat(1), flat(0), -1.0, None, ALU.mult))
            f(nc.vector.tensor_tensor(flat(1), flat(1), flat(0), ALU.max))
            f(nc.vector.tensor_scalar(flat(1), flat(1), -1.0, math.pi / 2, ALU.mult, ALU.add), sin_in)
            dve.wait_ge(sin_out, 1)
            for t in range(NT):
                rope(f, DKV[:, t, KV_LORA:288].unsqueeze(1), ang[:, 3, t, :], ang[:, 2, t, :], 16, sq)
                f(nc.vector.tensor_copy(KN[:, t, :, QK_NOPE:QK],
                                        DKV[:, t, KV_LORA:288].unsqueeze(1).broadcast_to([P, MLA_HEADS, QK_ROPE])))

        def kv_act(f, act):
            group_roots(f, act, ss, todo, mean_done, root_done)
            act.wait_ge(sin_in, 1)
            f(nc.scalar.activation(ang[:, 2:4, :, :].rearrange("p i t h -> p (i t h)"),
                                   ang[:, 0:2, :, :].rearrange("p i t h -> p (i t h)"), ACT.Sin), sin_out)

        elementwise(kv_dve, kv_act,
                    loads=[(lg[:, 0:KV_LORA], bcast(I["mla_kv_latent_g_2"])),
                           (lg[:, KV_LORA:], bcast(I["mla_q_latent_g_2"][0])),
                           (posri[:, :], bcast(I["positions_2"][0])), (frq[:, :], bcast(I["freqs"]))] +
                          [(posi[:, t:t + 1], I["positions_2"][0, t * P:(t + 1) * P].rearrange("(p o) -> p o", o=1))
                           for t in range(NT)])
    else:
        stage()
    transpose_all([(LT[:, k, t * P:(t + 1) * P], DKV[:, t, k * P:(k + 1) * P]) for k in range(2) for t in range(NT)])
    ukv_view = lambda c: (lambda slot: slot[:, 0:4 * D].rearrange("p (k n) -> p k n", k=4)
                          [:, 2 * (c // 2):2 * (c // 2) + 2, 512 * (c % 2):512 * (c % 2) + 512])
    project("ukv", lambda i, k, t: LT[:, k, t * P:(t + 1) * P],
            row_evac(lambda i, t: (KN[:, t, 8 * i:8 * i + 8, 0:QK_NOPE], 512) if i < 2 else
                     (VN[:, t, 512 * (i - 2):512 * (i - 2) + 512], 512)), alternate,
            chunks=[(0, ukv_view(c), 2) for c in range(4)])
    project("dq", ht, row_evac(lambda i, t: (DQ[:, t, :], Q_LORA)), alternate, width=Q_LORA)
    norm_stage([(DQ[:, t, :].unsqueeze(1), DQ[:, t, :].unsqueeze(1), lg[:, KV_LORA:], Q_LORA) for t in range(NT)])
    transpose_all([(QLT[:, k, t * P:(t + 1) * P], DQ[:, t, k * P:(k + 1) * P]) for k in range(3) for t in range(NT)])
    uq_view = lambda c: (lambda slot: slot[:, 0:3 * MLA_HEADS * QK].rearrange("p (k n) -> p k n", k=3)
                         [:, :, 512 * c:512 * c + 512])
    qn_flat = lambda t: QN[:, t, :, :].rearrange("p h d -> p (h d)")
    project("uq", lambda i, k, t: QLT[:, k, t * P:(t + 1) * P],
            row_evac(lambda i, t: (qn_flat(t)[:, 512 * i:512 * i + 512], 512)), alternate,
            chunks=[(0, uq_view(c), 3) for c in range(3)])

    def rope_q(f, dve):
        for t in range(NT):
            rope(f, QN[:, t, :, QK_NOPE:QK], ang[:, 3, t, :], ang[:, 2, t, :], 16, sq)
    elementwise(rope_q)
    QTM = zone("q_heads_t", [QK, MLA_HEADS, S])
    KTM = zone("k_heads_t", [QK, MLA_HEADS, S])
    transpose_all([(dst[:, h, t * P:(t + 1) * P], src[:, t, h, :])
                   for dst, src in ((QTM, QN), (KTM, KN)) for h in range(MLA_HEADS) for t in range(NT)])
    AO = QN[:, :, :, :].rearrange("p t h d -> p (t h d)")[:, 0:NT * D].rearrange("p (t n) -> p t n", t=NT)
    attention([dict(qT=QTM[:, h, t * P:(t + 1) * P], kT=KTM[:, h, :], nk=S,
                    v=[VN[:, k, h * V_HEAD:(h + 1) * V_HEAD] for k in range(NT)], scale=QK ** -0.5,
                    mask=pmask[:, t, :], coef=None, out=AO[:, t, h * V_HEAD:(h + 1) * V_HEAD], add=False, guard=False)
               for h in range(MLA_HEADS) for t in range(NT)])
    AOT = HKV
    transpose_all([(AOT[:, k, t * P:(t + 1) * P], AO[:, t, k * P:(k + 1) * P]) for k in range(KD) for t in range(NT)])
    gate_row(g1)
    out_project("mla_out", KD, AOT, gate=(GROW, TMP))
    peer(1, "peer_q1", GM[:, 3, :], sh2, g2)

    zone.at = WORK
    fg = zone("final_gain", [P, D])
    fo = zone("final_out", [P, NT, D])
    if Stage.count < upto:
        sq_done, mean_done, root_done = sem("final_squares"), sem("final_mean"), sem("final_root")

        def fin_act(f, act):
            for t in range(NT):
                f(nc.scalar.activation(fo[:, t, :], X[:, t, :], ACT.Square, accum_out=stats[:, t:t + 1]), sq_done)
            act.wait_ge(mean_done, 1)
            f(nc.scalar.activation(stats[:, 4:4 + NT], stats[:, 0:NT], ACT.Sqrt), root_done)

        def fin_dve(f, dve):
            dve.wait_ge(sq_done, NT)
            f(nc.vector.tensor_scalar(stats[:, 0:NT], stats[:, 0:NT], 1.0 / D, EPS, ALU.mult, ALU.add), mean_done)
            inverse_root(f, stats[:, 0:NT], stats[:, 4:4 + NT], stats[:, 8:8 + NT], mean_done, root_done, dve)
            for t in range(NT):
                f(nc.vector.scalar_tensor_tensor(fo[:, t, :], X[:, t, :], stats[:, 4 + t:5 + t], fg[:, :], ALU.mult, ALU.mult))
        elementwise(fin_dve, fin_act, loads=[(fg[:, :], bcast(I["final_g_2"]))])
    else:
        stage()
    out_done = sem("out_stored")
    with StageBlock() as block:
        @block.sync
        def _(sp):
            sp.dma_start(out[0].rearrange("(t p) d -> p t d", p=P), fo[:, :, :] if upto >= 99 else X[:, :, :]).then_inc(out_done, 16)
            sp.wait_ge(out_done, 16)
    ctx.close()


_HOST = ("rope4", "rope8", "ropec", "freqs")


def kernel(**inputs):
    import numpy as _np
    import concourse.bacc as _bacc
    from concourse.bass_utils import run_bass_kernel_spmd as _run

    nc = _bacc.Bacc("TRN2", target_bir_lowering=False, num_devices=1)
    arrays, args = {}, {}
    for name, value in [*inputs.items(), *rope_constants().items()]:
        a = _np.ascontiguousarray(value)
        arrays[f"in_{name}"] = a
        args[name] = nc.dram_tensor(f"in_{name}", a.shape, mybir.dt.from_np(a.dtype), kind="ExternalInput").ap()
    out = nc.dram_tensor("out", (1, S, D), F32, kind="ExternalOutput").ap()
    build(nc, args, out)
    r = _run(nc, [arrays], core_ids=[0])
    return r.results[0]["out"]
```

```python
import math
from contextlib import ExitStack

import numpy as np
import concourse.bass as bass
from concourse import mybir

F32 = mybir.dt.float32
F32R = mybir.dt.float32r
I32 = mybir.dt.int32
U32 = mybir.dt.uint32
ALU = mybir.AluOpType
ACT = mybir.ActivationFunctionType
AX = mybir.AxisListType

P = 128
S = 256
NT = S // P
D = 1024
KD = D // P
EPS = 1e-6
NEG = -1e30
TINY = 1.1754944e-38

B_HEADS, B_DK, B_DV = 8, 32, 64
M_HEADS, HD = 4, 64
D_HEADS, D_GROUPS = 8, 2
A_GROUPS = 4
C_KERNEL, C_BLOCKS = 31, 4
CMP_BLOCK, CMP_STRIDE = 32, 16
N_CMP = (S - CMP_BLOCK) // CMP_STRIDE + 1
MIX = 1280
KMIX = MIX // P
LAM_INIT = 0.8 - 0.6 * math.exp(-0.3)
ROPE_THETA, ROPE_THETA_2 = 500000.0, 10000.0

EVEN_IN, ODD_IN = 4096, 3864
CONV_WIDTH, LRU_HEADS = 4, 4
MLA_HEADS, QK_NOPE, QK_ROPE, V_HEAD = 16, 64, 32, 64
QK = QK_NOPE + QK_ROPE
Q_LORA, KV_LORA = 384, 256
PEER_HEADS, N_KEYS, TOPK = 8, 128, 16
SLOTS = PEER_HEADS * TOPK
TWO_PI = 2.0 * math.pi

EVEN_RANGES = [(0, 1024, "gelu_tanh"), (1024, 1536, "silu"), (1536, 3072, "copy"), (3072, 3584, "silu"),
               (3584, 3840, "copy"), (3840, 4096, "silu")]
ODD_RANGES = [(0, 512, "copy"), (512, 1024, "sigmoid"), (1024, 1536, "silu"), (1536, 2816, "copy"),
              (2816, 2840, "sigmoid"), (2840, 3352, "silu"), (3352, 3608, "copy"), (3608, 3864, "silu")]
FUNCS = {"gelu_tanh": ACT.Gelu_apprx_tanh, "silu": ACT.Silu, "sigmoid": ACT.Sigmoid, "copy": ACT.Copy}

VECTORS = [("mem_norm", 8), ("l0_norm", 8), ("l1_norm", 8), ("l0_a_bs", 4), ("l1_c_conv_w", 124),
           ("l1_c_conv_b", 4), ("norm_mix_g_2", 16), ("norm_ffn_g_2", 16), ("kv_norm_g_2", 8),
           ("lru_conv_w_2", 32), ("lru_conv_b_2", 8), ("lru_ba_2", 8), ("lru_bx_2", 8),
           ("lru_lambda_2", 8), ("c_2", 8),
           ("ada_b_2", 96), ("kv_ada_b_2", 16)]


def rope_constants():
    pos = np.arange(S, dtype=np.float32)
    end = (np.arange(N_CMP) * CMP_STRIDE + CMP_BLOCK - 1).astype(np.float32)
    out = {}
    for name, p, half in (("rope4", pos, 4), ("rope8", pos, 8), ("ropec", end, 8)):
        inv = (np.float32(ROPE_THETA) ** (-np.arange(half, dtype=np.float32) / half)).astype(np.float32)
        ang = (p[:, None] * inv[None, :]).astype(np.float32)
        out[name] = np.concatenate([np.cos(ang), np.sin(ang)], axis=1).astype(np.float32)
    half = QK_ROPE // 2
    out["freqs"] = (np.float32(ROPE_THETA_2) ** (-np.arange(half, dtype=np.float32) / half)).astype(np.float32)
    return out


class Ordered:

    def __init__(self, own, counts):
        self.own, self.counts, self.eng = own, counts, None

    def on(self, eng):
        self.eng = eng
        return self

    def __call__(self, ins, sem=None, wait=True):
        sem = self.own if sem is None else sem
        ins.then_inc(sem, 1)
        n = self.counts.get(sem.num, 0) + 1
        self.counts[sem.num] = n
        if wait:
            self.eng.wait_ge(sem, n)
        return n


def build(nc, I, out, upto=99):
    ctx = ExitStack()
    counts = {}
    lasting = lambda name: ctx.enter_context(nc.semaphore(name))
    of_stage, cleared = [], []

    def sem(name):
        of_stage.append(nc.alloc_semaphore(name))
        return of_stage[-1]

    class StageBlock:

        def __enter__(self):
            self.block = nc.Block()
            return self.block.__enter__()

        def __exit__(self, *exc):
            self.block.__exit__(*exc)
            for s in cleared:
                nc.release_semaphore(s)
            cleared[:] = of_stage
            of_stage.clear()
            for s in cleared:
                nc.sync.sem_clear(s)
                counts.pop(s.num, None)

    BASE = 16512
    TOP = 229344
    at = [BASE]

    def place(name, shape, dt=F32, size=None):
        n = size or int(np.prod(shape[1:])) * 4
        t = nc.alloc_sbuf_tensor_at(name, list(shape), dt, offset=at[0])
        at[0] += (n + 31) // 32 * 32
        return t

    NV = sum(n for _, n in VECTORS)
    NVT = (NV + P - 1) // P
    COLS = place("cols", [P, NVT * P])
    MOD = place("mod", [P, 2 * 48 + 16])
    GM = place("gain_mod", [P, 5, KD])
    ident = place("ident", [P, P])
    iota = place("iota_row", [P, P])
    stats = place("stats", [P, 64])
    CS = place("silu_c", [P, KD])
    X = place("x_res", [P, NT, D])
    AUX = at[0]
    HTH = place("h_t_high", [P, KD, S], F32R)
    HTL = place("h_t_low", [P, KD, S], F32R)
    at[0] = AUX
    GROW = place("gate_row", [P, D])
    TMP = place("gated", [P, 512])
    RINGS = at[0] = AUX + 4 * KD * S * 2
    HT = place("h_t", [P, KD, S])
    slot_e1 = place("slot_e1", [P, S])
    slot_e2 = place("slot_e2", [P, S])
    slot_g = place("slot_gate", [P, S])
    PANELS = at[0]
    col = {}
    n = 0
    for name, rows in VECTORS:
        col[name] = n
        n += rows

    def C(name, i=0, n=1):
        return COLS[:, col[name] + i:col[name] + i + n]

    SLOT = KMIX * 512 * 4
    WORK = max(PANELS + 2 * SLOT, RINGS + 53248)
    WORK_END = WORK + N_KEYS * S * 4
    assert WORK_END <= TOP, (WORK_END, TOP)
    slots = [nc.alloc_sbuf_tensor_at(f"panel{i}", [P, SLOT // 4], F32, offset=o)
             for i, o in enumerate((PANELS, PANELS + SLOT, WORK_END - SLOT))]

    MOD_RING = WORK_END - SLOT - 20480
    mod_ring = nc.alloc_sbuf_tensor_at("mod_ring", [P, 4, 2, 512], F32, offset=MOD_RING)
    mod_acc = nc.alloc_sbuf_tensor_at("mod_acc", [P, 2, 512], F32, offset=MOD_RING + 16384)

    class Zone:
        def __init__(self):
            self.at, self.n, self.limit = WORK, 0, MOD_RING

        def __call__(self, name, shape, dt=F32):
            self.n += 1
            t = nc.alloc_sbuf_tensor_at(f"{name}_{self.n}", list(shape), dt, offset=self.at)
            self.at += (int(np.prod(shape[1:])) * 4 + 31) // 32 * 32
            assert self.at <= self.limit, (name, self.at, self.limit)
            return t

    zone = Zone()
    banks = [nc.alloc_psum_tensor(f"bank{i}", [P, 512], F32) for i in range(8)]

    pe_order, act_order, dve_order, pool_order = (lasting(x) for x in ("pe_order", "act_order", "dve_order", "pool_order"))
    pe_f, act_f, dve_f, pool_f = (Ordered(s, counts) for s in (pe_order, act_order, dve_order, pool_order))
    loaded = [lasting(f"panel_loaded{i}") for i in range(3)]
    acc_ready = lasting("acc_ready")
    acc_free = {"a": lasting("acc_free_act"), "v": lasting("acc_free_dve")}
    small_loaded = lasting("small_loaded")
    small = [0]

    panels = []

    def panel(loads, groups):
        panels.append((loads, groups))
        return len(panels) - 1

    def rows_by_k(w, k, n0, n):
        view = lambda slot: slot[:, 0:k * n].rearrange("p (k n) -> p k n", k=k)
        return view, w[:, n0:n0 + n].rearrange("(k p) n -> p k n", p=P)

    def wide(w, k, total, groups=2, width=512):
        return [panel([rows_by_k(w, k, n0, min(width, total - n0))], groups) for n0 in range(0, total, width)]

    pn = {}
    pn["mkv"] = [panel([rows_by_k(I[f"l{l}_m_wkv"], KD, 0, 512)], 2) for l in range(2)]
    pn["even_in"] = wide(I["l0_w_in"], KD, EVEN_IN)
    pn["even_out"] = wide(I["l0_w_out"], KMIX, D)
    pn["odd_in"] = wide(I["l1_w_in"], KD, ODD_IN)

    CMP_K = CMP_BLOCK // 2

    def cmp_mats(w, o):
        view = lambda slot: slot[:, o * CMP_K * P:(o + 1) * CMP_K * P].rearrange("p (k h) -> p k h", h=P)
        return view, w.rearrange("(k p) h -> p k h", p=P)

    pn["cmp"] = [panel([cmp_mats(I["l1_d_cmp_w1_k"], 0), cmp_mats(I["l1_d_cmp_w1_v"], 1)], 2)]
    pn["odd_out"] = wide(I["l1_w_out"], KMIX, D)
    pn["lru_in"] = wide(I["lru_w_in_2"][0], KD, 2 * D)

    def head_mats(w, o):
        view = lambda slot: slot[:, o:o + 2048].rearrange("p (h n) -> p h n", h=8)
        return view, w[0].rearrange("h (i p) j -> p (h i) j", p=P)

    pn["lru_gates"] = [panel([head_mats(I["lru_wa_2"], 0), head_mats(I["lru_wx_2"], 2048)], 8)]
    pn["lru_out"] = wide(I["lru_w_out_2"][0], KD, D)
    pn["peer_q0"] = wide(I["peer_w_q_2"][0], KD, 2 * D)

    def side(w, k, o, n, total):
        view = lambda slot: slot[:, 0:k * total].rearrange("p (k n) -> p k n", k=k)[:, :, o:o + n]
        return view, w.rearrange("(k p) n -> p k n", p=P)

    pn["dkv"] = [panel([side(I["mla_w_dkv_2"], KD, 0, KV_LORA, 288), side(I["mla_w_kr_2"], KD, KV_LORA, 32, 288)], 2)]

    def stacked(w, k, o, n):
        view = lambda slot: slot[:, o * n:(o + k) * n].rearrange("p (k n) -> p k n", k=k)
        return view, w.rearrange("(k p) n -> p k n", p=P)

    pn["ukv"] = [panel([stacked(I["mla_w_uk_2"], 2, 0, D), stacked(I["mla_w_uv_2"], 2, 2, D)], 8)]
    pn["dq"] = [panel([rows_by_k(I["mla_w_dq_2"][0], KD, 0, Q_LORA)], 2)]
    pn["uq"] = [panel([rows_by_k(I["mla_w_uq_2"][0], 3, 0, MLA_HEADS * QK)], 6)]
    pn["mla_out"] = wide(I["mla_w_o_2"][0], KD, D)
    pn["peer_q1"] = wide(I["peer_w_q_2"][1], KD, 2 * D)

    first_group, dma_value = [0], []
    slot_count = [0, 0, 0]
    for i, (loads, groups) in enumerate(panels):
        first_group.append(first_group[-1] + groups)
        slot_count[i % 3] += 16 * len(loads)
        dma_value.append(slot_count[i % 3])
    issued = [0]

    def load_panels(sp, last):
        while issued[0] <= min(last, len(panels) - 1):
            i = issued[0]
            if i >= 3:
                sp.wait_ge(acc_ready, first_group[i - 2])
            for view, src in panels[i][0]:
                sp.dma_start(view(slots[i % 3]), src).then_inc(loaded[i % 3], 16)
            issued[0] += 1

    def wait_panel(pe, i):
        pe.wait_ge(loaded[i % 3], dma_value[i])

    owners = []

    def acc_bank(g):
        return banks[g % 4]

    def wait_acc_free(pe, g):
        if g >= 4:
            o = owners[g - 4]
            pe.wait_ge(acc_free[o], owners[:g - 3].count(o))

    def load_small(eng, pairs):
        for dst, src in pairs:
            eng.dma_start(dst, src).then_inc(small_loaded, 16)
            small[0] += 16

    def bcast(vec):
        return vec.partition_broadcast(P)

    class Stage:
        count = 0

    def stage():
        Stage.count += 1
        return Stage.count <= upto

    mod_panels = [(w, n0) for w, total in ((I["ada_w_2"][0], 6 * D), (I["ada_w_2"][1], 6 * D), (I["kv_ada_w_2"], 2 * D))
                  for n0 in range(0, total, 512)]
    mod_loaded = [lasting(f"mod_piece_loaded{i}") for i in range(4)]
    mod_used, mod_turned, mod_reduced = (
        lasting(f"mod_{x}") for x in ("piece_used", "turned", "reduced"))

    class Modulation:
        steps, loads, turned, reduced = 0, 0, 0, 0
        total = len(mod_panels) * KD

        def load(self, sp, steps):
            while self.loads < min((self.steps_planned + steps) // 2 + 4, self.total // 2):
                q = self.loads
                w, n0 = mod_panels[q // 4]
                if q >= 4:
                    sp.wait_ge(mod_used, q - 3)
                r = 2 * (q % 4) * P
                sp.dma_start(mod_ring[:, q % 4, :, :], w[r:r + 2 * P, n0:n0 + 512].rearrange("(k p) n -> p k n", p=P))\
                    .then_inc(mod_loaded[q % 4], 16)
                self.loads += 1
            self.steps_planned += steps

        steps_planned = 0

        def add(self, f, dve, steps):
            for _ in range(min(steps, self.total - self.steps)):
                n = self.steps
                q, k, panel = n // 2, n % KD, n // KD
                if n % 2 == 0:
                    dve.wait_ge(mod_loaded[q % 4], 16 * (q // 4) + 16)
                src, acc, c = mod_ring[:, q % 4, n % 2, :], mod_acc[:, panel % 2, :], CS[:, k:k + 1]
                if k == 0:
                    if panel >= 2:
                        dve.wait_ge(mod_turned, panel - 1)
                    ins = nc.vector.tensor_scalar(acc, src, c, None, ALU.mult)
                else:
                    ins = nc.vector.scalar_tensor_tensor(acc, src, c, acc, ALU.mult, ALU.add)
                if n % 2:
                    f(ins, mod_used)
                else:
                    f(ins)
                self.steps += 1

        def turn(self, pe, upto_step):
            while (self.turned + 1) * KD <= upto_step:
                n = self.turned
                pe.wait_ge(mod_used, 4 * n + 4)
                if n >= 2:
                    pe.wait_ge(mod_reduced, n - 1)
                for j in range(4):
                    last = nc.tensor.transpose(banks[4 + n % 2][:, j * P:(j + 1) * P],
                                               mod_acc[:, n % 2, j * P:(j + 1) * P], ident[:, :])
                last.then_inc(mod_turned, 1)
                self.turned += 1

        def reduce(self, f, dve, upto_step):
            while (self.reduced + 1) * KD <= upto_step:
                n = self.reduced
                dve.wait_ge(mod_turned, n + 1)
                f(nc.vector.tensor_reduce(MOD[:, 4 * n:4 * n + 4], banks[4 + n % 2][:, :].rearrange("p (a b) -> p a b", a=4),
                                          AX.X, ALU.add), mod_reduced)
                self.reduced += 1

    modulation = Modulation()


    def project(name, lhs, evac, owner, K=KD, width=None, chunks=None, ahead=3, mod_steps=0,
                beside=None):
        if not stage():
            return
        ps = pn[name]
        if chunks is None:
            ns = [min(512, width - 512 * i) for i in range(len(ps))]
            chunks = [(i, (lambda slot, n=n: slot[:, 0:K * n].rearrange("p (k n) -> p k n", k=K)), K)
                      for i, n in enumerate(ns)]
        g0 = first_group[ps[0]]
        todo = [(i, ps[c], view, k, t) for i, (c, view, k) in enumerate(chunks) for t in range(NT)]
        owners.extend(owner(i, t) for i, _, _, _, t in todo)
        m0 = modulation.steps
        with StageBlock() as block:
            @block.sync
            def _(sp):
                for j, (_, p, _, _, _) in enumerate(todo):
                    modulation.load(sp, mod_steps)
                    load_panels(sp, min(p + 3, ps[-1] + ahead))
                load_panels(sp, ps[-1] + ahead)

            @block.tensor
            def _(pe):
                for j, (i, p, view, k, t) in enumerate(todo):
                    w = view(slots[p % 3])
                    n = w.shape[2]
                    wait_panel(pe, p)
                    wait_acc_free(pe, g0 + j)
                    for q in range(k):
                        last = nc.tensor.matmul(acc_bank(g0 + j)[:, 0:n], lhs(i, q, t), w[:, q, :],
                                                start=(q == 0), stop=(q == k - 1))
                    last.then_inc(acc_ready, 1)
                    if mod_steps:
                        modulation.turn(pe, m0 + j * mod_steps)
                    if beside:
                        beside["pe"](pe, j)
                if mod_steps:
                    modulation.turn(pe, min(modulation.total, m0 + len(todo) * mod_steps))

            for who, get, eng_name in (("a", act_f, "scalar"), ("v", dve_f, "vector")):
                def body(eng, who=who, get=get):
                    f = get.on(eng)
                    for j, (i, _, _, _, t) in enumerate(todo):
                        if who == "v" and mod_steps:
                            modulation.add(f, eng, mod_steps)
                            modulation.reduce(f, eng, m0 + (j - 1) * mod_steps)
                        if owners[g0 + j] == who:
                            eng.wait_ge(acc_ready, g0 + j + 1)
                            evac(f, who, i, t, acc_bank(g0 + j), acc_free[who])
                        if beside and who == "v":
                            beside["dve"](f, eng, j)
                    if who == "v" and mod_steps:
                        modulation.reduce(f, eng, modulation.steps)
                (block.scalar if who == "a" else block.vector)(body)

    def copy_evac(dst, c_of):
        def evac(f, who, i, t, bank, free):
            c0, n = c_of(i)
            if who == "a":
                f(nc.scalar.activation(dst[:, t, c0:c0 + n], bank[:, 0:n], ACT.Copy), free, wait=False)
            else:
                f(nc.vector.tensor_copy(dst[:, t, c0:c0 + n], bank[:, 0:n]), free, wait=False)
        return evac

    def project_t(name, w_of, groups, ks, rhs, evac, owner, ahead=3, mod_steps=0):
        if not stage():
            return
        ps = pn[name]
        g0 = first_group[ps[0]]
        per = groups // len(ps)
        owners.extend(owner(g) for g in range(groups))
        m0 = modulation.steps
        with StageBlock() as block:
            @block.sync
            def _(sp):
                for g in range(groups):
                    modulation.load(sp, mod_steps)
                    load_panels(sp, min(ps[g // per] + 3, ps[-1] + ahead))
                load_panels(sp, ps[-1] + ahead)

            @block.tensor
            def _(pe):
                for g in range(groups):
                    p = ps[g // per]
                    wait_panel(pe, p)
                    wait_acc_free(pe, g0 + g)
                    for h in range(2):
                        for k in range(ks):
                            last = nc.tensor.matmul(acc_bank(g0 + g)[:, h * S:(h + 1) * S],
                                                    w_of(slots[p % 3], g, h, k), rhs(g, h, k),
                                                    start=(k == 0), stop=(k == ks - 1))
                    last.then_inc(acc_ready, 1)
                    if mod_steps:
                        modulation.turn(pe, m0 + g * mod_steps)
                if mod_steps:
                    modulation.turn(pe, min(modulation.total, m0 + groups * mod_steps))

            def body(eng, who, get):
                f = get.on(eng)
                for g in range(groups):
                    if who == "v" and mod_steps:
                        modulation.add(f, eng, mod_steps)
                        modulation.reduce(f, eng, m0 + (g - 1) * mod_steps)
                    if owners[g0 + g] == who:
                        eng.wait_ge(acc_ready, g0 + g + 1)
                        evac(f, who, g, acc_bank(g0 + g), acc_free[who])
                if who == "v" and mod_steps:
                    modulation.reduce(f, eng, modulation.steps)

            @block.scalar
            def _(act):
                body(act, "a", act_f)

            @block.vector
            def _(dve):
                body(dve, "v", dve_f)

    def inverse_root(f, v, y, t, mean_done, root_done, eng):
        eng.wait_ge(root_done, 1)
        f(nc.vector.reciprocal(y, y))
        f(nc.vector.tensor_tensor(t, y, y, ALU.mult))
        f(nc.vector.tensor_tensor(t, t, v, ALU.mult))
        f(nc.vector.tensor_scalar(t, t, -0.5, 1.5, ALU.mult, ALU.add))
        f(nc.vector.tensor_tensor(y, y, t, ALU.mult))

    def norm_transpose(src, dst, jobs, width=D):
        if not stage():
            return
        K = width // P
        mark = zone.at
        xn = zone("normed", [P, NT, width])
        n = Stage.count
        sq_done, mean_done, root_done, xn_done, tr_done, tr_free = (
            sem(f"norm{n}_{x}") for x in ("squares", "mean", "root", "normed", "transposed", "free"))
        with StageBlock() as block:
            @block.scalar
            def _(act):
                f = act_f.on(act)
                for t in range(NT):
                    f(nc.scalar.activation(xn[:, t, :], src[:, t, 0:width], ACT.Square,
                                           accum_out=stats[:, t:t + 1]), sq_done)
                act.wait_ge(mean_done, 1)
                f(nc.scalar.activation(stats[:, 4:4 + NT], stats[:, 0:NT], ACT.Sqrt), root_done)

            @block.vector
            def _(dve):
                f = dve_f.on(dve)
                dve.wait_ge(sq_done, NT)
                f(nc.vector.tensor_scalar(stats[:, 0:NT], stats[:, 0:NT], 1.0 / width, EPS, ALU.mult, ALU.add), mean_done)
                inverse_root(f, stats[:, 0:NT], stats[:, 4:4 + NT], stats[:, 8:8 + NT], mean_done, root_done, dve)
                for t in range(NT):
                    f(nc.vector.tensor_scalar(xn[:, t, :], src[:, t, 0:width], stats[:, 4 + t:5 + t], None, ALU.mult),
                      xn_done)
                for k in range(K):
                    dve.wait_ge(tr_done, (k | 1) + 1)
                    got = banks[4 + (k // 2) % 4][:, (k % 2) * S:(k % 2 + 1) * S]
                    for d, mult, add in jobs:
                        if add is None:
                            ins = nc.vector.tensor_scalar(d[:, k, :], got, mult[:, k:k + 1], None, ALU.mult)
                        else:
                            ins = nc.vector.tensor_scalar(d[:, k, :], got, mult[:, k:k + 1], add[:, k:k + 1],
                                                          ALU.mult, ALU.add)
                        f(ins, wait=False)

            @block.tensor
            def _(pe):
                pe.wait_ge(xn_done, NT)
                for k in range(K):
                    for t in range(NT):
                        c = (k % 2) * S + t * P
                        last = nc.tensor.transpose(banks[4 + (k // 2) % 4][:, c:c + P],
                                                   xn[:, t, k * P:(k + 1) * P], ident[:, :])
                    last.then_inc(tr_done, 1)
        zone.at = mark

    def transpose_all(pieces, loads=()):
        if not stage():
            return
        n = Stage.count
        tr_done = sem(f"tr{n}_done")
        freed = {"a": sem(f"tr{n}_free_act"), "v": sem(f"tr{n}_free_dve")}
        v0 = small[0] + 16 * len(loads)
        with StageBlock() as block:
            @block.sync
            def _(sp):
                load_small(sp, loads)

            @block.tensor
            def _(pe):
                if loads:
                    pe.wait_ge(small_loaded, v0)
                for i, (dst, src) in enumerate(pieces):
                    r, c = src.shape
                    if i >= 8:
                        who = "a" if i % 2 == 0 else "v"
                        pe.wait_ge(freed[who], (i - 8) // 2 + 1)
                    nc.tensor.transpose(banks[i % 8][0:c, 0:r], src, ident[0:r, 0:r]).then_inc(tr_done, 1)

            def body(eng, who, get):
                f = get.on(eng)
                for i, (dst, src) in enumerate(pieces):
                    if ("a" if i % 2 == 0 else "v") != who:
                        continue
                    r, c = src.shape
                    eng.wait_ge(tr_done, i + 1)
                    if who == "a":
                        ins = nc.scalar.activation(dst, banks[i % 8][0:c, 0:r], ACT.Copy)
                    else:
                        ins = nc.vector.tensor_copy(dst, banks[i % 8][0:c, 0:r])
                    f(ins, freed[who], wait=False)

            @block.scalar
            def _(act):
                body(act, "a", act_f)

            @block.vector
            def _(dve):
                body(dve, "v", dve_f)

    def group_norms(f, eng, ss, todo, mean_done, root_done, sq):
        p = todo[0][0].shape[0]
        c = 0
        for i, (src, dst, gain, d) in enumerate(todo):
            G = src.shape[1]
            view = sq[0:p, 0:G * d].rearrange("p (g d) -> p g d", d=d)
            f(nc.vector.tensor_tensor(view, src, src, ALU.mult))
            f(nc.vector.tensor_reduce(ss[0:p, 0, c:c + G], view, AX.X, ALU.add))
            f(nc.vector.tensor_scalar(ss[0:p, 0, c:c + G], ss[0:p, 0, c:c + G], 1.0 / d, EPS, ALU.mult, ALU.add),
              mean_done if i == len(todo) - 1 else None)
            c += G
        inverse_root(f, ss[0:p, 0, 0:c], ss[0:p, 1, 0:c], ss[0:p, 2, 0:c], mean_done, root_done, eng)
        c = 0
        for src, dst, gain, d in todo:
            G = src.shape[1]
            f(nc.vector.tensor_tensor(dst, src, ss[0:p, 1, c:c + G].unsqueeze(2).broadcast_to([p, G, d]), ALU.mult))
            if len(gain.shape) == 2:
                gain = gain[0:p].unsqueeze(1).broadcast_to([p, G, d])
            f(nc.vector.tensor_tensor(dst, dst, gain, ALU.mult))
            c += G

    def group_roots(f, eng, ss, todo, mean_done, root_done):
        p, c = todo[0][0].shape[0], sum(src.shape[1] for src, _, _, _ in todo)
        eng.wait_ge(mean_done, 1)
        f(nc.scalar.activation(ss[0:p, 1, 0:c], ss[0:p, 0, 0:c], ACT.Sqrt), root_done)

    def rope(f, x, cos, sin, half, tmp):
        p, G, _ = x.shape
        c = cos.unsqueeze(1).broadcast_to([p, G, half])
        s = sin.unsqueeze(1).broadcast_to([p, G, half])
        v = [tmp[0:p, i * G * half:(i + 1) * G * half].rearrange("p (g h) -> p g h", h=half) for i in range(4)]
        x1, x2 = x[:, :, 0:half], x[:, :, half:2 * half]
        f(nc.vector.tensor_tensor(v[0], x1, c, ALU.mult), wait=False)
        f(nc.vector.tensor_tensor(v[1], x2, s, ALU.mult), wait=False)
        f(nc.vector.tensor_tensor(v[2], x1, s, ALU.mult), wait=False)
        f(nc.vector.tensor_tensor(v[3], x2, c, ALU.mult))
        f(nc.vector.tensor_tensor(x1, v[0], v[1], ALU.subtract), wait=False)
        f(nc.vector.tensor_tensor(x2, v[2], v[3], ALU.add))

    def attention(units):
        if not stage():
            return
        mark = zone.at
        n = Stage.count
        room = HT[:, :, :]
        s_sb, p_sb = ([room[:, 4 * x + y, :] for y in range(4)] for x in range(2))
        s_bank = [banks[x] for x in (0, 1, 6, 7)]
        pt_sb = [zone("probs_t", [P, NT, P]) for _ in range(2)]
        st = zone("softmax_stats", [P, 8, 4])
        scored, maxed, exped, turned, pt_ready, pv_done, out_done, s_taken = (
            sem(f"att{n}_{x}") for x in ("scored", "maxed", "exped", "turned", "pt_ready", "pv_done", "out_done", "s_taken"))
        N = len(units)
        tiles = lambda u: [(k, min(P, u["nk"] - k * P)) for k in range((u["nk"] + P - 1) // P)]
        with StageBlock() as block:
            @block.tensor
            def _(pe):
                for i in range(N + 4):
                    if i < N:
                        u = units[i]
                        if i >= 4:
                            pe.wait_ge(s_taken, i - 3)
                        nc.tensor.matmul(s_bank[i % 4][:, 0:u["nk"]], u["qT"], u["kT"], start=True, stop=True)\
                            .then_inc(scored, 1)
                    if 3 <= i <= N + 2:
                        j, u = i - 3, units[i - 3]
                        pe.wait_ge(exped, j + 1)
                        if j >= 2:
                            pe.wait_ge(pt_ready, j - 1)
                        for k, m in tiles(u):
                            last = nc.tensor.transpose(banks[2 + j % 2][0:m, k * P:(k + 1) * P],
                                                       p_sb[j % 4][:, k * P:k * P + m], ident[:, :])
                        last.then_inc(turned, 1)
                    if i >= 4:
                        j, u = i - 4, units[i - 4]
                        pe.wait_ge(pt_ready, j + 1)
                        if j >= 2:
                            pe.wait_ge(out_done, j - 1)
                        tl = tiles(u)
                        for k, m in tl:
                            last = nc.tensor.matmul(banks[4 + j % 2][:, 0:u["v"][0].shape[1]], pt_sb[j % 2][0:m, k, :],
                                                    u["v"][k], start=(k == 0), stop=(k == len(tl) - 1))
                        last.then_inc(pv_done, 1)

            @block.scalar
            def _(act):
                f = act_f.on(act)
                for i in range(N + 1):
                    if i < N:
                        u = units[i]
                        act.wait_ge(maxed, i + 1)
                        if i >= 4:
                            act.wait_ge(turned, i - 3)
                        f(nc.scalar.activation(p_sb[i % 4][:, 0:u["nk"]], s_sb[i % 4][:, 0:u["nk"]], ACT.Exp,
                                               bias=st[:, i % 8, 0:1], accum_out=st[:, i % 8, 1:2]), exped, wait=False)
                    if i >= 1:
                        j, u = i - 1, units[i - 1]
                        act.wait_ge(turned, j + 1)
                        if j >= 2:
                            act.wait_ge(pv_done, j - 1)
                        m = min(P, u["nk"])
                        w = len(tiles(u)) * P
                        f(nc.scalar.activation(pt_sb[j % 2][0:m, :, :].rearrange("p a b -> p (a b)")[:, 0:w],
                                               banks[2 + j % 2][0:m, 0:w], ACT.Copy), pt_ready, wait=False)

            @block.vector
            def _(dve):
                f = dve_f.on(dve)
                inverted = {}
                for i in range(N + 5):
                    if i < N:
                        u = units[i]
                        nk = u["nk"]
                        s = s_sb[i % 4][:, 0:nk]
                        dve.wait_ge(scored, i + 1)
                        if i >= 4:
                            dve.wait_ge(exped, i - 3)
                        if u["mask"] is None:
                            ins = nc.vector.tensor_scalar(s, s_bank[i % 4][:, 0:nk], u["scale"], None, ALU.mult)
                        else:
                            ins = nc.vector.scalar_tensor_tensor(s, s_bank[i % 4][:, 0:nk], u["scale"], u["mask"],
                                                                 ALU.mult, ALU.add)
                        f(ins, s_taken, wait=False)
                    if 1 <= i <= N:
                        m, u = i - 1, units[i - 1]
                        dve.wait_ge(s_taken, m + 1)
                        ins = nc.vector.tensor_reduce(st[:, m % 8, 0:1], s_sb[m % 4][:, 0:u["nk"]], AX.X, ALU.max, negate=True)
                        if u["guard"]:
                            low = f(ins, wait=False)
                        else:
                            f(ins, maxed, wait=False)
                    if i >= 3 and i - 3 < N:
                        r, u = i - 3, units[i - 3]
                        dve.wait_ge(exped, r + 1)
                        total, inv = st[:, r % 8, 1:2], st[:, r % 8, 2:3]
                        if u["guard"]:
                            f(nc.vector.tensor_scalar(total, total, TINY, None, ALU.max))
                        new_inverse = f(nc.vector.reciprocal(inv, total), wait=False)
                    else:
                        new_inverse = None
                    if 1 <= i <= N and units[i - 1]["guard"]:
                        neg_max = st[:, (i - 1) % 8, 0:1]
                        dve.wait_ge(dve_order, low)
                        f(nc.vector.tensor_scalar(neg_max, neg_max, 1e29, None, ALU.min), maxed, wait=False)
                    if i >= 4 and i - 4 < N and units[i - 4]["coef"] is not None:
                        c, u = i - 4, units[i - 4]
                        inv = st[:, c % 8, 2:3]
                        dve.wait_ge(dve_order, inverted[c])
                        inverted[c] = f(nc.vector.tensor_tensor(inv, inv, u["coef"], ALU.mult), wait=False)
                    if i >= 5:
                        j, u = i - 5, units[i - 5]
                        dve.wait_ge(dve_order, inverted[j])
                        dve.wait_ge(pv_done, j + 1)
                        inv = st[:, j % 8, 2:3]
                        bank = banks[4 + j % 2][:, 0:u["v"][0].shape[1]]
                        if u["add"]:
                            dve.wait_ge(out_done, j)
                            ins = nc.vector.scalar_tensor_tensor(u["out"], bank, inv, u["out"], ALU.mult, ALU.add)
                        else:
                            ins = nc.vector.tensor_scalar(u["out"], bank, inv, None, ALU.mult)
                        f(ins, out_done, wait=False)
                    if new_inverse is not None:
                        inverted[i - 3] = new_inverse
        zone.at = mark

    def elementwise(dve_body=None, act_body=None, loads=(), pool_body=None, pe_body=None, prefetch_to=None):
        if not stage():
            return
        v0 = small[0] + 16 * len(loads)
        with StageBlock() as block:
            @block.sync
            def _(sp):
                load_small(sp, loads)
                if prefetch_to is not None:
                    load_panels(sp, prefetch_to)

            if act_body:
                @block.scalar
                def _(act):
                    if loads:
                        act.wait_ge(small_loaded, v0)
                    act_body(act_f.on(act), act)

            if dve_body:
                @block.vector
                def _(dve):
                    if loads:
                        dve.wait_ge(small_loaded, v0)
                    dve_body(dve_f.on(dve), dve)

            if pool_body:
                @block.gpsimd
                def _(pool):
                    if loads:
                        pool.wait_ge(small_loaded, v0)
                    pool_body(pool_f.on(pool), pool)

            if pe_body:
                @block.tensor
                def _(pe):
                    if loads:
                        pe.wait_ge(small_loaded, v0)
                    pe_body(pe_f.on(pe), pe)

    causal = zone("causal_mask", [P, S])
    cmpmask = zone("cmp_mask", [P, NT, N_CMP])
    masks_end = zone.at
    memx = zone("mem_rows", [P, NT, D])
    staged = zone("vector_rows", [P, NVT, P])
    vec_dmas, row = [], 0
    for name, rows in VECTORS:
        src = I[name]
        flat = src.rearrange(" ".join(f"d{i}" for i in range(len(src.shape))) + " -> (" +
                             " ".join(f"d{i}" for i in range(len(src.shape))) + ")") if len(src.shape) > 1 else src
        flat = flat.rearrange("(r c) -> r c", c=P)
        done = 0
        while done < rows:
            tile, r = divmod(row, P)
            m = min(rows - done, P - r)
            vec_dmas.append((staged[r:r + m, tile, :], flat[done:done + m, :]))
            done += m
            row += m

    def pool_constants(f, pool):
        f(nc.gpsimd.memset(ident[:, :], 0.0))
        f(nc.gpsimd.affine_select(out=ident[:, :], in_=ident[:, :], compare_op=ALU.not_equal, fill=1.0, base=0,
                                  pattern=[[-1, P]], channel_multiplier=1))
        f(nc.gpsimd.memset(causal[:, :], 0.0))
        f(nc.gpsimd.affine_select(out=causal[:, P:S], in_=causal[:, P:S], compare_op=ALU.is_ge, fill=NEG, base=0,
                                  pattern=[[-1, P]], channel_multiplier=1))
        f(nc.gpsimd.memset(cmpmask[:, :, :], 0.0))
        f(nc.gpsimd.affine_select(out=cmpmask[:, :, :], in_=cmpmask[:, :, :], compare_op=ALU.is_ge, fill=NEG,
                                  base=-(CMP_BLOCK - 1), pattern=[[P, NT], [-CMP_STRIDE, N_CMP]], channel_multiplier=1))
        f(nc.gpsimd.iota(iota[:, :], pattern=[[1, P]], base=0, channel_multiplier=0,
                         allow_small_or_imprecise_dtypes=True))

    elementwise(pool_body=pool_constants,
                loads=[(X[:, :, :], I["x"][0].rearrange("(t p) d -> p t d", p=P)),
                       (memx[:, :, :], I["mem"][0].rearrange("(t p) d -> p t d", p=P))] + vec_dmas,
                prefetch_to=2)
    last_rows = NV - (NVT - 1) * P
    transpose_all([(COLS[:, t * P:t * P + (P if t < NVT - 1 else last_rows)],
                    staged[0:(P if t < NVT - 1 else last_rows), t, :]) for t in range(NVT)])

    elementwise(act_body=lambda f, act: f(nc.scalar.activation(CS[:, :], C("c_2", 0, 8), ACT.Silu)))

    norm_transpose(memx, HT, [(HT, C("mem_norm", 0, 8), None)])
    zone.at = masks_end
    MKT = zone("mem_k_t", [P, 2, 2, S])
    MV = zone("mem_v", [P, 2, NT, 256])
    keep_first = zone.at
    kv_nat = zone("mem_kv", [P, NT, 2, 512])
    ht = lambda i, k, t: HT[:, k, t * P:(t + 1) * P]
    project("mkv", ht,
            lambda f, who, i, t, bank, free: f(
                nc.scalar.activation(kv_nat[:, t, i, :], bank[:, :], ACT.Copy) if who == "a" else
                nc.vector.tensor_copy(kv_nat[:, t, i, :], bank[:, :]), free, wait=False),
            lambda i, t: "av"[t], width=1024)
    gk = zone("mem_gains", [P, 2, HD])
    sq = zone("squares", [P, D])
    ss = zone("sums", [P, 3, 80])

    def norm_stage(todo, loads=(), after=None, before=None):
        if Stage.count >= upto:
            stage()
            return
        n = Stage.count
        mean_done, root_done = sem(f"gn{n}_mean"), sem(f"gn{n}_root")

        def dve_body(f, dve):
            if before:
                before(f, dve)
            group_norms(f, dve, ss, todo, mean_done, root_done, sq)
            if after:
                after(f, dve)

        elementwise(dve_body, lambda f, act: group_roots(f, act, ss, todo, mean_done, root_done), loads=loads)

    def mem_copy_v(f, dve):
        for t in range(NT):
            for l in range(2):
                f(nc.vector.tensor_copy(MV[:, l, t, :], kv_nat[:, t, l, 256:512]), wait=False)

    norm_stage([(kv_nat[:, t, l, 0:256].rearrange("p (h d) -> p h d", d=HD),
                 kv_nat[:, t, l, 0:256].rearrange("p (h d) -> p h d", d=HD), gk[:, l, :], HD)
                for t in range(NT) for l in range(2)],
               loads=[(gk[:, l, :], bcast(I[f"l{l}_m_knorm"])) for l in range(2)], after=mem_copy_v)
    transpose_all([(MKT[:, l, b, t * P:(t + 1) * P], kv_nat[:, t, l, b * P:(b + 1) * P])
                   for l in range(2) for b in range(2) for t in range(NT)])

    def ranges_evac(dst, ranges, width):
        def evac(f, who, i, t, bank, free):
            c0 = i * 512
            n = min(512, width - c0)
            parts = [(max(a, c0), min(b, c0 + n), fn) for a, b, fn in ranges if max(a, c0) < min(b, c0 + n)]
            for j, (a, b, fn) in enumerate(parts):
                last = j == len(parts) - 1
                if who == "v":
                    ins = nc.vector.tensor_copy(dst[:, t, a:b], bank[:, a - c0:b - c0])
                else:
                    ins = nc.scalar.activation(dst[:, t, a:b], bank[:, a - c0:b - c0], FUNCS[fn])
                f(ins, free if last else None, wait=False)
        return evac

    def ranges_owner(ranges, width):
        def owner(i, t):
            c0 = i * 512
            n = min(512, width - c0)
            return "v" if all(fn == "copy" for a, b, fn in ranges if max(a, c0) < min(b, c0 + n)) else "a"
        return owner

    def memory_units(l, qt, outs):
        return [dict(qT=qt[64 * (h % 2):64 * (h % 2) + 64, h // 2, t * P:(t + 1) * P],
                     kT=MKT[64 * (h % 2):64 * (h % 2) + 64, l, h // 2, :], nk=S,
                     v=[MV[:, l, k, h * HD:(h + 1) * HD] for k in range(NT)], scale=HD ** -0.5, mask=None,
                     coef=None, out=outs[:, t, h * HD:(h + 1) * HD], add=False, guard=False)
                for h in range(M_HEADS) for t in range(NT)]

    def out_project(name, K, mixt, gate=None, mod_steps=0):
        def evac(f, who, i, t, bank, free):
            xs = X[:, t, i * 512:(i + 1) * 512]
            if gate is None:
                f(nc.vector.tensor_tensor(xs, bank[:, :], xs, ALU.add), free)
            else:
                tmp = gate[1][:, 0:512]
                f(nc.vector.tensor_tensor(tmp, bank[:, :], gate[0][:, i * 512:(i + 1) * 512], ALU.mult), free)
                f(nc.vector.tensor_tensor(xs, tmp, xs, ALU.add))
        project(name, lambda i, k, t: mixt[:, k, t * P:(t + 1) * P], evac, lambda i, t: "v", K=K, width=D,
                mod_steps=mod_steps)

    norm_transpose(X, HT, [(HT, C("l0_norm", 0, 8), None)])
    zone.at = keep_first
    ss = zone("sums", [P, 3, 80])
    P0 = zone("even_in", [P, NT, EVEN_IN])
    mix = zone("mix", [P, NT, MIX])
    project("even_in", ht, ranges_evac(P0, EVEN_RANGES, EVEN_IN), ranges_owner(EVEN_RANGES, EVEN_IN), width=EVEN_IN,
            mod_steps=4)

    mark0 = zone.at
    vgain = zone("a_vgain", [P, 512])
    sq = zone("squares", [P, D])
    ws = zone("a_ws", [P, A_GROUPS, P])
    wst = zone("a_ws_t", [P, A_GROUPS, P])
    norm_stage([(P0[:, t, 512:1024].rearrange("p (g d) -> p g d", d=P),
                 P0[:, t, 512:1024].rearrange("p (g d) -> p g d", d=P),
                 vgain[:, :].rearrange("p (g d) -> p g d", d=P), P) for t in range(NT)],
               loads=[(vgain[:, :], bcast(I["l0_a_vnorm"])),
                      (ws[:, :, :], I["l0_a_ws"].rearrange("g t s -> t g s"))])
    transpose_all([(wst[:, g, :], ws[:, g, :]) for g in range(A_GROUPS)])
    if Stage.count < upto:
        wmask, z_done = sem("a_w_masked"), sem("a_z_done")

        def a_pool(f, pool):
            f(nc.gpsimd.affine_select(out=wst[:, :, :], in_=wst[:, :, :], compare_op=ALU.is_ge, fill=0.0, base=0,
                                      pattern=[[0, A_GROUPS], [1, P]], channel_multiplier=-1), wmask)

        def a_pe(f, pe):
            pe.wait_ge(wmask, 1)
            for t in range(NT):
                for g in range(A_GROUPS):
                    last = nc.tensor.matmul(banks[t][:, g * P:(g + 1) * P], wst[:, g, :],
                                            P0[:, t, 512 + g * P:512 + (g + 1) * P], start=True, stop=True)
                last.then_inc(z_done, 1)

        def a_dve(f, dve):
            for t in range(NT):
                dve.wait_ge(z_done, t + 1)
                for g in range(A_GROUPS):
                    c = slice(g * P, (g + 1) * P)
                    f(nc.vector.scalar_tensor_tensor(mix[:, t, c], banks[t][:, c], C("l0_a_bs", g),
                                                     P0[:, t, c], ALU.add, ALU.mult))
                f(nc.vector.tensor_tensor(mix[:, t, 0:512], mix[:, t, 0:512], P0[:, t, 1024:1536], ALU.mult))
        elementwise(a_dve, pool_body=a_pool, pe_body=a_pe)
    else:
        stage()
    zone.at = mark0

    sq = zone("squares", [P, D])
    bg = zone("b_gains", [P, 2, B_DK])
    mg = zone("m_qgain", [P, HD])
    rp = zone("rope4", [P, NT, 8])
    lamv = zone("lambda_vecs", [P, 4, B_DK])
    lam = zone("lambda", [P, 4])
    QT = zone("b_q_t", [P, 4, S])
    KT = zone("b_k_t", [P, 4, S])
    MQT = zone("m_q_t", [P, 2, S])
    if Stage.count < upto:
        lam_prod, lam_exp = sem("lambda_dots"), sem("lambda_exps")
        n = Stage.count
        mean_done, root_done = sem(f"gn{n}_mean"), sem(f"gn{n}_root")
        todo = []
        for t in range(NT):
            for a, b, g, d in ((1536, 2048, bg[:, 0, :], B_DK), (2048, 2560, bg[:, 1, :], B_DK), (3584, 3840, mg[:, :], HD)):
                v = P0[:, t, a:b].rearrange("p (g d) -> p g d", d=d)
                todo.append((v, v, g, d))

        def qk_dve(f, dve):
            for i in range(2):
                f(nc.vector.tensor_tensor(lamv[:, 2 * i, :], lamv[:, 2 * i, :], lamv[:, 2 * i + 1, :], ALU.mult))
                f(nc.vector.tensor_reduce(lam[:, i:i + 1], lamv[:, 2 * i, :], AX.X, ALU.add), lam_prod)
            group_norms(f, dve, ss, todo, mean_done, root_done, sq)
            for t in range(NT):
                for v in (todo[3 * t][0], todo[3 * t + 1][0]):
                    rope(f, v, rp[:, t, 0:4], rp[:, t, 4:8], 4, sq)
            dve.wait_ge(lam_exp, 1)
            f(nc.vector.tensor_tensor(lam[:, 2:3], lam[:, 1:2], lam[:, 0:1], ALU.subtract))
            f(nc.vector.tensor_scalar(lam[:, 2:3], lam[:, 2:3], -LAM_INIT, None, ALU.add))

        def qk_act(f, act):
            act.wait_ge(lam_prod, 2)
            f(nc.scalar.activation(lam[:, 0:2], lam[:, 0:2], ACT.Exp), lam_exp)
            group_roots(f, act, ss, todo, mean_done, root_done)

        elementwise(qk_dve, qk_act,
                    loads=[(bg[:, 0, :], bcast(I["l0_b_qnorm"])), (bg[:, 1, :], bcast(I["l0_b_knorm"])),
                           (mg[:, :], bcast(I["l0_m_qnorm"])),
                           (rp[:, :, :], I["rope4"].rearrange("(t p) c -> p t c", p=P))] +
                          [(lamv[:, i, :], bcast(I[f"l0_b_{x}"])) for i, x in enumerate(("lq1", "lk1", "lq2", "lk2"))])
    else:
        stage()
    transpose_all([(T[:, b, t * P:(t + 1) * P], P0[:, t, c0 + b * P:c0 + (b + 1) * P])
                   for T, c0, nb in ((QT, 1536, 4), (KT, 2048, 4), (MQT, 3584, 2)) for b in range(nb) for t in range(NT)])
    units = []
    for h in range(B_HEADS):
        for m in range(2):
            for t in range(NT):
                g = 2 * h + m
                r = slice(32 * (g % 4), 32 * (g % 4) + 32)
                nk = (t + 1) * P
                units.append(dict(qT=QT[r, g // 4, t * P:(t + 1) * P], kT=KT[r, g // 4, 0:nk], nk=nk,
                                  v=[P0[:, k, 2560 + h * B_DV:2560 + (h + 1) * B_DV] for k in range(t + 1)],
                                  scale=B_DK ** -0.5, mask=causal[:, S - nk:S], coef=lam[:, 2:3] if m else None,
                                  out=mix[:, t, 512 + h * B_DV:512 + (h + 1) * B_DV], add=bool(m), guard=False))
    attention(units + memory_units(0, MQT, mix[:, :, 1024:1280]))
    subln = zone("b_subln", [P, B_DV])
    sn = [mix[:, t, 512:1024].rearrange("p (h d) -> p h d", d=B_DV) for t in range(NT)]

    def after_b(f, dve):
        for t in range(NT):
            f(nc.vector.scalar_tensor_tensor(mix[:, t, 512:1024], mix[:, t, 512:1024], 1.0 - LAM_INIT,
                                             P0[:, t, 3072:3584], ALU.mult, ALU.mult), wait=False)
            f(nc.vector.tensor_tensor(mix[:, t, 1024:1280], mix[:, t, 1024:1280], P0[:, t, 3840:4096], ALU.mult))

    norm_stage([(v, v, subln[:, :], B_DV) for v in sn], loads=[(subln[:, :], bcast(I["l0_b_subln"]))], after=after_b)
    mixt = P0[:, :, :].rearrange("p a b -> p (a b)")[:, 0:KMIX * S].rearrange("p (k s) -> p k s", k=KMIX)
    transpose_all([(mixt[:, k, t * P:(t + 1) * P], mix[:, t, k * P:(k + 1) * P]) for k in range(KMIX) for t in range(NT)])
    out_project("even_out", KMIX, mixt, mod_steps=8)


    norm_transpose(X, HT, [(HT, C("l1_norm", 0, 8), None)])
    zone.at = keep_first
    ss = zone("sums", [P, 3, 80])
    P1 = zone("odd_in", [P, NT, ODD_IN])
    mix = zone("mix", [P, NT, MIX])
    mark1 = zone.at
    PAD = C_KERNEL - 1
    CT = zone("conv_in_t", [P, C_BLOCKS, PAD + S])
    CY = zone("conv_out_t", [P, C_BLOCKS, S])
    odd_owner = ranges_owner(ODD_RANGES, ODD_IN)
    glu_done, glu_turned, conv_ready = sem("glu_done"), sem("glu_turned"), sem("conv_input")
    odd_g0 = first_group[pn["odd_in"][0]]
    taps = [(k, b) for k in range(C_KERNEL) for b in range(C_BLOCKS)]
    GLU_AT, TURN_AT, CONV_AT = 4, 5, 7
    CHUNKS = NT * len(pn["odd_in"])

    def glu_and_conv(f, dve, j):
        if j == GLU_AT:
            dve.wait_ge(acc_free["a"], owners[:odd_g0 + 2 * NT].count("a"))
            dve.wait_ge(acc_free["v"], owners[:odd_g0 + NT].count("v"))
            f(nc.vector.memset(CT[:, :, 0:PAD], 0.0), wait=False)
            for t in range(NT):
                f(nc.vector.tensor_tensor(P1[:, t, 0:512], P1[:, t, 0:512], P1[:, t, 512:1024], ALU.mult), glu_done, wait=False)
        if j == TURN_AT + 1:
            for t in range(NT):
                dve.wait_ge(glu_turned, t + 1)
                f(nc.vector.tensor_copy(CT[:, :, PAD + t * P:PAD + (t + 1) * P],
                                        banks[6 + t][:, :].rearrange("p (b c) -> p b c", b=C_BLOCKS)))
        if j >= CONV_AT:
            n = CHUNKS - CONV_AT
            lo, hi = (len(taps) * (j - CONV_AT + x) // n for x in range(2))
            for k, b in taps[lo:hi]:
                w = C("l1_c_conv_w", C_BLOCKS * k + b)
                if b == 0:
                    dve.wait_ge(dve_order, counts[dve_order.num])
                if k == 0:
                    ins = nc.vector.tensor_scalar(CY[:, b, :], CT[:, b, 0:S], w, C("l1_c_conv_b", b), ALU.mult, ALU.add)
                else:
                    ins = nc.vector.scalar_tensor_tensor(CY[:, b, :], CT[:, b, k:k + S], w, CY[:, b, :],
                                                         ALU.mult, ALU.add)
                f(ins, wait=False)

    def glu_transposes(pe, j):
        if j == TURN_AT:
            for t in range(NT):
                pe.wait_ge(glu_done, t + 1)
                for b in range(C_BLOCKS):
                    last = nc.tensor.transpose(banks[6 + t][:, b * P:(b + 1) * P], P1[:, t, b * P:(b + 1) * P], ident[:, :])
                last.then_inc(glu_turned, 1)

    project("odd_in", ht, ranges_evac(P1, ODD_RANGES, ODD_IN), odd_owner, width=ODD_IN, mod_steps=1,
            beside=dict(dve=glu_and_conv, pe=glu_transposes))
    CN = zone("conv_out", [P, NT, 512])
    sq = zone("squares", [P, D])
    cgain = zone("c_norm", [P, 512])
    transpose_all([(CN[:, t, b * P:(b + 1) * P], CY[:, b, t * P:(t + 1) * P])
                   for b in range(C_BLOCKS) for t in range(NT)])
    norm_stage([(CN[:, t, :].unsqueeze(1), CN[:, t, :].unsqueeze(1), cgain[:, :], 512) for t in range(NT)],
               loads=[(cgain[:, :], bcast(I["l1_c_norm"]))])
    if Stage.count < upto:
        c_silu = sem("c_silu")

        def c_act(f, act):
            f(nc.scalar.activation(CN[:, :, :], CN[:, :, :], ACT.Silu), c_silu)

        def c_dve(f, dve):
            dve.wait_ge(c_silu, 1)
            f(nc.vector.tensor_tensor(mix[:, :, 0:512], CN[:, :, :], P1[:, :, 1024:1536], ALU.mult))
        elementwise(c_dve, c_act)
    else:
        stage()
    zone.at = mark1

    sq = zone("squares", [P, D])
    dg = zone("d_gains", [P, 2, HD])
    mg = zone("m_qgain", [P, HD])
    rp = zone("rope8", [P, NT, 16])
    rc = zone("rope_cmp", [P, 16])
    twice = [HT[:, :, :].rearrange("p k s -> p (k s)")[:, n * 1024:(n + 1) * 1024]
             .rearrange("p (t i g a d) -> p t i g a d", t=NT, i=2, g=D_GROUPS, a=2) for n in range(2)]
    KDUP, RAW2 = twice
    DQT = zone("d_q_t", [P, 4, S])
    KDT = zone("d_k_t", [P, 2, D_GROUPS, S])
    RT = zone("cmp_raw_t", [P, 2, D_GROUPS, S])
    MQT = zone("m_q_t", [P, 2, S])
    posr = zone("cmp_pos", [CMP_K, 2, P])
    POST = zone("cmp_pos_t", [P, 2, CMP_K])
    OP = zone("cmp_operand", [P, 2, CMP_K, D_GROUPS, N_CMP])
    HID = zone("cmp_hidden", [P, 2, D_GROUPS, N_CMP])
    W2 = zone("cmp_w2", [P, 2, HD])
    KC = zone("k_cmp", [N_CMP, 2, D_GROUPS, HD])
    KCD = zone("k_cmp_twice", [N_CMP, D_GROUPS, 2, HD])
    KCT = zone("k_cmp_t", [P, D_GROUPS, N_CMP])

    heads = lambda t, a, b: P1[:, t, a:b].rearrange("p (g d) -> p g d", d=HD)
    K_SLC, K_WIN = 2304, 2560
    todo = []
    for t in range(NT):
        for a, b, g in ((1536, 2048, dg[:, 0, :]), (K_SLC, K_SLC + P, dg[:, 1, :]), (K_WIN, K_WIN + P, dg[:, 1, :]),
                        (3352, 3608, mg[:, :])):
            todo.append((heads(t, a, b), heads(t, a, b), g, HD))

    def rotate(f, dve):
        for t in range(NT):
            for a, b in ((1536, 2048), (K_SLC, K_SLC + P), (K_WIN, K_WIN + P)):
                rope(f, heads(t, a, b), rp[:, t, 0:8], rp[:, t, 8:16], 8, sq)
            for i, a in enumerate((K_SLC, K_WIN)):
                f(nc.vector.tensor_copy(KDUP[:, t, i, :, :, :],
                                        heads(t, a, a + P).unsqueeze(2).broadcast_to([P, D_GROUPS, 2, HD])), wait=False)
            for i in range(2):
                a = 2048 + i * P
                f(nc.vector.tensor_copy(RAW2[:, t, i, :, :, :],
                                        heads(t, a, a + P).unsqueeze(2).broadcast_to([P, D_GROUPS, 2, HD])), wait=False)

    norm_stage(todo, loads=[(dg[:, 0, :], bcast(I["l1_d_qnorm"])), (dg[:, 1, :], bcast(I["l1_d_knorm"])),
                            (mg[:, :], bcast(I["l1_m_qnorm"])),
                            (rp[:, :, :], I["rope8"].rearrange("(t p) c -> p t c", p=P)),
                            (rc[0:N_CMP, :], I["ropec"])] +
               [(posr[:, i, :], I[f"l1_d_cmp_pos_{x}"].rearrange("(k s) d -> k (s d)", s=2)) for i, x in enumerate("kv")] +
               [(W2[:, i, :], I[f"l1_d_cmp_w2_{x}"]) for i, x in enumerate("kv")], after=rotate)
    transpose_all([(DQT[:, b, t * P:(t + 1) * P], P1[:, t, 1536 + b * P:1536 + (b + 1) * P])
                   for b in range(4) for t in range(NT)] +
                  [(KDT[:, i, g, t * P:(t + 1) * P], KDUP[:, t, i, g].rearrange("p a d -> p (a d)"))
                   for i in range(2) for g in range(D_GROUPS) for t in range(NT)] +
                  [(RT[:, i, g, t * P:(t + 1) * P], RAW2[:, t, i, g].rearrange("p a d -> p (a d)"))
                   for i in range(2) for g in range(D_GROUPS) for t in range(NT)] +
                  [(MQT[:, b, t * P:(t + 1) * P], P1[:, t, 3352 + b * P:3352 + (b + 1) * P])
                   for b in range(2) for t in range(NT)] +
                  [(POST[:, i, :], posr[:, i, :]) for i in range(2)])

    if Stage.count < upto:
        operand_ready, cmp_done = sem("cmp_operand_ready"), sem("cmp_done")
        g0 = first_group[pn["cmp"][0]]
        owners.extend("aa")

        def cmp_dve(f, dve):
            span = CMP_STRIDE * (N_CMP - 1) + 1
            for i in range(2):
                for k in range(CMP_K):
                    for odd in range(2):
                        r = slice(HD * odd, HD * odd + HD)
                        first = 2 * k + odd
                        f(nc.vector.tensor_scalar(OP[r, i, k, :, :], RT[r, i, :, first:first + span:CMP_STRIDE],
                                                  POST[r, i, k:k + 1], None, ALU.add), operand_ready, wait=False)
            dve.wait_ge(cmp_done, 1)
            f(nc.vector.tensor_copy(KC[:, :, :, :].rearrange("p a g d -> p (a g d)"),
                                    acc_bank(g0)[0:N_CMP, 0:2 * D_GROUPS * HD]))

        def cmp_pe(f, pe):
            p = pn["cmp"][0]
            wait_panel(pe, p)
            n = D_GROUPS * N_CMP
            for i in range(2):
                w = slots[p % 3][:, i * CMP_K * P:(i + 1) * CMP_K * P].rearrange("p (k h) -> p k h", h=P)
                pe.wait_ge(operand_ready, (i + 1) * CMP_BLOCK)
                for k in range(CMP_K):
                    last = nc.tensor.matmul(banks[4 + i][:, 0:n], w[:, k, :],
                                            OP[:, i, k, :, :].rearrange("p g n -> p (g n)"),
                                            start=(k == 0), stop=(k == CMP_K - 1))
                last.then_inc(acc_ready, 1)
            pe.wait_ge(acc_free["a"], owners[:g0 + 2].count("a"))
            for i in range(2):
                for g in range(D_GROUPS):
                    c = (i * D_GROUPS + g) * HD
                    last = nc.tensor.matmul(acc_bank(g0)[0:N_CMP, c:c + HD], HID[:, i, g, :], W2[:, i, :],
                                            start=True, stop=True)
            last.then_inc(cmp_done, 1)

        def cmp_act(f, act):
            for i in range(2):
                act.wait_ge(acc_ready, g0 + i + 1)
                f(nc.scalar.activation(HID[:, i, :, :].rearrange("p g n -> p (g n)"),
                                       banks[4 + i][:, 0:D_GROUPS * N_CMP], ACT.Silu), acc_free["a"], wait=False)

        elementwise(cmp_dve, cmp_act, pe_body=cmp_pe, prefetch_to=pn["cmp"][-1] + 3)
    else:
        stage()
    kcv = KC[:, 0, :, :]

    def rotate_cmp(f, dve):
        rope(f, kcv, rc[0:N_CMP, 0:8], rc[0:N_CMP, 8:16], 8, sq)
        f(nc.vector.tensor_copy(KCD[:, :, :, :], kcv.unsqueeze(2).broadcast_to([N_CMP, D_GROUPS, 2, HD])))

    norm_stage([(kcv, kcv, dg[:, 1, :], HD)], after=rotate_cmp)
    transpose_all([(KCT[:, g, :], KCD[:, g, :, :].rearrange("p a d -> p (a d)")) for g in range(D_GROUPS)])
    units = []
    for h in range(D_HEADS):
        g = h // (D_HEADS // D_GROUPS)
        r = slice(64 * (h % 2), 64 * (h % 2) + 64)
        for t in range(NT):
            nk = (t + 1) * P
            same = dict(qT=DQT[r, h // 2, t * P:(t + 1) * P], scale=HD ** -0.5,
                        out=mix[:, t, 512 + h * HD:512 + (h + 1) * HD])
            gate = lambda j: P1[:, t, 2816 + 3 * h + j:2816 + 3 * h + j + 1]
            units.append(dict(same, kT=KCT[r, g, :], nk=N_CMP, v=[KC[:, 1, g, :]], mask=cmpmask[:, t, :],
                              coef=gate(0), add=False, guard=True))
            for j, (i, v0) in enumerate(((0, 2432), (1, 2688))):
                units.append(dict(same, kT=KDT[r, i, g, 0:nk], nk=nk,
                                  v=[P1[:, k, v0 + g * HD:v0 + (g + 1) * HD] for k in range(t + 1)],
                                  mask=causal[:, S - nk:S], coef=gate(1 + j), add=True, guard=False))
    attention(units + memory_units(1, MQT, mix[:, :, 1024:1280]))

    def gate_d(f, dve):
        for t in range(NT):
            f(nc.vector.tensor_tensor(mix[:, t, 512:1024], mix[:, t, 512:1024], P1[:, t, 2840:3352], ALU.mult), wait=False)
            f(nc.vector.tensor_tensor(mix[:, t, 1024:1280], mix[:, t, 1024:1280], P1[:, t, 3608:3864], ALU.mult), wait=False)

    elementwise(gate_d)
    mixt = P1[:, :, :].rearrange("p a b -> p (a b)")[:, 0:KMIX * S].rearrange("p (k s) -> p k s", k=KMIX)
    transpose_all([(mixt[:, k, t * P:(t + 1) * P], mix[:, t, k * P:(k + 1) * P]) for k in range(KMIX) for t in range(NT)])
    out_project("odd_out", KMIX, mixt, mod_steps=8)

    zone.at = WORK

    def mods(base):
        return [MOD[:, base + 8 * i:base + 8 * i + 8] for i in range(6)]

    def gain_stage(jobs, a, b):
        def body(f, dve):
            f(nc.vector.tensor_tensor(MOD[:, a:b], MOD[:, a:b], C("ada_b_2", a, b - a), ALU.add))
            for i, scale, gain in jobs:
                f(nc.vector.scalar_tensor_tensor(GM[:, i, :], scale, 1.0, gain, ALU.add, ALU.mult), wait=False)
        elementwise(body)

    def gate_row(cols):
        if not stage():
            return
        mark = zone.at
        diag = zone("gate_diag", [P, KD, P])
        ones = zone("ones", [P, P])
        n = Stage.count
        diag_ready, row_ready = sem(f"diag{n}_ready"), sem(f"row{n}_ready")
        with StageBlock() as block:
            @block.vector
            def _(dve):
                f = dve_f.on(dve)
                f(nc.vector.memset(ones[:, :], 1.0))
                f(nc.vector.tensor_tensor(diag[:, :, :], ident[:, :].unsqueeze(1).broadcast_to([P, KD, P]),
                                          cols.unsqueeze(2).broadcast_to([P, KD, P]), ALU.mult), diag_ready)
                for i in range(2):
                    dve.wait_ge(row_ready, i + 1)
                    f(nc.vector.tensor_copy(GROW[:, i * 512:(i + 1) * 512], banks[i][:, :]), wait=False)

            @block.tensor
            def _(pe):
                pe.wait_ge(diag_ready, 1)
                for i in range(2):
                    nc.tensor.matmul(banks[i][:, :], ones[:, :],
                                     diag[:, 4 * i:4 * i + 4, :].rearrange("p a b -> p (a b)"),
                                     start=True, stop=True).then_inc(row_ready, 1)
        zone.at = mark

    sh1, sc1, g1, sh2, sc2, g2 = mods(0)
    gain_stage([(0, sc1, C("norm_mix_g_2", 0, 8)), (1, sc2, C("norm_ffn_g_2", 0, 8))], 0, 48)
    norm_transpose(X, HT, [(HT, GM[:, 0, :], sh1)])

    LP = CONV_WIDTH - 1
    RC = zone("rec_in_t", [P, KD, LP + S])
    GT = zone("gate_t", [P, KD, S])
    XC = zone("conv_t", [P, KD, S])
    R = zone("r_t", [P, KD, S])
    IG = zone("i_t", [P, KD, S])
    A = zone("a_t", [P, KD, S])
    TH = zone("tanh_t", [P, KD, S])
    HS = zone("hs_t", [P, KD, S])
    SPL = zone("softplus", [P, 6, KD])

    def block_of(slot, K, b):
        return slot[:, 0:K * 512].rearrange("p (k n) -> p k n", k=K)[:, :, b * P:(b + 1) * P]

    def lru_evac(f, who, g, bank, free):
        if g < 4:
            f(nc.scalar.activation(GT[:, 2 * g:2 * g + 2, :].rearrange("p a b -> p (a b)"), bank[:, :], ACT.Gelu), free, wait=False)
        else:
            f(nc.vector.tensor_copy(RC[:, 2 * (g - 4):2 * (g - 4) + 2, LP:LP + S], bank[:, :].rearrange("p (a b) -> p a b", a=2)),
              free, wait=False)

    ht_all = lambda g, h, k: HT[:, k, :]
    panel_block = lambda slot, g, h, k: block_of(slot, KD, 2 * (g % 2) + h)[:, k, :]
    project_t("lru_in", panel_block, 8, KD, ht_all, lru_evac, lambda g: "a" if g < 4 else "v",
              mod_steps=6)

    if Stage.count < upto:
        exp_in, exp_out = sem("softplus_in"), sem("softplus_exp")

        def lru_conv(f, dve):
            f(nc.vector.memset(RC[:, :, 0:LP], 0.0))
            for k in range(CONV_WIDTH):
                for b in range(KD):
                    w = C("lru_conv_w_2", KD * k + b)
                    if k == 0:
                        ins = nc.vector.tensor_scalar(XC[:, b, :], RC[:, b, 0:S], w, C("lru_conv_b_2", b), ALU.mult, ALU.add)
                    else:
                        ins = nc.vector.scalar_tensor_tensor(XC[:, b, :], RC[:, b, k:k + S], w, XC[:, b, :],
                                                             ALU.mult, ALU.add)
                    f(ins, wait=(b == KD - 1))
            lamc = C("lru_lambda_2", 0, 8)
            v = [SPL[:, i, :] for i in range(6)]
            f(nc.vector.tensor_scalar(v[1], lamc, -1.0, None, ALU.mult))
            f(nc.vector.tensor_tensor(v[2], v[1], lamc, ALU.min), exp_in)
            dve.wait_ge(exp_out, 1)
            f(nc.vector.tensor_scalar(v[3], v[2], 2.0, None, ALU.add))
            f(nc.vector.reciprocal(v[3], v[3]))
            f(nc.vector.tensor_tensor(v[2], v[2], v[3], ALU.mult))
            f(nc.vector.tensor_tensor(v[3], v[2], v[2], ALU.mult))
            f(nc.vector.memset(v[4], 1.0 / 19))
            for n in range(17, 0, -2):
                f(nc.vector.tensor_tensor(v[4], v[4], v[3], ALU.mult))
                f(nc.vector.tensor_scalar(v[4], v[4], 1.0 / n, None, ALU.add))
            f(nc.vector.tensor_tensor(v[4], v[4], v[2], ALU.mult))
            f(nc.vector.tensor_scalar(v[1], v[1], 0.0, None, ALU.max))
            f(nc.vector.scalar_tensor_tensor(v[0], v[4], 2.0, v[1], ALU.mult, ALU.add))
            f(nc.vector.tensor_scalar(v[0], v[0], -8.0, None, ALU.mult))

        def lru_exp(f, act):
            act.wait_ge(exp_in, 1)
            f(nc.scalar.activation(SPL[:, 2, :], SPL[:, 2, :], ACT.Exp), exp_out)
        elementwise(lru_conv, lru_exp)
    else:
        stage()

    def gates_evac(f, who, g, bank, free):
        dst, name, h = (R, "lru_ba_2", g) if g < 4 else (IG, "lru_bx_2", g - 4)
        for j in range(2):
            f(nc.scalar.activation(dst[:, 2 * h + j, :], bank[:, j * S:(j + 1) * S], ACT.Sigmoid,
                                   bias=C(name, 2 * h + j)), free if j else None, wait=False)

    project_t("lru_gates",
              lambda slot, g, h, k: slot[:, 2048 * (g // 4):2048 * (g // 4) + 2048].rearrange("p (h n) -> p h n", h=8)
              [:, 2 * (g % 4) + k, h * P:(h + 1) * P], 8, 2,
              lambda g, h, k: XC[:, 2 * (g % 4) + k, :], gates_evac, lambda g: "a")
    if Stage.count < upto:
        la_ready, a_ready, th_ready, m_ready, root_ready = (sem(f"lru_{x}") for x in ("la", "a", "tanh", "mult", "root"))

        def scan_dve(f, dve):
            for b in range(KD):
                f(nc.vector.tensor_scalar(R[:, b, :], R[:, b, :], SPL[:, 0, b:b + 1], None, ALU.mult), wait=(b == KD - 1))
            f(nc.vector.memset(SPL[:, 1, :], 0.0), la_ready)
            f(nc.vector.tensor_tensor(IG[:, :, :], IG[:, :, :], XC[:, :, :], ALU.mult))
            dve.wait_ge(th_ready, 1)
            f(nc.vector.tensor_tensor(R[:, :, :], A[:, :, :], A[:, :, :], ALU.mult))
            f(nc.vector.scalar_tensor_tensor(TH[:, :, :], R[:, :, :], 1.0, TH[:, :, :], ALU.add, ALU.mult), m_ready)
            dve.wait_ge(root_ready, 1)
            f(nc.vector.tensor_tensor(TH[:, :, :], TH[:, :, :], IG[:, :, :], ALU.mult))
            for b in range(KD):
                f(nc.vector.tensor_tensor_scan(HS[:, b, :], A[:, b, :], TH[:, b, :], 0.0, ALU.mult, ALU.add),
                  wait=(b == KD - 1))
            f(nc.vector.tensor_tensor(HS[:, :, :], HS[:, :, :], GT[:, :, :], ALU.mult))

        def scan_act(f, act):
            act.wait_ge(la_ready, 1)
            f(nc.scalar.activation(A[:, :, :], R[:, :, :], ACT.Exp), a_ready)
            f(nc.scalar.activation(TH[:, :, :], R[:, :, :], ACT.Tanh), th_ready)
            act.wait_ge(m_ready, 1)
            f(nc.scalar.activation(TH[:, :, :], TH[:, :, :], ACT.Sqrt, scale=-1.0), root_ready)
        elementwise(scan_dve, scan_act)
    else:
        stage()
    gate_row(g1)
    out_project("lru_out", KD, HS, gate=(GROW, TMP), mod_steps=8)

    def peer(l, q_name, gain, shift, gate_cols):
        norm_transpose(X, HT, [(HT, gain, shift)])
        zone.at = WORK
        zone.limit = WORK_END - SLOT
        H = PEER_HEADS
        QT = zone("peer_q_t", [P, 2, 2, S])
        SK = zone("sub_keys", [P, 2 * H, P])
        SKT = zone("sub_keys_t", [P, 2 * H, P])
        SC = zone("key_scores", [P, 2, 2, NT, N_KEYS])
        VAL = zone("key_values", [P, H, 2, NT, TOPK])
        IDX = zone("key_index", [P, H, 2, NT, TOPK], U32)
        IDF = zone("key_index_f", [P, H, 2, NT, TOPK])
        CAND = zone("candidates", [P, 2, NT, TOPK * TOPK])
        CV = zone("cand_values", [P, H, NT, TOPK])
        CI = zone("cand_index", [P, H, NT, TOPK], U32)
        C12 = zone("cand_pair", [P, H, 2, NT * TOPK], U32)
        C12F = zone("cand_pair_f", [P, H, 2, NT * TOPK])
        EQ = zone("pick", [P, H, 2 * NT * TOPK, TOPK])
        EN = zone("expert_keys", [P, 3, NT, SLOTS])
        SUM = zone("gate_sums", [P, NT * H])

        if stage():
            ps = pn[q_name]
            g0 = first_group[ps[0]]
            owners.extend("a" for _ in range(H))
            keys_loaded = small[0] + 16
            keys_turned, keys_t, scored, sc_ready, keys_done, decode_in, decoded, exp_in, exp_out = (
                sem(f"peer{l}_{x}") for x in ("keys_turned", "keys_t", "scored", "scores_copied", "keys_done", "pairs",
                                              "decoded", "shifted", "exped"))
            with StageBlock() as block:
                @block.sync
                def _(sp):
                    load_small(sp, [(SK[:, :, :], I["peer_sub_keys_2"][l].rearrange("h p n d -> n (h p) d"))])
                    for h in range(H):
                        load_panels(sp, min(ps[h // 2] + 3, ps[-1]))

                @block.tensor
                def _(pe):
                    for h in range(H + 1):
                        if h < H:
                            p = ps[h // 2]
                            wait_panel(pe, p)
                            wait_acc_free(pe, g0 + h)
                            for half in range(2):
                                for k in range(KD):
                                    last = nc.tensor.matmul(acc_bank(g0 + h)[:, half * S:(half + 1) * S],
                                                            panel_block(slots[p % 3], h, half, k), HT[:, k, :],
                                                            start=(k == 0), stop=(k == KD - 1))
                            last.then_inc(acc_ready, 1)
                        if h == 0:
                            pe.wait_ge(small_loaded, keys_loaded)
                            for j in range(2 * H):
                                last = nc.tensor.transpose(banks[4 + j // 4][:, (j % 4) * P:(j % 4 + 1) * P], SK[:, j, :],
                                                           ident[:, :])
                                if j % 4 == 3:
                                    last.then_inc(keys_turned, 1)
                        if h >= 1:
                            g = h - 1
                            pe.wait_ge(keys_t, 4)
                            pe.wait_ge(acc_free["a"], owners[:g0 + g + 1].count("a"))
                            if g >= 2:
                                pe.wait_ge(sc_ready, g - 1)
                            for i in range(2):
                                for t in range(NT):
                                    c = (i * NT + t) * P
                                    last = nc.tensor.matmul(banks[4 + g % 2][:, c:c + P], QT[:, g % 2, i, t * P:(t + 1) * P],
                                                            SKT[:, 2 * g + i, :], start=True, stop=True)
                            last.then_inc(scored, 1)

                @block.scalar
                def _(act):
                    f = act_f.on(act)
                    for h in range(H + 1):
                        if h < H:
                            act.wait_ge(acc_ready, g0 + h + 1)
                            if h >= 2:
                                act.wait_ge(scored, h - 1)
                            f(nc.scalar.activation(QT[:, h % 2, :, :].rearrange("p a b -> p (a b)"),
                                                   acc_bank(g0 + h)[:, :], ACT.Copy), acc_free["a"], wait=False)
                        if h == 0:
                            for j in range(4):
                                act.wait_ge(keys_turned, j + 1)
                                nc.scalar.activation(SKT[:, 4 * j:4 * j + 4, :].rearrange("p a b -> p (a b)"),
                                                     banks[4 + j][:, :], ACT.Copy).then_inc(keys_t, 1)
                        if h >= 1:
                            g = h - 1
                            act.wait_ge(scored, g + 1)
                            if g >= 2:
                                act.wait_ge(keys_done, g - 1)
                            nc.scalar.activation(SC[:, g % 2, :, :, :].rearrange("p i t n -> p (i t n)"),
                                                 banks[4 + g % 2][:, :], ACT.Copy).then_inc(sc_ready, 1)
                    act.wait_ge(exp_in, 1)
                    gates = EN[:, 2, :, :].rearrange("p t s -> p (t s)")
                    f(nc.scalar.activation(gates, gates, ACT.Exp), exp_out)

                @block.gpsimd
                def _(pool):
                    f = pool_f.on(pool)
                    for h in range(H):
                        pool.wait_ge(decode_in, h + 1)
                        eq = EQ[:, h, :, :].rearrange("p (a k) j -> p a k j", k=TOPK)
                        f(nc.gpsimd.tensor_tensor(eq, eq, IDF[:, h, :, :, :].rearrange("p i t j -> p (i t) j").unsqueeze(2)
                                                  .broadcast_to([P, 2 * NT, TOPK, TOPK]), ALU.mult), decoded)

                @block.vector
                def _(dve):
                    f = dve_f.on(dve)
                    v = nc.vector
                    rows = [(i, t) for i in range(2) for t in range(NT)]

                    def sum_up(h):
                        f(v.tensor_reduce(EN[:, 0:2, :, h * TOPK:(h + 1) * TOPK].rearrange("p i t k -> p (i t) k"),
                                          EQ[:, h, :, :].rearrange("p (a k) j -> p a k j", k=TOPK), AX.X, ALU.add), wait=False)

                    def settle():
                        dve.wait_ge(dve_order, counts[dve_order.num])

                    for h in range(H + 2):
                        keys, cand, pairs = h < H, 1 <= h <= H, h >= 2
                        g, e = h - 1, h - 2
                        if keys:
                            dve.wait_ge(sc_ready, h + 1)
                            ks = [(SC[:, h % 2, i, t, :], VAL[:, h, i, t, :], IDX[:, h, i, t, :]) for i, t in rows]
                        if cand:
                            cs = [(CAND[:, g % 2, t, :], CV[:, g, t, :], CI[:, g, t, :]) for t in range(NT)]
                            for t in range(NT):
                                a = VAL[:, g, 0, t, :].unsqueeze(2).broadcast_to([P, TOPK, TOPK])
                                b = VAL[:, g, 1, t, :].unsqueeze(1).broadcast_to([P, TOPK, TOPK])
                                f(v.tensor_tensor(cs[t][0].rearrange("p (a b) -> p a b", a=TOPK), a, b, ALU.add), wait=False)
                        if keys:
                            for sc, val, idx in ks:
                                f(v.max(val[:, 0:8], sc), wait=False)
                        if pairs:
                            ci = CI[:, e, :, :].rearrange("p t k -> p (t k)")
                            f(v.tensor_scalar(C12[:, e, 0, :], ci, 4, None, ALU.logical_shift_right), wait=False)
                            f(v.tensor_scalar(C12[:, e, 1, :], ci, 15, None, ALU.bitwise_and), wait=False)
                        settle()
                        if cand:
                            for sc, val, idx in cs:
                                f(v.max(val[:, 0:8], sc), wait=False)
                        if keys:
                            for sc, val, idx in ks:
                                f(v.max_index(idx[:, 0:8], val[:, 0:8], sc), wait=False)
                        if pairs:
                            f(v.tensor_copy(C12F[:, e, :, :].rearrange("p i s -> p (i s)"),
                                            C12[:, e, :, :].rearrange("p i s -> p (i s)")), wait=False)
                        settle()
                        if cand:
                            for sc, val, idx in cs:
                                f(v.max_index(idx[:, 0:8], val[:, 0:8], sc), wait=False)
                        if keys:
                            for sc, val, idx in ks:
                                f(v.match_replace(sc, val[:, 0:8], sc, -3e38), wait=False)
                        if pairs:
                            n = 2 * NT * TOPK
                            v.tensor_tensor(EQ[:, e, :, :], C12F[:, e, :, :].rearrange("p i s -> p (i s)").unsqueeze(2)
                                            .broadcast_to([P, n, TOPK]),
                                            iota[:, 0:TOPK].unsqueeze(1).broadcast_to([P, n, TOPK]),
                                            ALU.is_equal).then_inc(decode_in, 1)
                        settle()
                        if cand:
                            for sc, val, idx in cs:
                                f(v.match_replace(sc, val[:, 0:8], sc, -3e38), wait=False)
                        if keys:
                            for sc, val, idx in ks:
                                f(v.max(val[:, 8:16], sc), wait=False)
                        settle()
                        if cand:
                            for sc, val, idx in cs:
                                f(v.max(val[:, 8:16], sc), wait=False)
                        if keys:
                            for sc, val, idx in ks[:-1]:
                                f(v.max_index(idx[:, 8:16], val[:, 8:16], sc), wait=False)
                            sc, val, idx = ks[-1]
                            v.max_index(idx[:, 8:16], val[:, 8:16], sc).then_inc(keys_done, 1)
                            dve.wait_ge(keys_done, h + 1)
                        settle()
                        if cand:
                            for sc, val, idx in cs:
                                f(v.max_index(idx[:, 8:16], val[:, 8:16], sc), wait=False)
                        if keys:
                            f(v.tensor_copy(IDF[:, h, :, :, :].rearrange("p i t k -> p (i t k)"),
                                            IDX[:, h, :, :, :].rearrange("p i t k -> p (i t k)")), wait=False)
                        if h >= 4:
                            dve.wait_ge(decoded, h - 3)
                            sum_up(h - 4)
                        settle()
                    th = NT * H
                    for t in range(NT):
                        f(v.tensor_tensor(EN[:, 2, t, :].rearrange("p (h k) -> p h k", h=H), CV[:, :, t, :],
                                          CV[:, :, t, 0:1].broadcast_to([P, H, TOPK]), ALU.subtract),
                          exp_in if t == NT - 1 else None)
                    for h in range(H - 2, H):
                        dve.wait_ge(decoded, h + 1)
                        sum_up(h)
                    gw = EN[:, 2, :, :].rearrange("p t (h k) -> p (t h) k", h=H)
                    dve.wait_ge(exp_out, 1)
                    f(v.tensor_reduce(SUM[:, :], gw, AX.X, ALU.add))
                    f(v.reciprocal(SUM[:, :], SUM[:, :]))
                    f(v.tensor_tensor(gw, gw, SUM[:, :].unsqueeze(2).broadcast_to([P, th, TOPK]), ALU.mult))

        transpose_all([(dst[:, t * P:(t + 1) * P], EN[:, i, t, :])
                       for i, dst in enumerate((slot_e1, slot_e2, slot_g)) for t in range(NT)])

        G = nc.alloc_sbuf_tensor_at(f"gates{l}", [P, N_KEYS, S], F32, offset=WORK)
        R4 = 4
        O1 = nc.alloc_sbuf_tensor_at(f"onehot1_{l}", [P, R4, 4, P], F32, offset=PANELS)
        O2 = nc.alloc_sbuf_tensor_at(f"onehot2_{l}", [P, R4, 4, P], F32, offset=PANELS + R4 * 2048)
        if stage():
            hot, built, stored = sem(f"peer{l}_onehots"), sem(f"peer{l}_built"), sem(f"peer{l}_stored")
            high, plain, gated = sem(f"peer{l}_h_high"), sem(f"peer{l}_plain_onehots"), sem(f"peer{l}_gated")
            ACT_TOKENS = 2

            def at_least(eng, s, value):
                if type(value) is not int or value > 0:
                    eng.wait_ge(s, value)

            with StageBlock() as block:
                @block.vector
                def _(dve):
                    dve.wait_ge(high, 1)
                    nc.vector.tensor_tensor(HTL[:, :, :], HT[:, :, :], HTH[:, :, :].bitcast(F32), ALU.subtract)\
                        .then_inc(dve_order, 1)
                    counts[dve_order.num] += 1

                    def step(n, s):
                        at_least(dve, built, n - R4 + 1)
                        tok = slice(4 * n, 4 * n + 4) if type(n) is int else bass.ds(4 * n, 4)
                        rows = iota[:, :].unsqueeze(1)
                        nc.vector.tensor_tensor(O2[:, s, :, :], rows.broadcast_to([P, 4, P]),
                                                slot_e2[:, tok].unsqueeze(2).broadcast_to([P, 4, P]), ALU.is_equal)
                        tok = slice(4 * n, 4 * n + ACT_TOKENS) if type(n) is int else bass.ds(4 * n, ACT_TOKENS)
                        nc.vector.tensor_tensor(O1[:, s, 0:ACT_TOKENS, :], rows.broadcast_to([P, ACT_TOKENS, P]),
                                                slot_e1[:, tok].unsqueeze(2).broadcast_to([P, ACT_TOKENS, P]),
                                                ALU.is_equal).then_inc(plain, 1)
                        for u in range(ACT_TOKENS, 4):
                            tok = slice(4 * n + u, 4 * n + u + 1) if type(n) is int else bass.ds(4 * n + u, 1)
                            last = nc.vector.tensor_scalar(O1[:, s, u, :], iota[:, :], slot_e1[:, tok], slot_g[:, tok],
                                                           ALU.is_equal, ALU.mult)
                        last.then_inc(hot, 1)
                    for s in range(R4):
                        step(s, s)
                    with dve.Fori(1, S // 16) as i:
                        for s in range(R4):
                            step(R4 * i + s, s)

                @block.tensor
                def _(pe):
                    def step(n, s):
                        pe.wait_ge(hot, n + 1)
                        pe.wait_ge(gated, n + 1)
                        at_least(pe, stored, n - R4 + 1)
                        for u in range(4):
                            last = nc.tensor.matmul(banks[s][:, u * P:(u + 1) * P], O2[:, s, u, :], O1[:, s, u, :],
                                                    start=True, stop=True)
                        last.then_inc(built, 1)
                    for s in range(R4):
                        step(s, s)
                    with pe.Fori(1, S // 16) as i:
                        for s in range(R4):
                            step(R4 * i + s, s)

                @block.scalar
                def _(act):
                    nc.scalar.activation(HTH[:, :, :], HT[:, :, :], ACT.Copy).then_inc(high, 1)

                    def gate(n, s):
                        act.wait_ge(plain, n + 1)
                        for u in range(ACT_TOKENS):
                            tok = slice(4 * n + u, 4 * n + u + 1) if type(n) is int else bass.ds(4 * n + u, 1)
                            last = nc.scalar.activation(O1[:, s, u, :], O1[:, s, u, :], ACT.Copy, scale=slot_g[:, tok])
                        last.then_inc(gated, 1)

                    def store(n, s):
                        act.wait_ge(built, n + 1)
                        tok = slice(4 * n, 4 * n + 4) if type(n) is int else bass.ds(4 * n, 4)
                        nc.scalar.activation(G[:, :, tok], banks[s][:, :].rearrange("p (t e) -> p e t", t=4), ACT.Copy)\
                            .then_inc(stored, 1)

                    gate(0, 0)
                    for s in range(1, R4):
                        gate(s, s)
                        store(s - 1, s - 1)
                    with act.Fori(1, S // 16) as i:
                        for s in range(R4):
                            gate(R4 * i + s, s)
                            store(R4 * i + s - 1, (s - 1) % R4)
                    store(S // 4 - 1, R4 - 1)

        NB = N_KEYS
        o = RINGS

        def ring(name, shape, dt=F32):
            nonlocal o
            t = nc.alloc_sbuf_tensor_at(f"{name}{l}", [P] + shape, dt, offset=o)
            o += int(np.prod(shape)) * 4
            assert o <= WORK
            return t

        UTH, UTL = ring("u_t_high", [2, KD, P], F32R), ring("u_t_low", [2, KD, P], F32R)
        VH, VL = ring("v_high", [2, D], F32R), ring("v_low", [2, D], F32R)
        UR, VR = ring("u_ring", [2, D]), ring("v_ring", [2, D])
        AA = ring("activated", [2, S])
        WH, WL = ring("weighted_high", [S], F32R), ring("weighted_low", [S], F32R)
        if stage():
            u_loaded = [sem(f"peer{l}_u_loaded{i}") for i in range(2)]
            v_loaded = [sem(f"peer{l}_v_loaded{i}") for i in range(2)]
            turned, ut_high, ut_low, v_high, v_low, acted, gelued, w_full, w_high, weighted, applied, cleared_acc, zeroed = (
                sem(f"peer{l}_{x}") for x in ("turned", "ut_high", "ut_low", "v_high", "v_low", "acted", "gelued", "w_full",
                                              "w_high", "weighted", "applied", "cleared", "zeroed"))
            u_dram, v_dram = I["peer_u_2"][l], I["peer_v_2"][l]

            def rows(b):
                return slice(b * P, (b + 1) * P) if type(b) is int else bass.ds(b * P, P)

            with StageBlock() as block:
                @block.sync
                def _(sp):
                    def step(b, k):
                        at_least(sp, turned, 2 * b - 2)
                        sp.dma_start(UR[:, k, :], u_dram[rows(b), :]).then_inc(u_loaded[k], 16)
                        at_least(sp, v_low, b - 1)
                        sp.dma_start(VR[:, k, :], v_dram[rows(b), :]).then_inc(v_loaded[k], 16)
                    for k in range(2):
                        step(k, k)
                    with sp.Fori(1, NB // 2) as i:
                        for k in range(2):
                            step(2 * i + k, k)

                @block.tensor
                def _(pe):
                    def turn(b, k, lap):
                        pe.wait_ge(u_loaded[k], 16 * lap + 16)
                        for half in range(2):
                            at_least(pe, ut_low, 2 * b - 1 + half)
                            for j in range(4):
                                c = 4 * half + j
                                last = nc.tensor.transpose(banks[half][:, j * P:(j + 1) * P],
                                                           UR[:, k, c * P:(c + 1) * P], ident[:, :])
                            last.then_inc(turned, 1)

                    def act_on(b, k):
                        at_least(pe, gelued, b - 1)
                        pe.wait_ge(ut_low, 2 * b + 2)
                        for n, (u, h) in enumerate(((UTH, HTH), (UTH, HTL), (UTL, HTH))):
                            for j in range(KD):
                                last = nc.tensor.matmul(banks[2 + k][:, 0:S], u[:, k, j, :], h[:, j, :],
                                                        start=(n + j == 0), stop=(n == 2 and j == KD - 1))
                        last.then_inc(acted, 1)

                    def apply(b, k, final):
                        pe.wait_ge(v_low, b + 1)
                        pe.wait_ge(weighted, b + 1)
                        for t in range(NT):
                            for n, (w, v) in enumerate(((WH, VH), (WH, VL), (WL, VH))):
                                for half in range(2):
                                    last = nc.tensor.matmul(banks[4 + 2 * t + half][:, :], w[:, t * P:(t + 1) * P],
                                                            v[:, k, half * 512:(half + 1) * 512], start=False,
                                                            stop=final and n == 2, skip_group_check=True)
                        last.then_inc(applied, 1)

                    pe.wait_ge(zeroed, 1)
                    for i in range(4):
                        nc.tensor.matmul(banks[4 + i][:, :], WH[:, 0:P], HTH[:, 0:2, :].rearrange("p a b -> p (a b)"),
                                         start=True, stop=False, skip_group_check=True).then_inc(cleared_acc, 1)
                    turn(0, 0, 0)
                    turn(1, 1, 0)
                    act_on(0, 0)

                    def step(b, k, lap, turns=True, acts=True, final=False):
                        if turns:
                            turn(b + 2, k, lap + 1)
                        if acts:
                            act_on(b + 1, 1 - k)
                        apply(b, k, final)
                    for k in range(2):
                        step(k, k, 0)
                    with pe.Fori(1, NB // 2 - 1) as i:
                        for k in range(2):
                            step(2 * i + k, k, i)
                    for k in range(2):
                        step(NB - 2 + k, k, 0, turns=False, acts=k < 1, final=k == 1)

                def pipeline(eng, split_u, split_v, other, lap_of=lambda i: i):
                    split_u(0, 0)
                    split_u(1, 1)
                    split_v(0, 0, 0)
                    other(0, 0)

                    def step(b, k, lap, turns=True, others=True):
                        if turns:
                            split_u(b + 2, k)
                        if others:
                            split_v(b + 1, 1 - k, lap + k)
                            other(b + 1, 1 - k)
                    for k in range(2):
                        step(k, k, 0)
                    with eng.Fori(1, NB // 2 - 1) as i:
                        for k in range(2):
                            step(2 * i + k, k, i)
                    for k in range(2):
                        step(NB - 2 + k, k, NB // 2 - 1, turns=False, others=k < 1)

                @block.scalar
                def _(act):
                    def split_u(b, s):
                        for half in range(2):
                            act.wait_ge(turned, 2 * b + 1 + half)
                            at_least(act, acted, b - 1)
                            nc.scalar.activation(UTH[:, s, 4 * half:4 * half + 4, :].rearrange("p a b -> p (a b)"),
                                                 banks[half][:, :], ACT.Copy).then_inc(ut_high, 1)

                    def split_v(b, s, lap):
                        act.wait_ge(v_loaded[s], 16 * lap + 16)
                        at_least(act, applied, b - 1)
                        nc.scalar.activation(VH[:, s, :], VR[:, s, :], ACT.Copy).then_inc(v_high, 1)

                    def gelu(b, s):
                        act.wait_ge(acted, b + 1)
                        at_least(act, weighted, b - 1)
                        nc.scalar.activation(AA[:, s, :], banks[2 + s][:, 0:S], ACT.Gelu).then_inc(gelued, 1)
                    pipeline(act, split_u, split_v, gelu)

                @block.vector
                def _(dve):
                    f = dve_f.on(dve)
                    f(nc.vector.memset(WH[:, 0:P].bitcast(F32), 0.0), zeroed)
                    dve.wait_ge(cleared_acc, 4)

                    def split_u(b, s):
                        for half in range(2):
                            dve.wait_ge(ut_high, 2 * b + 1 + half)
                            at_least(dve, acted, b - 1)
                            c = slice(4 * half, 4 * half + 4)
                            nc.vector.tensor_tensor(UTL[:, s, c, :].rearrange("p a b -> p (a b)"), banks[half][:, :],
                                                    UTH[:, s, c, :].rearrange("p a b -> p (a b)").bitcast(F32),
                                                    ALU.subtract).then_inc(ut_low, 1)

                    def split_v(b, s, lap):
                        dve.wait_ge(v_high, b + 1)
                        at_least(dve, applied, b - 1)
                        nc.vector.tensor_tensor(VL[:, s, :], VR[:, s, :], VH[:, s, :].bitcast(F32), ALU.subtract)\
                            .then_inc(v_low, 1)

                    def weigh(b, s):
                        dve.wait_ge(gelued, b + 1)
                        g = G[:, b, :] if type(b) is int else G[:, bass.ds(b, 1), :].rearrange("p a s -> p (a s)")
                        nc.vector.tensor_tensor(AA[:, s, :], AA[:, s, :], g, ALU.mult).then_inc(w_full, 1)
                        dve.wait_ge(w_full, b + 1)
                        at_least(dve, applied, b)
                        nc.vector.tensor_copy(WH[:, :], AA[:, s, :]).then_inc(w_high, 1)
                        dve.wait_ge(w_high, b + 1)
                        nc.vector.tensor_tensor(WL[:, :], AA[:, s, :], WH[:, :].bitcast(F32), ALU.subtract)\
                            .then_inc(weighted, 1)
                    pipeline(dve, split_u, split_v, weigh)
        zone.at = WORK
        gate_row(gate_cols)

        def add_experts(f, dve):
            for t in range(NT):
                for half in range(2):
                    c = slice(half * 512, (half + 1) * 512)
                    f(nc.vector.tensor_tensor(TMP[:, :], banks[4 + 2 * t + half][:, :], GROW[:, c], ALU.mult))
                    f(nc.vector.tensor_tensor(X[:, t, c], X[:, t, c], TMP[:, :], ALU.add))
        elementwise(add_experts)

    peer(0, "peer_q0", GM[:, 1, :], sh2, g2)

    assert modulation.reduced == len(mod_panels) or upto < 99
    sh1, sc1, g1, sh2, sc2, g2 = mods(48)
    gain_stage([(2, sc1, C("norm_mix_g_2", 8, 8)), (3, sc2, C("norm_ffn_g_2", 8, 8)),
                (4, MOD[:, 104:112], C("kv_norm_g_2", 0, 8))], 48, 112)
    HKV = zone("h_kv_t", [P, KD, S])
    norm_transpose(X, HT, [(HT, GM[:, 2, :], sh1), (HKV, GM[:, 4, :], MOD[:, 96:104])])
    DKV = zone("latent_kv", [P, NT, 288])
    DQ = zone("latent_q", [P, NT, Q_LORA])
    LT = zone("latent_kv_t", [P, 2, S])
    QLT = zone("latent_q_t", [P, 3, S])
    KN = zone("k_rows", [P, NT, MLA_HEADS, QK])
    VN = zone("v_rows", [P, NT, D])
    QN = zone("q_rows", [P, NT, MLA_HEADS, QK])
    sq = zone("squares", [P, D])
    lg = zone("latent_gains", [P, KV_LORA + Q_LORA])
    ss = zone("sums", [P, 3, 16])
    posi = zone("positions", [P, NT], I32)
    posri = zone("positions_row", [P, S], I32)
    posf = zone("positions_f", [P, NT])
    posrf = zone("positions_row_f", [P, S])
    frq = zone("freqs", [P, 16])
    ang = zone("angles", [P, 6, NT, 16])
    pmask = zone("pos_mask", [P, NT, S])

    def row_evac(dst_of):
        def evac(f, who, i, t, bank, free):
            dst, n = dst_of(i, t)
            src = bank[:, 0:n] if len(dst.shape) == 2 else bank[:, 0:n].rearrange("p (a b) -> p a b", a=dst.shape[1])
            f(nc.scalar.activation(dst, src, ACT.Copy) if who == "a" else nc.vector.tensor_copy(dst, src), free, wait=False)
        return evac

    alternate = lambda i, t: "av"[t]
    project("dkv", lambda i, k, t: HKV[:, k, t * P:(t + 1) * P], row_evac(lambda i, t: (DKV[:, t, :], 288)), alternate,
            width=288)
    if Stage.count < upto:
        n = Stage.count
        mean_done, root_done = sem(f"gn{n}_mean"), sem(f"gn{n}_root")
        sin_in, sin_out = sem("angle_reduced"), sem("angle_sines")
        todo = [(DKV[:, t, 0:KV_LORA].unsqueeze(1), DKV[:, t, 0:KV_LORA].unsqueeze(1), lg[:, 0:KV_LORA], KV_LORA)
                for t in range(NT)]
        flat = lambda i: ang[:, i, :, :].rearrange("p t h -> p (t h)")
        MAGIC = 12582912.0
        C1, C2 = 6.28125, TWO_PI - 6.28125
        C2H = float(np.float32(C2))
        C3 = float(C2 - C2H)
        PI = 3.1415925

        def kv_dve(f, dve):
            group_norms(f, dve, ss, todo, mean_done, root_done, sq)
            f(nc.vector.tensor_copy(posf[:, :], posi[:, :]))
            f(nc.vector.tensor_copy(posrf[:, :], posri[:, :]))
            for t in range(NT):
                f(nc.vector.tensor_scalar(ang[:, 0, t, :], frq[:, :], posf[:, t:t + 1], None, ALU.mult))
                f(nc.vector.tensor_scalar(pmask[:, t, :], posrf[:, :], posf[:, t:t + 1], NEG, ALU.is_gt, ALU.mult))
            f(nc.vector.tensor_scalar(flat(1), flat(0), 1.0 / TWO_PI, None, ALU.mult))
            f(nc.vector.tensor_scalar(flat(1), flat(1), MAGIC, None, ALU.add))
            f(nc.vector.tensor_scalar(flat(1), flat(1), MAGIC, None, ALU.subtract))
            for c in (C1, C2H, C3):
                f(nc.vector.scalar_tensor_tensor(flat(0), flat(1), -c, flat(0), ALU.mult, ALU.add))
            f(nc.vector.tensor_scalar(flat(0), flat(0), PI, -PI, ALU.min, ALU.max))
            f(nc.vector.tensor_scalar(flat(1), flat(0), -1.0, None, ALU.mult))
            f(nc.vector.tensor_tensor(flat(1), flat(1), flat(0), ALU.max))
            f(nc.vector.tensor_scalar(flat(1), flat(1), -1.0, math.pi / 2, ALU.mult, ALU.add), sin_in)
            dve.wait_ge(sin_out, 1)
            for t in range(NT):
                rope(f, DKV[:, t, KV_LORA:288].unsqueeze(1), ang[:, 3, t, :], ang[:, 2, t, :], 16, sq)
                f(nc.vector.tensor_copy(KN[:, t, :, QK_NOPE:QK],
                                        DKV[:, t, KV_LORA:288].unsqueeze(1).broadcast_to([P, MLA_HEADS, QK_ROPE])))

        def kv_act(f, act):
            group_roots(f, act, ss, todo, mean_done, root_done)
            act.wait_ge(sin_in, 1)
            f(nc.scalar.activation(ang[:, 2:4, :, :].rearrange("p i t h -> p (i t h)"),
                                   ang[:, 0:2, :, :].rearrange("p i t h -> p (i t h)"), ACT.Sin), sin_out)

        elementwise(kv_dve, kv_act,
                    loads=[(lg[:, 0:KV_LORA], bcast(I["mla_kv_latent_g_2"])),
                           (lg[:, KV_LORA:], bcast(I["mla_q_latent_g_2"][0])),
                           (posri[:, :], bcast(I["positions_2"][0])), (frq[:, :], bcast(I["freqs"]))] +
                          [(posi[:, t:t + 1], I["positions_2"][0, t * P:(t + 1) * P].rearrange("(p o) -> p o", o=1))
                           for t in range(NT)])
    else:
        stage()
    transpose_all([(LT[:, k, t * P:(t + 1) * P], DKV[:, t, k * P:(k + 1) * P]) for k in range(2) for t in range(NT)])
    ukv_view = lambda c: (lambda slot: slot[:, 0:4 * D].rearrange("p (k n) -> p k n", k=4)
                          [:, 2 * (c // 2):2 * (c // 2) + 2, 512 * (c % 2):512 * (c % 2) + 512])
    project("ukv", lambda i, k, t: LT[:, k, t * P:(t + 1) * P],
            row_evac(lambda i, t: (KN[:, t, 8 * i:8 * i + 8, 0:QK_NOPE], 512) if i < 2 else
                     (VN[:, t, 512 * (i - 2):512 * (i - 2) + 512], 512)), alternate,
            chunks=[(0, ukv_view(c), 2) for c in range(4)])
    project("dq", ht, row_evac(lambda i, t: (DQ[:, t, :], Q_LORA)), alternate, width=Q_LORA)
    norm_stage([(DQ[:, t, :].unsqueeze(1), DQ[:, t, :].unsqueeze(1), lg[:, KV_LORA:], Q_LORA) for t in range(NT)])
    transpose_all([(QLT[:, k, t * P:(t + 1) * P], DQ[:, t, k * P:(k + 1) * P]) for k in range(3) for t in range(NT)])
    uq_view = lambda c: (lambda slot: slot[:, 0:3 * MLA_HEADS * QK].rearrange("p (k n) -> p k n", k=3)
                         [:, :, 512 * c:512 * c + 512])
    qn_flat = lambda t: QN[:, t, :, :].rearrange("p h d -> p (h d)")
    project("uq", lambda i, k, t: QLT[:, k, t * P:(t + 1) * P],
            row_evac(lambda i, t: (qn_flat(t)[:, 512 * i:512 * i + 512], 512)), alternate,
            chunks=[(0, uq_view(c), 3) for c in range(3)])

    def rope_q(f, dve):
        for t in range(NT):
            rope(f, QN[:, t, :, QK_NOPE:QK], ang[:, 3, t, :], ang[:, 2, t, :], 16, sq)
    elementwise(rope_q)
    QTM = zone("q_heads_t", [QK, MLA_HEADS, S])
    KTM = zone("k_heads_t", [QK, MLA_HEADS, S])
    transpose_all([(dst[:, h, t * P:(t + 1) * P], src[:, t, h, :])
                   for dst, src in ((QTM, QN), (KTM, KN)) for h in range(MLA_HEADS) for t in range(NT)])
    AO = QN[:, :, :, :].rearrange("p t h d -> p (t h d)")[:, 0:NT * D].rearrange("p (t n) -> p t n", t=NT)
    attention([dict(qT=QTM[:, h, t * P:(t + 1) * P], kT=KTM[:, h, :], nk=S,
                    v=[VN[:, k, h * V_HEAD:(h + 1) * V_HEAD] for k in range(NT)], scale=QK ** -0.5,
                    mask=pmask[:, t, :], coef=None, out=AO[:, t, h * V_HEAD:(h + 1) * V_HEAD], add=False, guard=False)
               for h in range(MLA_HEADS) for t in range(NT)])
    AOT = HKV
    transpose_all([(AOT[:, k, t * P:(t + 1) * P], AO[:, t, k * P:(k + 1) * P]) for k in range(KD) for t in range(NT)])
    gate_row(g1)
    out_project("mla_out", KD, AOT, gate=(GROW, TMP))
    peer(1, "peer_q1", GM[:, 3, :], sh2, g2)

    zone.at = WORK
    fg = zone("final_gain", [P, D])
    fo = zone("final_out", [P, NT, D])
    if Stage.count < upto:
        sq_done, mean_done, root_done = sem("final_squares"), sem("final_mean"), sem("final_root")

        def fin_act(f, act):
            for t in range(NT):
                f(nc.scalar.activation(fo[:, t, :], X[:, t, :], ACT.Square, accum_out=stats[:, t:t + 1]), sq_done)
            act.wait_ge(mean_done, 1)
            f(nc.scalar.activation(stats[:, 4:4 + NT], stats[:, 0:NT], ACT.Sqrt), root_done)

        def fin_dve(f, dve):
            dve.wait_ge(sq_done, NT)
            f(nc.vector.tensor_scalar(stats[:, 0:NT], stats[:, 0:NT], 1.0 / D, EPS, ALU.mult, ALU.add), mean_done)
            inverse_root(f, stats[:, 0:NT], stats[:, 4:4 + NT], stats[:, 8:8 + NT], mean_done, root_done, dve)
            for t in range(NT):
                f(nc.vector.scalar_tensor_tensor(fo[:, t, :], X[:, t, :], stats[:, 4 + t:5 + t], fg[:, :], ALU.mult, ALU.mult))
        elementwise(fin_dve, fin_act, loads=[(fg[:, :], bcast(I["final_g_2"]))])
    else:
        stage()
    out_done = sem("out_stored")
    with StageBlock() as block:
        @block.sync
        def _(sp):
            sp.dma_start(out[0].rearrange("(t p) d -> p t d", p=P), fo[:, :, :] if upto >= 99 else X[:, :, :]).then_inc(out_done, 16)
            sp.wait_ge(out_done, 16)
    ctx.close()


_HOST = ("rope4", "rope8", "ropec", "freqs")


def kernel(**inputs):
    import numpy as _np
    import concourse.bacc as _bacc
    from concourse.bass_utils import run_bass_kernel_spmd as _run

    nc = _bacc.Bacc("TRN2", target_bir_lowering=False, num_devices=1)
    arrays, args = {}, {}
    for name, value in [*inputs.items(), *rope_constants().items()]:
        a = _np.ascontiguousarray(value)
        arrays[f"in_{name}"] = a
        args[name] = nc.dram_tensor(f"in_{name}", a.shape, mybir.dt.from_np(a.dtype), kind="ExternalInput").ap()
    out = nc.dram_tensor("out", (1, S, D), F32, kind="ExternalOutput").ap()
    build(nc, args, out)
    r = _run(nc, [arrays], core_ids=[0])
    return r.results[0]["out"]
```
